# Optimizing a Trainium2 kernel written in Bass

```python
import math
import jax, jax.numpy as jnp
from jax import lax
import numpy as np

D_MODEL = 1024
BATCH = 1
SEQ = 1024
DEPTH = 1

CHUNK = 64
D_MIX = D_MODEL
HG_WIDTH = D_MIX // 2
DA_WIDTH = D_MIX - HG_WIDTH
HG_HEADS = 4
HG_DK = HG_WIDTH // HG_HEADS
HG_DV = HG_DK
DA_HEADS = 4
DA_DV = DA_WIDTH // DA_HEADS
DA_DH = DA_DV // 2
Q_BLOCK = 128
HG_Q_COLS = HG_HEADS * HG_DK
HG_F_COLS = HG_HEADS * HG_DK
HG_I_COLS = HG_HEADS * HG_DV
HG_G_COLS = HG_HEADS * HG_DV
DA_Q_COLS = DA_HEADS * 2 * DA_DH
DA_K_COLS = DA_HEADS * 2 * DA_DH
DA_V_COLS = DA_HEADS * DA_DV
D_IN = HG_Q_COLS + HG_F_COLS + HG_I_COLS + HG_G_COLS + DA_Q_COLS + DA_K_COLS + DA_V_COLS
D_CAT = HG_HEADS * HG_DV + DA_HEADS * DA_DV
PEER_HEADS = 8
PEER_N_KEYS = 128
PEER_N_EXPERTS = PEER_N_KEYS * PEER_N_KEYS
PEER_D_KEY = 256
PEER_HALF = PEER_D_KEY // 2
PEER_TOPK = 16
TOKEN_BLOCK = 128
RMS_EPS = 1e-6

kernel_name = "hymba_hgrn2_diffattn_peer_block"

def rmsnorm(x, w):
    xf = x.astype(jnp.float32)
    y = xf * lax.rsqrt(jnp.mean(xf * xf, axis=-1, keepdims=True) + RMS_EPS)
    return (y * w.astype(jnp.float32)).astype(x.dtype)

def rmsnorm_f32(x, w):
    y = x * lax.rsqrt(jnp.mean(x * x, axis=-1, keepdims=True) + RMS_EPS)
    return y * w.astype(jnp.float32)

def lambda_init(layer_idx):
    return 0.8 - 0.6 * math.exp(-0.3 * layer_idx)

def hgrn2_group(q, f_logit, inp, gate, lb, norm_w):
    B, S = q.shape[0], q.shape[1]
    n_chunks = S // CHUNK
    lbf = lb.astype(jnp.float32)
    f = lbf + (1.0 - lbf) * jax.nn.sigmoid(f_logit.astype(jnp.float32))
    k = 1.0 - f
    log_f = jnp.log(f)
    qf = q.astype(jnp.float32) * (HG_DK ** -0.5)
    vf = inp.astype(jnp.float32)

    def to_chunks(t, d):
        return t.reshape(B, n_chunks, CHUNK, HG_HEADS, d).transpose(1, 0, 3, 2, 4)

    qc, kc, ac = to_chunks(qf, HG_DK), to_chunks(k, HG_DK), to_chunks(log_f, HG_DK)
    vc = to_chunks(vf, HG_DV)
    tri = jnp.tril(jnp.ones((CHUNK, CHUNK), dtype=bool))

    def step(state, xs):
        qb, kb, vb, ab = xs
        b = jnp.cumsum(ab, axis=2)
        diff = b[:, :, :, None, :] - b[:, :, None, :, :]
        decay = jnp.exp(jnp.where(tri[:, :, None], diff, -jnp.inf))
        scores = jnp.einsum('bhtd,bhsd,bhtsd->bhts', qb, kb, decay)
        o = jnp.einsum('bhts,bhse->bhte', scores, vb) \
            + jnp.einsum('bhtd,bhde->bhte', qb * jnp.exp(b), state)
        b_last = b[:, :, -1]
        state = jnp.exp(b_last)[..., None] * state \
            + jnp.einsum('bhsd,bhse->bhde', kb * jnp.exp(b_last[:, :, None, :] - b), vb)
        return state, o

    s0 = jnp.zeros((B, HG_HEADS, HG_DK, HG_DV), jnp.float32)
    _, oc = lax.scan(step, s0, (qc, kc, vc, ac))
    o = oc.transpose(1, 0, 3, 2, 4).reshape(B, S, HG_HEADS, HG_DV)
    g = gate.astype(jnp.float32).reshape(B, S, HG_HEADS, HG_DV)
    o = rmsnorm_f32(o, norm_w) * jax.nn.silu(g)
    return o.reshape(B, S, HG_HEADS * HG_DV)

def diff_attention_group(q, k, v, lam_params, norm_w, layer_idx):
    B, S = q.shape[0], q.shape[1]
    n_blocks = S // Q_BLOCK
    lam_init = lambda_init(layer_idx)
    lp = lam_params.astype(jnp.float32)
    lam = jnp.exp(jnp.sum(lp[0] * lp[1])) - jnp.exp(jnp.sum(lp[2] * lp[3])) + lam_init
    scale = DA_DH ** -0.5
    qf = q.astype(jnp.float32).reshape(B, n_blocks, Q_BLOCK, DA_HEADS, 2, DA_DH).transpose(1, 0, 2, 3, 4, 5)
    kf = k.astype(jnp.float32).reshape(B, S, DA_HEADS, 2, DA_DH)
    vf = v.astype(jnp.float32).reshape(B, S, DA_HEADS, DA_DV)
    key_chunk = jnp.arange(S) // CHUNK

    def one_block(args):
        qb, blk = args
        s = jnp.einsum('bqhcd,bkhcd->bhcqk', qb, kf) * scale
        q_chunk = (blk * Q_BLOCK + jnp.arange(Q_BLOCK)) // CHUNK
        mask = key_chunk[None, :] <= q_chunk[:, None]
        p = jax.nn.softmax(jnp.where(mask, s, -jnp.inf), axis=-1)
        a = p[:, :, 0] - lam * p[:, :, 1]
        return jnp.einsum('bhqk,bkhe->bqhe', a, vf)

    o = lax.map(one_block, (qf, jnp.arange(n_blocks)))
    o = o.transpose(1, 0, 2, 3, 4).reshape(B, S, DA_HEADS, DA_DV)
    o = rmsnorm_f32(o, norm_w) * (1.0 - lam_init)
    return o.reshape(B, S, DA_HEADS * DA_DV)

def peer_ffn(x, w_query, sub_keys, u, v):
    B, S, D = x.shape
    xt = x.reshape((B * S) // TOKEN_BLOCK, TOKEN_BLOCK, D)
    wq = w_query.reshape(D, PEER_HEADS, PEER_D_KEY)

    def one_block(xb):
        qh = jnp.einsum('td,dhk->thk', xb, wq)
        s1 = jnp.einsum('thk,hnk->thn', qh[..., :PEER_HALF], sub_keys[:, 0])
        s2 = jnp.einsum('thk,hnk->thn', qh[..., PEER_HALF:], sub_keys[:, 1])
        v1, i1 = lax.top_k(s1, PEER_TOPK)
        v2, i2 = lax.top_k(s2, PEER_TOPK)
        T = xb.shape[0]
        cand = (v1[..., :, None] + v2[..., None, :]).reshape(T, PEER_HEADS, PEER_TOPK * PEER_TOPK)
        cand_idx = (i1[..., :, None] * PEER_N_KEYS + i2[..., None, :]).reshape(T, PEER_HEADS, PEER_TOPK * PEER_TOPK)
        top_s, pos = lax.top_k(cand, PEER_TOPK)
        idx = jnp.take_along_axis(cand_idx, pos, axis=-1)
        g = jax.nn.softmax(top_s.astype(jnp.float32), axis=-1).astype(xb.dtype)
        ue = u[idx]
        act = jax.nn.gelu(jnp.einsum('thkd,td->thk', ue, xb))
        ve = v[idx]
        return jnp.einsum('thk,thkd->td', g * act, ve)

    out = lax.map(one_block, xt)
    return out.reshape(B, S, D)

def setup_inputs(seed: int = 0) -> dict:
    key = jax.random.key(seed)
    ks = jax.random.split(key, 16)
    f32 = jnp.float32
    nrm = lambda k, shape, s: jax.random.normal(k, shape, f32) * s
    gain = lambda k, shape: 1.0 + 0.02 * jax.random.normal(k, shape, f32)
    return {
        "x": nrm(ks[0], (BATCH, SEQ, D_MODEL), 1.0),
        "norm_mix_w": gain(ks[1], (DEPTH, D_MODEL)),
        "w_in": nrm(ks[2], (DEPTH, D_MODEL, D_IN), D_MODEL ** -0.5),
        "hgrn_lb_param": nrm(ks[3], (DEPTH + 1, HG_HEADS * HG_DK), 0.5),
        "hgrn_norm_w": gain(ks[4], (DEPTH, HG_DV)),
        "diff_lambda": nrm(ks[5], (DEPTH, 4, DA_DH), 0.1),
        "diff_norm_w": gain(ks[6], (DEPTH, DA_DV)),
        "w_out": nrm(ks[7], (DEPTH, D_CAT, D_MODEL), D_CAT ** -0.5),
        "norm_ffn_w": gain(ks[8], (DEPTH, D_MODEL)),
        "peer_w_query": nrm(ks[9], (DEPTH, D_MODEL, PEER_HEADS * PEER_D_KEY), D_MODEL ** -0.5),
        "peer_sub_keys": nrm(ks[10], (DEPTH, PEER_HEADS, 2, PEER_N_KEYS, PEER_HALF), PEER_HALF ** -0.5),
        "peer_u": nrm(ks[11], (DEPTH, PEER_N_EXPERTS, D_MODEL), D_MODEL ** -0.5),
        "peer_v": nrm(ks[12], (DEPTH, PEER_N_EXPERTS, D_MODEL), 0.5),
        "norm_final_w": gain(ks[13], (D_MODEL,)),
    }

def reference(x, norm_mix_w, w_in, hgrn_lb_param, hgrn_norm_w, diff_lambda, diff_norm_w,
              w_out, norm_ffn_w, peer_w_query, peer_sub_keys, peer_u, peer_v, norm_final_w):
    lower_bounds = jnp.cumsum(jax.nn.softmax(hgrn_lb_param.astype(jnp.float32), axis=0), axis=0)
    c1 = HG_Q_COLS
    c2 = c1 + HG_F_COLS
    c3 = c2 + HG_I_COLS
    c4 = c3 + HG_G_COLS
    c5 = c4 + DA_Q_COLS
    c6 = c5 + DA_K_COLS
    h = x
    for l in range(DEPTH):
        n1 = rmsnorm(h, norm_mix_w[l])
        proj = jnp.einsum('bsd,de->bse', n1, w_in[l])
        hg_out = hgrn2_group(proj[..., :c1], proj[..., c1:c2], proj[..., c2:c3], proj[..., c3:c4],
                             lower_bounds[l], hgrn_norm_w[l])
        da_out = diff_attention_group(proj[..., c4:c5], proj[..., c5:c6], proj[..., c6:],
                                      diff_lambda[l], diff_norm_w[l], l)
        mixed = jnp.concatenate([hg_out, da_out], axis=-1).astype(h.dtype)
        h = h + jnp.einsum('bse,ed->bsd', mixed, w_out[l])
        n2 = rmsnorm(h, norm_ffn_w[l])
        h = h + peer_ffn(n2, peer_w_query[l], peer_sub_keys[l], peer_u[l], peer_v[l]).astype(h.dtype)
    return rmsnorm(h, norm_final_w)


_drawn_inputs = setup_inputs


def setup_inputs(seed=0):
    import zlib

    import numpy as np

    out = dict(_drawn_inputs(seed))
    spreads = {}
    factors = {}
    for name, (base, spread) in spreads.items():
        noise = np.random.default_rng([zlib.crc32(name.encode()), seed]).standard_normal(out[name].shape)
        drawn = base * np.exp(spread * noise) if base else spread * noise
        out[name] = __import__('jax').numpy.asarray(drawn.astype(out[name].dtype))
    for name, factor in factors.items():
        out[name] = (out[name] * factor).astype(out[name].dtype)
    return out
```

```python
from contextlib import ExitStack

import concourse.bass as bass
import numpy as np
from concourse import mybir

F32 = mybir.dt.float32
F32R = mybir.dt.float32r
U32 = mybir.dt.uint32
ALU = mybir.AluOpType
ACT = mybir.ActivationFunctionType
AX_X = mybir.AxisListType.X

P = 128
T = 1024
D = 1024
KD = D // P
TT = T // P
HEADS = 4
SECTIONS = 7
CHUNK = 64
PEER_HEADS = 8
TOPK = 16
KEYS = 128
UNITS = TT * PEER_HEADS
HALF_T = T // 2
LEVELS = 7
EPS = 1e-6
LAMBDA_INIT = 0.2
LOWEST = -3.0e38


class Links:

    def __init__(self, eng, sem):
        self.eng, self.sem, self.n, self.shift = eng, sem, 0, 0

    def __call__(self, ins):
        self.n += 1
        ins.then_inc(self.sem, 1)
        self.eng.wait_ge(self.sem, self.shift + self.n)

    def mark(self, ins):
        self.n += 1
        ins.then_inc(self.sem, 1)
        return self.n

    def wait(self, n):
        self.eng.wait_ge(self.sem, self.shift + n)

    def loop(self, i, per_turn):
        self.start, self.per_turn, self.shift = self.n, per_turn, i * per_turn

    def end(self, turns):
        assert self.n - self.start == self.per_turn, (self.n - self.start, self.per_turn)
        self.n, self.shift = self.start + turns * self.per_turn, 0


def spread(ap, axis, n):
    ap = ap.unsqueeze(axis)
    shape = list(ap.shape)
    shape[axis] = n
    return ap.broadcast_to(shape)


def build(nc, x_t, x_n, w_in, w_out, w_q, sub_t, u_t, v, norm_mix, norm_ffn, norm_fin, lb, hg_norm,
          da_norm, lam, cst, level_masks, out, h_dram, s_dram, gates_dram, stop=99):
    with ExitStack() as ctx:
        base = (nc.sbuf_base + 127) // 128 * 128
        KB = 1024

        def at(name, kb, shape, dt=F32):
            return nc.alloc_sbuf_tensor_at(name, shape, dt, offset=base + int(kb * KB))

        def sem(name):
            return ctx.enter_context(nc.semaphore(name))

        PS = ctx.enter_context(nc.psum_tensor("PS", [P, 8, 512], F32))

        def bank(b, n=1):
            return PS[:, b, :] if n == 1 else PS[:, b:b + n, :]

        def bank_tiles(b, n=1):
            return PS[:, b:b + n, :].rearrange("p a (b c) -> p (a b) c", c=128)

        consts = at("consts", 0, [P, 400])
        ident, ones, iota, iota16 = consts[:, 0:128], consts[:, 128:256], consts[:, 256:384], consts[:, 384:400]
        masks = at("masks", 2, [P, 8, 128])
        hg_gain = at("hg_gain", 6, [P, 128])
        da_gain = at("da_gain", 6.5, [P, 128])
        lam_in = at("lam_in", 7, [P, 4, 64])
        mix_w = at("mix_w", 8, [P, KD])
        lb_in = at("lb_in", 8.0625, [P, 2, HEADS])
        small = at("small", 8.125, [P, 96])
        eps = small[:, 0:1]
        lbs, one_lb, lb_t = small[:, 4:8], small[:, 8:12], small[:, 12:20]
        lams, lam_t = small[:, 20:21], small[:, 24:26]
        zero_col = small[:, 28:29]
        norm_ss, norm_r = at("norm_ss", 8.5, [P, 32]), at("norm_r", 8.625, [P, 32])
        l_sum, l_rec, mx, nmx = (at(n, 8.75 + i / 16, [P, 2, 2]) for i, n in enumerate(("l_sum", "l_rec", "mx", "nmx")))
        zeros = at("zeros", 9, [P, 128])

        X = at("X", 10, [P, KD, T])
        W = [at(f"W{i}", 42 + 16 * i, [P, KD, 512]) for i in range(2)]
        sq = [at(f"sq{i}", 74 + 4 * i, [P, T]) for i in range(2)]
        rstd = at("rstd", 82, [P, T])
        Q = at("Q", 74, [P, HEADS, T])
        F = at("F", 90, [P, HEADS, T])
        K = at("K", 106, [P, HEADS, T])
        INP = at("INP", 122, [P, TT, 512])
        GATE = at("GATE", 138, [P, TT, 512])
        DQ = at("DQ", 154, [P, HEADS, T])
        DK = at("DK", 170, [P, HEADS, T])
        DV = at("DV", 186, [P, TT, 512])
        E = [at(f"E{i}", 10 + 4.5 * i, [P, 9, 128]) for i in range(2)]
        QL = [at(f"QL{i}", 19 + 4.5 * i, [P, 9, 128]) for i in range(2)]
        KL = [at(f"KL{i}", 28 + 4.5 * i, [P, 9, 128]) for i in range(2)]
        M = [at(f"M{i}", 42 + 4 * i, [P, 8, 128]) for i in range(2)]
        KN = [at(f"KN{i}", 50 + i / 2, [P, 128]) for i in range(2)]
        STATE = at("STATE", 51, [P, HEADS, 128])
        BL = [at(f"BL{i}", 53 + i / 16, [P, 1]) for i in range(2)]
        PR = [[at(f"PR{i}{c}", 74 + 8 * i + 4 * c, [P, T]) for c in range(2)] for i in range(2)]
        AT = [at(f"AT{i}", 90 + 4 * i, [P, TT, 128]) for i in range(2)]
        DA = at("DA", 106, [P, TT, 512])
        SQN = [at(f"SQN{i}", 98 + 2 * i, [P, 512]) for i in range(2)]
        MT = at("MT", 10, [P, KD, T])
        WO = at("WO", 42, [P, KD, D])
        N2H = at("N2H", 154, [P, KD, T], F32R)
        N2L = at("N2L", 74, [P, KD, T], F32R)
        XN = [at(f"XN{i}", 138 + 4 * i, [P, D]) for i in range(2)]
        H = [at(f"H{i}", 146 + 4 * i, [P, D]) for i in range(2)]
        N2 = [at(f"N2{i}", 186 + 4 * i, [P, D]) for i in range(2)]
        ffn_w = at("ffn_w", 194, [P, D])
        junk = at("junk", 198, [P, D])
        WQ = [at(f"WQ{i}", 10 + 16 * i, [P, KD, 512]) for i in range(2)]
        WQH = [at(f"WQH{i}", 42 + 4 * i, [P, KD, 128], F32R) for i in range(2)]
        WQL = [at(f"WQL{i}", 50 + 4 * i, [P, KD, 128], F32R) for i in range(2)]
        QH = [at(f"QH{i}", 58 + 4 * i, [P, T]) for i in range(2)]
        SUB = at("SUB", 106, [P, 16, 128])
        SS = [at(f"SS{i}", 114 + 4 * i, [P, TT, 128]) for i in range(2)]
        SU = [at(f"SU{i}", 10 + i, [P, 2, 128]) for i in range(4)]
        SU2 = [at(f"SU2{i}", 14 + i, [P, 2, 128]) for i in range(2)]
        TOPV = at("TOPV", 16, [P, 2, TOPK])
        TOPI = at("TOPI", 16.25, [P, 2, TOPK], U32)
        CAND = at("CAND", 17, [P, TOPK * TOPK])
        CAND2 = at("CAND2", 18, [P, TOPK * TOPK])
        su_seen = at("su_seen", 19.5, [P, 1])
        TOPC = at("TOPC", 19, [P, TOPK])
        TOPP = at("TOPP", 19.25, [P, TOPK], U32)
        I12 = at("I12", 20, [P, 2, UNITS * TOPK])
        CS = at("CS", 28, [P, UNITS * TOPK])
        POS = at("POS", 32, [P, UNITS * TOPK], U32)
        AB = [at(f"AB{i}", 36 + 4 * i, [P, UNITS * TOPK]) for i in range(2)]
        ABU = at("ABU", 44, [P, UNITS * TOPK], U32)
        EQ = at("EQ", 48, [P, P * TOPK])
        EQ2 = at("EQ2", 56, [P, P * TOPK])
        PK = at("PK", 64, [P, 3, P])
        PT = at("PT", 106, [P, 3, T])
        gsum = at("gsum", 118, [P, UNITS])
        grec = at("grec", 118.25, [P, UNITS])
        gmax = at("gmax", 118.5, [P, UNITS])
        OH = [[at(f"OH{i}{j}", 122 + 2 * i + j / 2, [P, 128]) for j in range(4)] for i in range(2)]
        OG = [[at(f"OG{i}{j}", 126 + 2 * i + j / 2, [P, 128]) for j in range(4)] for i in range(2)]
        GS = [at(f"GS{i}", 10 + 32 * i, [P, KEYS, 64]) for i in range(2)]
        UR = [at(f"UR{i}", 10 + 4 * i, [P, KD, 128]) for i in range(2)]
        VR = [at(f"VR{i}", 18 + 4 * i, [P, D]) for i in range(2)]
        UH = [at(f"UH{i}", 26 + 4 * i, [P, KD, 128], F32R) for i in range(2)]
        UL = [at(f"UL{i}", 34 + 4 * i, [P, KD, 128], F32R) for i in range(2)]
        GT = [at(f"GT{i}", 42 + 2 * i, [P, HALF_T]) for i in range(2)]
        AF = [at(f"AF{i}", 46 + 2 * i, [P, HALF_T]) for i in range(2)]
        AH = [at(f"AH{i}", 50 + 2 * i, [P, HALF_T], F32R) for i in range(4)]
        AL = [at(f"AL{i}", 58 + 2 * i, [P, HALF_T], F32R) for i in range(4)]
        VH = [at(f"VH{i}", 106 + 4 * i, [P, D], F32R) for i in range(4)]
        VL = [at(f"VL{i}", 122 + 4 * i, [P, D], F32R) for i in range(4)]
        ACC = at("ACC", 138, [P, TT // 2, D])
        fin_w = at("fin_w", 66, [P, D])
        FSQ = at("FSQ", 70, [P, D])

        consts_in, x_in = sem("consts_in"), [sem(f"x_in{k}") for k in range(KD)]
        w_in_sem = [sem(f"w_in{i}") for i in range(2)]
        stage_done = sem("stage_done")
        sq_ready, sq_used, root_ready, n1_ready = sem("sq_ready"), sem("sq_used"), sem("root_ready"), sem("n1_ready")
        proj_done = sem("proj_done")
        proj_out = {"act": sem("proj_out_act"), "dve": sem("proj_out_dve")}
        ready = sem("ready")
        log_f = sem("log_f")
        hg_diff, hg_exp, hg_q, hg_k, hg_scores, hg_mask, hg_kn, hg_pe, hg_state, hg_out = (
            sem("hg_" + n) for n in ("diff", "exp", "q", "k", "scores", "mask", "kn", "pe", "state", "out"))
        at_s, at_max, at_exp, at_comb, at_tr, at_t, at_o, at_oe = (
            sem("at_" + n) for n in ("s", "max", "exp", "comb", "tr", "t", "o", "oe"))
        nrm_sq, nrm_ss, nrm_root, nrm_r = sem("nrm_sq"), sem("nrm_ss"), sem("nrm_root"), sem("nrm_r")
        mt_tr, mt_act, mt_dve, wo_in, wo_done, h_ready, h_ss, n2_ready, n2_tr, n2_hi, n2_lo = (
            sem(n) for n in ("mt_tr", "mt_act", "mt_dve", "wo_in", "wo_done", "h_ready", "h_ss", "n2_ready", "n2_tr", "n2_hi", "n2_lo"))
        xn_in = [sem(f"xn_in{i}") for i in range(2)]
        h_out = [sem(f"h_out{i}") for i in range(2)]
        wq_in = [sem(f"wq_in{i}") for i in range(2)]
        wq_hi, wq_lo, qh_done, qh_out, sc_done, sc_out = (sem(n) for n in ("wq_hi", "wq_lo", "qh_done", "qh_out", "sc_done", "sc_out"))
        ss_out = [sem(f"ss_out{i}") for i in range(2)]
        su_in = [sem(f"su_in{i}") for i in range(4)]
        su_used, pk_ready, pk_tr, pt_ready, g_exp, g_shift = (sem(n) for n in ("su_used", "pk_ready", "pk_tr", "pt_ready", "g_exp", "g_shift"))
        oh_ready, quad_done, quad_out, gs_out = sem("oh_ready"), sem("quad_done"), sem("quad_out"), [sem(f"gs_out{i}") for i in range(2)]
        gate_gain = sem("gate_gain")
        u_in, v_in, g_in = ([sem(f"{n}_in{i}") for i in range(2)] for n in "uvg")
        uh, ul, vh, vl, s1, gelu, prod, ah, al, s2, acc_add = (
            sem("p_" + n) for n in ("uh", "ul", "vh", "vl", "s1", "gelu", "prod", "ah", "al", "s2", "acc"))
        acc_in, y_ss, y_root, y_ready, y_out = (sem(n) for n in ("acc_in", "y_ss", "y_root", "y_ready", "y_out"))
        act_own, dve_own, pool_own = sem("act_own"), sem("dve_own"), sem("pool_own")

        def stage_end(eng, n):
            eng.drain().then_inc(stage_done, 1)
            eng.wait_ge(stage_done, 5 * n)

        def taker(G):
            return "act" if G // 8 in (1, 3) or G % 2 == 0 else "dve"

        def taken(G):
            return taker(G), sum(taker(g) == taker(G) for g in range(G + 1))

        def proj_dst(G):
            s, g = divmod(G, 8)
            dst = (Q, F, INP, GATE, DQ, DK, DV)[s]
            if s in (2, 3, 6):
                return dst[:, g, :]
            return dst[:, g // 2, (g % 2) * 512:(g % 2) * 512 + 512]

        att = [(h, b) for h in range(HEADS) for b in range(TT)]

        block = ctx.enter_context(nc.Block())

        @block.sync
        def _(sp):
            for dst, src in ((consts[:, :], cst), (masks[:, :, :], level_masks), (mix_w[:, :], norm_mix),
                             (lb_in[:, :, :], lb)):
                sp.dma_start(dst, src).then_inc(consts_in, 16)
            for k in range(KD):
                sp.dma_start(X[:, k, :], x_t[:, k, :]).then_inc(x_in[k], 16)
            for dst, src in ((hg_gain[:, :], hg_norm), (da_gain[:, :], da_norm), (lam_in[:, :, :], lam)):
                sp.dma_start(dst, src).then_inc(consts_in, 16)
            for s in range(SECTIONS):
                if s == 2:
                    stage_end(sp, 1)
                if s >= 2:
                    sp.wait_ge(proj_done, 8 * (s - 1))
                sp.dma_start(W[s % 2][:, :, :], w_in[:, :, s * 512:(s + 1) * 512]).then_inc(w_in_sem[s % 2], 16)
            for n in (2, 3):
                stage_end(sp, n)
            sp.dma_start(WO[:, :, :], w_out).then_inc(wo_in, 16)
            for n in (4, 5):
                stage_end(sp, n)
            sp.dma_start(XN[0][:, :], x_n[0]).then_inc(xn_in[0], 16)
            sp.dma_start(ffn_w[:, :], norm_ffn).then_inc(wo_in, 16)
            for t in range(TT):
                if t + 1 < TT:
                    if t >= 1:
                        sp.wait_ge(h_ready, t)
                    sp.dma_start(XN[(t + 1) % 2][:, :], x_n[t + 1]).then_inc(xn_in[(t + 1) % 2], 16)
                sp.wait_ge(h_ready, t + 1)
                sp.dma_start(h_dram[t], H[t % 2][:, :]).then_inc(h_out[t % 2], 16)
            sp.wait_ge(h_out[0], 16 * TT // 2)
            sp.wait_ge(h_out[1], 16 * TT // 2)
            stage_end(sp, 6)
            if stop == 6:
                sp.dma_start(out, h_dram).then_inc(y_out, 16)
                sp.wait_ge(y_out, 16)
                return
            sp.dma_start(SUB[:, :, :], sub_t).then_inc(consts_in, 16)
            for s in range(2):
                sp.dma_start(WQ[s % 2][:, :, :], w_q[:, :, s * 512:(s + 1) * 512]).then_inc(wq_in[s % 2], 16)
            for m in range(16):
                sp.wait_ge(sc_out, m + 1)
                dst = s_dram[:, m // 2, :, (m % 2) * 128:(m % 2) * 128 + 128].rearrange("a p n -> p a n")
                sp.dma_start(dst, SS[m % 2][:, :, :]).then_inc(ss_out[m % 2], 16)
                if m in (3, 7):
                    s = m // 4 + 2
                    sp.wait_ge(wq_lo, m + 1)
                    sp.dma_start(WQ[s % 2][:, :, :], w_q[:, :, s * 512:(s + 1) * 512]).then_inc(wq_in[s % 2], 16)
            sp.wait_ge(ss_out[0], 16 * 8)
            sp.wait_ge(ss_out[1], 16 * 8)
            stage_end(sp, 7)
            s_units = s_dram.rearrange("a h p n -> (a h) p n")
            with sp.Fori(0, UNITS // 4) as i:
                for j in range(4):
                    sp.wait_ge(su_used, i * 4 + j + 1)
                    sp.dma_start(SU[j][:, :, :],
                                 s_units[bass.ds(i * 4 + j, 1), :, :].rearrange("o p (a n) -> p (o a) n", a=2)
                                 ).then_inc(su_in[j], 16)
            stage_end(sp, 8)
            for t in range(T // 64):
                sp.wait_ge(quad_out, 16 * (t + 1) + 2)
                sp.dma_start(gates_dram[:, :, t * 64:(t + 1) * 64].rearrange("a p t -> p a t"),
                             GS[t % 2][:, :, :]).then_inc(gs_out[t % 2], 16)
            for q in gs_out:
                sp.wait_ge(q, 16 * T // 128)
            stage_end(sp, 9)
            sp.dma_start(fin_w[:, :], norm_fin).then_inc(consts_in, 16)
            for half in range(2):
                c0 = half * KEYS

                def load_u(c, j):
                    sp.wait_ge(ul, c0 + c + 1)
                    sp.dma_start(UR[j % 2][:, :, :], u_t[bass.ds(c, 1)].rearrange("o p k n -> p (o k) n")
                                 ).then_inc(u_in[j % 2], 16)

                def load_vg(c, j):
                    sp.wait_ge(prod, c0 + c + 1)
                    sp.dma_start(GT[j % 2][:, :], gates_dram[bass.ds(c, 1), :, half * HALF_T:(half + 1) * HALF_T]
                                 .rearrange("o p t -> p (o t)")).then_inc(g_in[j % 2], 16)
                    sp.wait_ge(stage_done, 5 * 9)
                    sp.wait_ge(vl, c0 + c + 1)
                    sp.dma_start(VR[j % 2][:, :], v[bass.ds(c, 1)].rearrange("o p d -> p (o d)")).then_inc(v_in[j % 2], 16)

                if half:
                    sp.wait_ge(y_out, 16 * 4)
                sp.dma_start(ACC[:, :, :], h_dram[half * 4:half * 4 + 4].rearrange("a p d -> p a d")).then_inc(acc_in, 16)
                load_u(0, 0)
                load_u(1, 1)
                for j in range(2):
                    load_vg(j, j)
                    load_u(j + 2, j)
                with sp.Fori(0, KEYS // 4 - 1) as i:
                    for j in range(4):
                        load_vg(i * 4 + (2 + j), j)
                        load_u(i * 4 + (4 + j), j)
                for j in range(2):
                    load_vg(KEYS - 2 + j, j)
                for t in range(4):
                    sp.wait_ge(y_ready, half * 4 + t + 1)
                    sp.dma_start(out[half * 4 + t], ACC[:, t, :]).then_inc(y_out, 16)
            sp.wait_ge(y_out, 16 * TT)

        @block.tensor
        def _(pe):
            pe.sem_inc(hg_pe, 2)
            pe.sem_inc(s1, 2)
            pe.sem_inc(s2, 16)
            pe.sem_inc(quad_done, 2)
            pe.sem_inc(pk_tr, 1)
            pe.wait_ge(consts_in, 16 * 7)
            for k in range(KD):
                pe.wait_ge(sq_ready, k + 1)
                for th in range(2):
                    mm = pe.matmul(bank(th), ones, sq[k % 2][:, th * 512:(th + 1) * 512], start=k == 0, stop=k == KD - 1)
                mm.then_inc(sq_used, 1)
            stage_end(pe, 1)
            for G in range(8 * SECTIONS):
                s, g = divmod(G, 8)
                if g == 0:
                    pe.wait_ge(w_in_sem[s % 2], 16 * (s // 2 + 1))
                if G >= 4:
                    who, n = taken(G - 4)
                    pe.wait_ge(proj_out[who], n)
                for k in range(KD):
                    if s in (2, 3, 6):
                        l, r = X[:, k, g * P:(g + 1) * P], W[s % 2][:, k, :]
                    else:
                        l, r = W[s % 2][:, k, (g // 2) * P:(g // 2 + 1) * P], X[:, k, (g % 2) * 512:(g % 2 + 1) * 512]
                    mm = pe.matmul(bank(G % 4), l, r, start=k == 0, stop=k == KD - 1)
                mm.then_inc(proj_done, 1)
            stage_end(pe, 2)
            with pe.Fori(0, TT) as n:
                def scores(h):
                    p = h % 2
                    pe.wait_ge(hg_q, n * 4 + h + 3)
                    pe.wait_ge(hg_k, n * 4 + h + 3)
                    pe.wait_ge(hg_mask, n * 4 + h + 1)
                    for l in range(8):
                        pe.matmul(bank_tiles(2 * p, 2)[:, l, :], KL[p][:, l if l < 7 else 8, :],
                                  QL[p][:, l + 1, :], start=True, stop=True)
                    pe.wait_ge(hg_state, n * 4 + h + 1)
                    pe.transpose(PS[:, 6 + p, 0:128], KL[p][:, 7, :], ident).then_inc(hg_scores, 1)

                def outputs(h):
                    p = h % 2
                    vals = INP[:, bass.ds(n, 1), h * 128:(h + 1) * 128].rearrange("p o e -> p (o e)")
                    pe.wait_ge(hg_mask, n * 4 + h + 3)
                    pe.wait_ge(hg_out, n * 4 + h + 1)
                    for l in range(8):
                        pe.matmul(PS[:, 4 + p, 0:128], M[p][:, l, :], vals, start=l == 0, stop=False)
                    pe.matmul(PS[:, 4 + p, 0:128], QL[p][:, 0, :], STATE[:, h, :], start=False, stop=True)
                    pe.wait_ge(hg_kn, n * 4 + h + 1)
                    pe.matmul(PS[:, 6 + p, 0:128], KN[p][:, :], vals, start=True, stop=True).then_inc(hg_pe, 1)

                scores(0)
                scores(1)
                outputs(0)
                scores(2)
                outputs(1)
                scores(3)
                outputs(2)
                outputs(3)
            stage_end(pe, 3)
            def att_scores(u):
                h, b = att[u]
                if u >= 1:
                    pe.wait_ge(at_exp, 2 * u)
                for c in range(2):
                    for n0 in range(0, (b + 1) * P, 512):
                        n1 = min((b + 1) * P, n0 + 512)
                        mm = pe.matmul(PS[:, 2 * c + n0 // 512, 0:n1 - n0],
                                       DQ[64 * c:64 * c + 64, h, b * P:(b + 1) * P],
                                       DK[64 * c:64 * c + 64, h, n0:n1], start=True, stop=True)
                    mm.then_inc(at_s, 1)

            def att_turn(u):
                h, b = att[u]
                pe.wait_ge(at_comb, u + 1)
                if u >= 1:
                    pe.wait_ge(at_t, u)
                for j in range(b + 1):
                    mm = pe.transpose(PS[:, 4 + j // 4, (j % 4) * P:(j % 4 + 1) * P],
                                      PR[u % 2][0][:, j * P:(j + 1) * P], ident)
                mm.then_inc(at_tr, 1)

            def att_out(u):
                h, b = att[u]
                pe.wait_ge(at_t, u + 1)
                if u >= 2:
                    pe.wait_ge(at_oe, u - 1)
                for j in range(b + 1):
                    mm = pe.matmul(PS[:, 6 + u % 2, 0:128], AT[u % 2][:, j, :], DV[:, j, h * 128:(h + 1) * 128],
                                   start=j == 0, stop=j == b)
                mm.then_inc(at_o, 1)

            for u in range(len(att) + 2):
                if u < len(att):
                    att_scores(u)
                if u >= 2:
                    att_out(u - 2)
                if 1 <= u <= len(att):
                    att_turn(u - 1)
            stage_end(pe, 4)
            stage_end(pe, 5)
            def turn_mixed(t):
                if t >= 1:
                    pe.wait_ge(mt_act, t)
                    pe.wait_ge(mt_dve, t)
                for k in range(KD):
                    src = INP if k < 4 else DA
                    mm = pe.transpose(PS[:, k // 4, (k % 4) * P:(k % 4 + 1) * P], src[:, t, (k % 4) * P:(k % 4 + 1) * P], ident)
                mm.then_inc(mt_tr, 1)

            def project_out(t):
                pe.wait_ge(mt_act, t + 1)
                pe.wait_ge(mt_dve, t + 1)
                if t >= 1:
                    pe.wait_ge(h_ready, t)
                for dh in range(2):
                    for k in range(KD):
                        mm = pe.matmul(bank(2 + dh), MT[:, k, t * P:(t + 1) * P], WO[:, k, dh * 512:(dh + 1) * 512],
                                       start=k == 0, stop=k == KD - 1)
                mm.then_inc(wo_done, 1)

            def turn_n2(t):
                pe.wait_ge(n2_ready, t + 1)
                if t >= 2:
                    pe.wait_ge(n2_lo, t - 1)
                for k in range(KD):
                    mm = pe.transpose(PS[:, 4 + 2 * (t % 2) + k // 4, (k % 4) * P:(k % 4 + 1) * P],
                                      N2[t % 2][:, k * P:(k + 1) * P], ident)
                mm.then_inc(n2_tr, 1)

            pe.wait_ge(wo_in, 32)
            turn_mixed(0)
            for t in range(TT + 1):
                if t + 1 < TT:
                    turn_mixed(t + 1)
                if t < TT:
                    project_out(t)
                if t >= 1:
                    turn_n2(t - 1)
            stage_end(pe, 6)
            if stop == 6:
                return
            pe.wait_ge(consts_in, 16 * 8)

            def queries(m):
                pe.wait_ge(wq_lo, m + 1)
                if m >= 1:
                    pe.wait_ge(qh_out, m)
                for th in range(2):
                    ts = slice(th * 512, (th + 1) * 512)
                    for k in range(KD):
                        for j, (a, b) in enumerate(((WQH, N2H), (WQH, N2L), (WQL, N2H))):
                            mm = pe.matmul(bank(th), a[m % 2][:, k, :], b[:, k, ts], start=k == 0 and j == 0,
                                           stop=k == KD - 1 and j == 2)
                mm.then_inc(qh_done, 1)

            def key_scores(m):
                pe.wait_ge(qh_out, m + 1)
                if m >= 2:
                    pe.wait_ge(sc_out, m - 1)
                for t in range(TT):
                    mm = pe.matmul(PS[:, 4 + 2 * (m % 2) + t // 4, (t % 4) * P:(t % 4 + 1) * P],
                                   QH[m % 2][:, t * P:(t + 1) * P], SUB[:, m, :], start=True, stop=True)
                mm.then_inc(sc_done, 1)

            for m in range(17):
                if m < 16:
                    queries(m)
                if m >= 1:
                    key_scores(m - 1)
            stage_end(pe, 7)
            with pe.Fori(0, TT) as t:
                pe.wait_ge(pk_ready, t + 1)
                pe.wait_ge(pt_ready, t + 1)
                for j in range(3):
                    mm = pe.transpose(PS[:, 0, j * P:(j + 1) * P], PK[:, j, :], ident)
                mm.then_inc(pk_tr, 1)
            stage_end(pe, 8)
            with pe.Fori(0, T // 8) as i:
                for p in range(2):
                    pe.wait_ge(oh_ready, i * 2 + p + 1)
                    pe.wait_ge(quad_out, i * 2 + p + 1)
                    for j in range(4):
                        mm = pe.matmul(PS[:, p, j * P:(j + 1) * P], OH[p][j][:, :], OG[p][j][:, :], start=True, stop=True)
                    mm.then_inc(quad_done, 1)
            stage_end(pe, 9)
            for half in range(2):
                c0 = half * KEYS
                ts = slice(half * HALF_T, (half + 1) * HALF_T)

                def first(c, j):
                    pe.wait_ge(ul, c0 + c + 3)
                    pe.wait_ge(gelu, c0 + c + 1)
                    for k in range(KD):
                        for q, (a, b) in enumerate(((UH, N2H), (UH, N2L), (UL, N2H))):
                            mm = pe.matmul(bank(j % 2), a[j % 2][:, k, :], b[:, k, ts], start=k == 0 and q == 0,
                                           stop=k == KD - 1 and q == 2)
                    mm.then_inc(s1, 1)

                def second(g, j):
                    pe.wait_ge(al, c0 + g * 2 + 4)
                    pe.wait_ge(vl, c0 + g * 2 + 4)
                    for t in range(8):
                        tt, dh = divmod(t, 2)
                        pe.wait_ge(acc_add, (c0 // 2) * 8 + g * 8 + t + 1)
                        for c in (2 * j, 2 * j + 1):
                            for q, (a, b) in enumerate(((AH, VH), (AH, VL), (AL, VH))):
                                mm = pe.matmul(bank(2 + t % 4), a[c][:, tt * P:(tt + 1) * P], b[c][:, dh * 512:(dh + 1) * 512],
                                               start=c == 2 * j and q == 0, stop=c == 2 * j + 1 and q == 2)
                        mm.then_inc(s2, 1)

                first(0, 0)
                first(1, 1)
                with pe.Fori(0, KEYS // 4 - 1) as i:
                    for j in range(2):
                        first(i * 4 + (2 * j + 2), 0)
                        first(i * 4 + (2 * j + 3), 1)
                        second(i * 2 + j, j)
                first(KEYS - 2, 0)
                first(KEYS - 1, 1)
                second(KEYS // 2 - 2, 0)
                second(KEYS // 2 - 1, 1)

        @block.scalar
        def _(act):
            link = Links(act, act_own)
            act.sem_inc(hg_out, 2)
            act.sem_inc(gelu, 2)
            act.sem_inc(quad_out, 2)
            act.sem_inc(pt_ready, 1)
            for k in range(KD):
                act.wait_ge(x_in[k], 16)
                if k >= 2:
                    act.wait_ge(sq_used, k - 1)
                act.activation(sq[k % 2][:, :], X[:, k, :], ACT.Square).then_inc(sq_ready, 1)
            act.wait_ge(sq_used, KD)
            act.wait_ge(ready, 1)
            act.activation(rstd[:, :].rearrange("p (a b) -> p a b", a=2), bank(0, 2), ACT.Sqrt, bias=eps,
                           scale=1.0 / D).then_inc(root_ready, 1)
            act.wait_ge(ready, 2)
            link(act.activation(lb_t, lb_t, ACT.Exp))
            act.activation(lam_t, lam_t, ACT.Exp).then_inc(root_ready, 1)
            stage_end(act, 1)
            for G in range(8 * SECTIONS):
                if taker(G) != "act":
                    continue
                act.wait_ge(proj_done, G + 1)
                func = {1: ACT.Sigmoid, 3: ACT.Silu}.get(G // 8, ACT.Copy)
                act.activation(proj_dst(G), bank(G % 4), func, scale=P ** -0.5 if G // 8 == 0 else 1.0
                               ).then_inc(proj_out["act"], 1)
            stage_end(act, 2)
            for h in range(HEADS):
                act.wait_ge(log_f, h + 1)
                act.activation(F[:, h, :], F[:, h, :], ACT.Ln).then_inc(ready, 1)
            with act.Fori(0, TT) as n:
                def decay(h):
                    act.wait_ge(hg_diff, n * 4 + h + 1)
                    act.activation(E[h % 2][:, :, :], E[h % 2][:, :, :], ACT.Exp).then_inc(hg_exp, 1)

                def turned(h):
                    act.wait_ge(hg_scores, n * 4 + h + 1)
                    act.wait_ge(hg_pe, n * 4 + h + 1)
                    act.copy(KN[h % 2][:, :], PS[:, 6 + h % 2, 0:128]).then_inc(hg_kn, 1)

                def result(h):
                    act.wait_ge(hg_pe, n * 4 + h + 3)
                    act.copy(INP[:, bass.ds(n, 1), h * 128:(h + 1) * 128].rearrange("p o e -> p (o e)"),
                             PS[:, 4 + h % 2, 0:128]).then_inc(hg_out, 1)

                decay(0)
                decay(1)
                turned(0)
                decay(2)
                turned(1)
                result(0)
                decay(3)
                turned(2)
                result(1)
                turned(3)
                result(2)
                result(3)
            stage_end(act, 3)
            def att_exp(u):
                h, b = att[u]
                nk = (b + 1) * P
                for c in range(2):
                    act.wait_ge(at_max, 2 * u + c + 1)
                    if u >= 2 and c == 0:
                        act.wait_ge(at_tr, u - 1)
                    act.activation(PR[u % 2][c][:, 0:nk], PS[:, 2 * c:2 * c + 2, :].rearrange("p a b -> p (a b)")[:, 0:nk],
                                   ACT.Exp, bias=nmx[:, u % 2, c:c + 1], scale=0.125,
                                   accum_out=l_sum[:, u % 2, c:c + 1]).then_inc(at_exp, 1)

            for u in range(len(att) + 2):
                if u < len(att):
                    att_exp(u)
                if 1 <= u <= len(att):
                    h, b = att[u - 1]
                    act.wait_ge(at_tr, u)
                    if u >= 3:
                        act.wait_ge(at_o, u - 2)
                    act.copy(AT[(u - 1) % 2][:, 0:b + 1, :], bank_tiles(4, 2)[:, 0:b + 1, :]).then_inc(at_t, 1)
                if u >= 2:
                    h, b = att[u - 2]
                    act.wait_ge(at_o, u - 1)
                    act.copy(DA[:, b, h * 128:(h + 1) * 128], PS[:, 6 + u % 2, 0:128]).then_inc(at_oe, 1)
            stage_end(act, 4)
            for i in range(2 * TT):
                t, da = i % TT, i // TT
                if i >= 2:
                    act.wait_ge(nrm_ss, i - 1)
                act.activation(SQN[i % 2][:, :], (DA if da else INP)[:, t, :], ACT.Square).then_inc(nrm_sq, 1)
                if i % TT == TT - 1:
                    act.wait_ge(nrm_ss, i + 1)
                    act.activation(norm_r[:, :], norm_ss[:, :], ACT.Sqrt, bias=eps, scale=1.0 / P).then_inc(nrm_root, 1)
                    act.wait_ge(nrm_r, da + 1)
            stage_end(act, 5)
            for t in range(TT + 1):
                if t < TT:
                    act.wait_ge(mt_tr, t + 1)
                    act.copy(MT[:, 0:4, t * P:(t + 1) * P], bank_tiles(0)).then_inc(mt_act, 1)
                if t >= 1:
                    act.wait_ge(n2_tr, t)
                    b = 4 + 2 * ((t - 1) % 2)
                    act.copy(N2H[:, :, (t - 1) * P:t * P], bank_tiles(b, 2)).then_inc(n2_hi, 1)
                if t < TT:
                    act.wait_ge(h_ready, t + 1)
                    link(act.activation(junk[:, :], H[t % 2][:, :], ACT.Square, accum_out=norm_ss[:, t:t + 1]))
                    act.activation(norm_ss[:, t:t + 1], norm_ss[:, t:t + 1], ACT.Sqrt, bias=eps, scale=1.0 / D).then_inc(h_ss, 1)
            stage_end(act, 6)
            if stop == 6:
                return
            def wq_split(m):
                if m % 4 == 0:
                    act.wait_ge(wq_in[(m // 4) % 2], 16 * (m // 8 + 1))
                if m >= 2:
                    act.wait_ge(qh_done, m - 1)
                act.copy(WQH[m % 2][:, :, :], WQ[(m // 4) % 2][:, :, (m % 4) * P:(m % 4 + 1) * P]).then_inc(wq_hi, 1)

            wq_split(0)
            for m in range(16):
                if m + 1 < 16:
                    wq_split(m + 1)
                act.wait_ge(qh_done, m + 1)
                if m >= 2:
                    act.wait_ge(sc_done, m - 1)
                act.copy(QH[m % 2][:, :].rearrange("p (a b) -> p a b", a=2), bank(0, 2)).then_inc(qh_out, 1)
                act.wait_ge(sc_done, m + 1)
                if m >= 2:
                    act.wait_ge(ss_out[m % 2], 16 * (m // 2))
                act.copy(SS[m % 2][:, :, :], bank_tiles(4 + 2 * (m % 2), 2)).then_inc(sc_out, 1)
            stage_end(act, 7)
            act.wait_ge(g_shift, 1)
            act.activation(CS[:, :], CS[:, :], ACT.Exp).then_inc(g_exp, 1)
            with act.Fori(0, TT) as t:
                act.wait_ge(pk_tr, t + 2)
                act.copy(PT[:, :, bass.ds(t * P, P)], bank_tiles(0)[:, 0:3, :]).then_inc(pt_ready, 1)
            stage_end(act, 8)
            for t in range(T // 64):
                if t >= 2:
                    act.wait_ge(gs_out[t % 2], 16 * (t // 2))
                with act.Fori(0, 64 // 8) as i:
                    for p in range(2):
                        act.wait_ge(quad_done, i * 2 + (t * 16 + p + 3))
                        act.copy(GS[t % 2][:, :, bass.ds(i * 8 + 4 * p, 4)].rearrange("p a t -> p t a"),
                                 bank_tiles(p)).then_inc(quad_out, 1)
            stage_end(act, 9)
            for half in range(2):
                c0 = half * KEYS

                def u_hi(c, j):
                    act.wait_ge(s1, c0 + c + 1)
                    act.wait_ge(u_in[j % 2], turns(c, j))
                    act.copy(UH[j % 2][:, :, :], UR[j % 2][:, :, :]).then_inc(uh, 1)

                def v_hi(c, j):
                    act.wait_ge(s2, buffers_free(c, j))
                    act.wait_ge(v_in[j % 2], turns(c, j))
                    act.copy(VH[j % 4][:, :], VR[j % 2][:, :]).then_inc(vh, 1)

                def turns(c, j):
                    return (c - j % 2 + c0) * 8 + 16

                def buffers_free(c, j):
                    return (c - j % 2 + c0) * 4 + 8

                def act_gelu(c, j):
                    act.wait_ge(al, c0 + c + 1)
                    act.wait_ge(s1, c0 + c + 3)
                    act.activation(AF[j % 2][:, :], bank(j % 2), ACT.Gelu_apprx_tanh).then_inc(gelu, 1)

                def a_hi(c, j):
                    act.wait_ge(s2, buffers_free(c, j))
                    act.wait_ge(prod, c0 + c + 3)
                    act.copy(AH[j % 4][:, :], AF[j % 2][:, :]).then_inc(ah, 1)

                def period(c, j, more_u=True):
                    for q in range(2):
                        act_gelu(c + q, j + q)
                        a_hi(c + q, j + q)
                    for q in range(2):
                        v_hi(c + q, j + q)
                        if more_u:
                            u_hi(c + 2 + q, j + q)

                u_hi(0, 0)
                u_hi(1, 1)
                period(0, 0)
                with act.Fori(0, KEYS // 4 - 1) as i:
                    period(i * 4 + 2, 2)
                    period(i * 4 + 4, 0)
                period(KEYS - 2, 2, more_u=False)
                for t in range(4):
                    act.wait_ge(acc_add, (half + 1) * KEYS * 4 + 4)
                    if t == 0:
                        act.wait_ge(acc_in, 16 * (half + 1))
                    link(act.activation(FSQ[:, :], ACC[:, t, :], ACT.Square, accum_out=norm_ss[:, t:t + 1]))
                act.activation(norm_ss[:, 0:4], norm_ss[:, 0:4], ACT.Sqrt, bias=eps, scale=1.0 / D).then_inc(y_root, 1)

        @block.vector
        def _(dve):
            link = Links(dve, dve_own)
            dve.sem_inc(hg_mask, 2)
            dve.sem_inc(hg_q, 2)
            dve.sem_inc(hg_state, 2)
            dve.sem_inc(su_used, 4)
            dve.sem_inc(ul, 2)
            dve.sem_inc(prod, 2)
            dve.sem_inc(al, 2)
            dve.sem_inc(acc_add, 4)
            link(dve.memset(zeros[:, :], 0.0))
            dve.memset(eps, EPS).then_inc(ready, 1)
            dve.wait_ge(consts_in, 16 * 7)
            link(dve.tensor_tensor(lb_t[:, 0:4], lb_in[:, 0, :], lb_in[:, 1, :], ALU.max))
            link(dve.tensor_tensor(lb_t[:, 4:8], lb_in[:, 1, :], lb_t[:, 0:4], ALU.subtract))
            link(dve.tensor_tensor(lb_t[:, 0:4], lb_in[:, 0, :], lb_t[:, 0:4], ALU.subtract))
            for r in range(2):
                link(dve.tensor_tensor(lam_in[:, 2 * r, :], lam_in[:, 2 * r, :], lam_in[:, 2 * r + 1, :], ALU.mult))
                ins = dve.reduce_sum(lam_t[:, r:r + 1], lam_in[:, 2 * r, :], AX_X)
                if r == 0:
                    link(ins)
                else:
                    ins.then_inc(ready, 1)
            dve.wait_ge(root_ready, 1)
            link(dve.reciprocal(rstd[:, :], rstd[:, :]))
            for k in range(KD):
                link(dve.scalar_tensor_tensor(out=X[:, k, :], in0=X[:, k, :], scalar=mix_w[:, k:k + 1], in1=rstd[:, :],
                                              op0=ALU.mult, op1=ALU.mult))
            dve.wait_ge(root_ready, 2)
            link(dve.tensor_tensor(one_lb, lb_t[:, 0:4], lb_t[:, 4:8], ALU.add))
            link(dve.reciprocal(one_lb, one_lb))
            link(dve.tensor_tensor(lbs, lb_t[:, 0:4], one_lb, ALU.mult))
            link(dve.tensor_scalar(one_lb, lbs, -1.0, 1.0, ALU.mult, ALU.add))
            link(dve.tensor_tensor(lams, lam_t[:, 0:1], lam_t[:, 1:2], ALU.subtract))
            link(dve.tensor_scalar(lams, lams, LAMBDA_INIT, None, ALU.add))
            stage_end(dve, 1)
            for G in range(8 * SECTIONS):
                if taker(G) != "dve":
                    continue
                dve.wait_ge(proj_done, G + 1)
                dve.tensor_scalar(proj_dst(G), bank(G % 4), P ** -0.5 if G // 8 == 0 else 1.0, None, ALU.mult
                                  ).then_inc(proj_out["dve"], 1)
            stage_end(dve, 2)
            for h in range(HEADS):
                link(dve.tensor_scalar(F[:, h, :], F[:, h, :], one_lb[:, h:h + 1], lbs[:, h:h + 1], ALU.mult, ALU.add))
                dve.tensor_scalar(K[:, h, :], F[:, h, :], -1.0, 1.0, ALU.mult, ALU.add).then_inc(log_f, 1)
            link(dve.memset(STATE[:, :, :], 0.0))
            dve.wait_ge(ready, 2 + HEADS)
            with dve.Fori(0, TT) as n:
                link.loop(n, 3 * HEADS)

                def differences(h):
                    d = E[h % 2]
                    dve.wait_ge(hg_q, n * 4 + h + 1)
                    dve.wait_ge(hg_k, n * 4 + h + 1)
                    b = d[:, 0, :]
                    link(dve.tensor_tensor_scan(b, F[:, h, bass.ds(n * P, P)], zeros[:, :], 0.0, ALU.add, ALU.add))
                    for l in range(LEVELS):
                        m = 64 >> l
                        view = b.rearrange("p (a m) -> p a m", m=2 * m)
                        dve.tensor_tensor(d[:, 1 + l, :].rearrange("p (a m) -> p a m", m=2 * m), view,
                                          view[:, :, m - 1:m].broadcast_to([P, P // (2 * m), 2 * m]), ALU.subtract)
                    link(dve.tensor_scalar(d[:, 8, :], b, b[:, P - 1:P], None, ALU.subtract))
                    dve.scalar_tensor_tensor(out=d[:, :, :], in0=d[:, :, :], scalar=-1.0, in1=d[:, :, :],
                                             op0=ALU.mult, op1=ALU.min).then_inc(hg_diff, 1)

                def queries(h):
                    p = h % 2
                    q = Q[:, h, bass.ds(n * P, P)]
                    dve.wait_ge(hg_pe, n * 4 + h + 1)
                    dve.wait_ge(hg_exp, n * 4 + h + 1)
                    dve.wait_ge(hg_state, n * 4 + h + 1)
                    dve.tensor_copy(QL[p][:, 8, :], q)
                    link(dve.tensor_copy(BL[p][:, :], E[p][:, 0, P - 1:P]))
                    dve.tensor_tensor(QL[p][:, 0:8, :], E[p][:, 0:8, :], spread(q, 1, 8), ALU.mult).then_inc(hg_q, 1)

                def mask(h):
                    p = h % 2
                    dve.wait_ge(hg_scores, n * 4 + h + 1)
                    dve.wait_ge(hg_pe, n * 4 + h + 1)
                    dve.tensor_tensor(M[p][:, :, :], bank_tiles(2 * p, 2), masks[:, :, :], ALU.mult).then_inc(hg_mask, 1)

                def state(h):
                    dve.wait_ge(hg_pe, n * 4 + h + 3)
                    dve.scalar_tensor_tensor(out=STATE[:, h, :], in0=STATE[:, h, :], scalar=BL[h % 2][:, :],
                                             in1=PS[:, 6 + h % 2, 0:128], op0=ALU.mult, op1=ALU.add).then_inc(hg_state, 1)

                differences(0)
                differences(1)
                queries(0)
                differences(2)
                queries(1)
                mask(0)
                differences(3)
                state(0)
                queries(2)
                mask(1)
                state(1)
                queries(3)
                mask(2)
                state(2)
                mask(3)
                state(3)
                link.end(TT)
            stage_end(dve, 3)
            for u in range(len(att) + 1):
                if u >= 1:
                    h, b = att[u - 1]
                    p, nk = (u - 1) % 2, (b + 1) * P
                    dve.wait_ge(at_exp, 2 * u)
                    link(dve.reciprocal(l_rec[:, p, :], l_sum[:, p, :]))
                    link(dve.tensor_scalar(l_rec[:, p, 1:2], l_rec[:, p, 1:2], lams, None, ALU.mult))
                    link(dve.tensor_scalar(PR[p][1][:, 0:nk], PR[p][1][:, 0:nk], l_rec[:, p, 1:2], None, ALU.mult))
                    dve.scalar_tensor_tensor(out=PR[p][0][:, 0:nk], in0=PR[p][0][:, 0:nk], scalar=l_rec[:, p, 0:1],
                                             in1=PR[p][1][:, 0:nk], op0=ALU.mult, op1=ALU.subtract).then_inc(at_comb, 1)
                if u < len(att):
                    h, b = att[u]
                    nk = (b + 1) * P
                    for c in range(2):
                        s = PS[:, 2 * c:2 * c + 2, :].rearrange("p a b -> p (a b)")
                        dve.wait_ge(at_s, 2 * u + c + 1)
                        link(dve.memset(s[0:CHUNK, nk - CHUNK:nk], -1.0e30))
                        link(dve.reduce_max(mx[:, u % 2, c:c + 1], s[:, 0:nk], AX_X))
                        dve.tensor_scalar(nmx[:, u % 2, c:c + 1], mx[:, u % 2, c:c + 1], -0.125, None, ALU.mult
                                          ).then_inc(at_max, 1)
            stage_end(dve, 4)
            link(dve.tensor_scalar(da_gain[:, :], da_gain[:, :], 1.0 - LAMBDA_INIT, None, ALU.mult))
            for da in range(2):
                buf = DA if da else INP
                for t in range(TT):
                    i = da * TT + t
                    dve.wait_ge(nrm_sq, i + 1)
                    dve.reduce_sum(norm_ss[:, t * 4:t * 4 + 4], SQN[i % 2][:, :].rearrange("p (h e) -> p h e", h=4), AX_X
                                   ).then_inc(nrm_ss, 1)
                dve.wait_ge(nrm_root, da + 1)
                link(dve.reciprocal(norm_r[:, :], norm_r[:, :]))
                if not da:
                    dve.wait_ge(gate_gain, TT)
                for t in range(TT):
                    o = buf[:, t, :].rearrange("p (h e) -> p h e", h=4)
                    link(dve.tensor_tensor(o, o, spread(norm_r[:, t * 4:t * 4 + 4], 2, P), ALU.mult))
                    by = spread(da_gain[:, :], 1, 4) if da else GATE[:, t, :].rearrange("p (h e) -> p h e", h=4)
                    ins = dve.tensor_tensor(o, o, by, ALU.mult)
                    if t == TT - 1:
                        ins.then_inc(nrm_r, 1)
            stage_end(dve, 5)
            dve.wait_ge(wo_in, 32)
            for t in range(TT + 1):
                if t < TT:
                    dve.wait_ge(mt_tr, t + 1)
                    dve.tensor_copy(MT[:, 4:8, t * P:(t + 1) * P], bank_tiles(1)).then_inc(mt_dve, 1)
                if t >= 1:
                    dve.wait_ge(n2_hi, t)
                    b = 4 + 2 * ((t - 1) % 2)
                    ts = slice((t - 1) * P, t * P)
                    dve.tensor_tensor(N2L[:, :, ts], bank_tiles(b, 2), N2H[:, :, ts].bitcast(F32), ALU.subtract).then_inc(n2_lo, 1)
                if t < TT:
                    dve.wait_ge(wo_done, t + 1)
                    dve.wait_ge(xn_in[t % 2], 16 * (t // 2 + 1))
                    if t >= 2:
                        dve.wait_ge(h_out[t % 2], 16 * (t // 2))
                    dve.tensor_tensor(H[t % 2][:, :].rearrange("p (a b) -> p a b", a=2), bank(2, 2),
                                      XN[t % 2][:, :].rearrange("p (a b) -> p a b", a=2), ALU.add).then_inc(h_ready, 1)
                    dve.wait_ge(h_ss, t + 1)
                    link(dve.reciprocal(norm_r[:, t:t + 1], norm_ss[:, t:t + 1]))
                    if t >= 2:
                        dve.wait_ge(n2_tr, t - 1)
                    dve.scalar_tensor_tensor(out=N2[t % 2][:, :], in0=H[t % 2][:, :], scalar=norm_r[:, t:t + 1],
                                             in1=ffn_w[:, :], op0=ALU.mult, op1=ALU.mult).then_inc(n2_ready, 1)
            stage_end(dve, 6)
            if stop == 6:
                return
            for m in range(16):
                dve.wait_ge(wq_hi, m + 1)
                dve.tensor_tensor(WQL[m % 2][:, :, :], WQ[(m // 4) % 2][:, :, (m % 4) * P:(m % 4 + 1) * P],
                                  WQH[m % 2][:, :, :].bitcast(F32), ALU.subtract).then_inc(wq_lo, 1)
            stage_end(dve, 7)
            def top16(src, src2, vals, idx):
                for s, v in zip(src, vals):
                    dve.max(v[:, 0:8], s)
                dve.drain()
                for s, v, i in zip(src, vals, idx):
                    dve.max_index(i[:, 0:8], v[:, 0:8], s)
                for s, s2, v in zip(src, src2, vals):
                    dve.match_replace(s2, v[:, 0:8], s, LOWEST)
                dve.drain()
                for s2, v in zip(src2, vals):
                    dve.max(v[:, 8:16], s2)
                dve.drain()
                for s2, v, i in zip(src2, vals, idx):
                    dve.max_index(i[:, 8:16], v[:, 8:16], s2)
                dve.drain()

            with dve.Fori(0, UNITS // 4) as i:
                for j in range(4):
                    dve.wait_ge(su_in[j], i * 16 + 16)
                    dve.tensor_copy(su_seen[:, :], SU[j][:, 0, 0:1])
                    dve.drain()
                    top16([SU[j][:, a, :] for a in range(2)], [SU2[j % 2][:, a, :] for a in range(2)],
                          [TOPV[:, a, :] for a in range(2)], [TOPI[:, a, :] for a in range(2)])
                    col = bass.ds(i * 4 * TOPK + j * TOPK, TOPK)
                    dve.tensor_copy(I12[:, :, col], TOPI[:, :, :]).then_inc(su_used, 1)
                    dve.tensor_tensor(CAND[:, :].rearrange("p (a b) -> p a b", a=TOPK), spread(TOPV[:, 0, :], 2, TOPK),
                                      spread(TOPV[:, 1, :], 1, TOPK), ALU.add)
                    dve.drain()
                    top16([CAND[:, :]], [CAND2[:, :]], [TOPC], [TOPP])
                    dve.tensor_copy(CS[:, col], TOPC[:, :])
                    dve.tensor_copy(POS[:, col], TOPP[:, :])
            dve.drain()
            cs = CS[:, :].rearrange("p (u k) -> p u k", k=TOPK)
            link(dve.tensor_copy(gmax[:, :], cs[:, :, 0]))
            dve.tensor_tensor(cs, cs, spread(gmax[:, :], 2, TOPK), ALU.subtract).then_inc(g_shift, 1)
            link(dve.tensor_scalar(ABU[:, :], POS[:, :], 4, None, ALU.logical_shift_right))
            link(dve.tensor_copy(AB[0][:, :], ABU[:, :]))
            link(dve.tensor_scalar(ABU[:, :], POS[:, :], 15, None, ALU.bitwise_and))
            link(dve.tensor_copy(AB[1][:, :], ABU[:, :]))
            dve.wait_ge(g_exp, 1)
            link(dve.reduce_sum(gsum[:, :], cs, AX_X))
            link(dve.reciprocal(grec[:, :], gsum[:, :]))
            link(dve.tensor_tensor(cs, cs, spread(grec[:, :], 2, TOPK), ALU.mult))
            with dve.Fori(0, TT) as t:
                link.loop(t, 4)
                eq = EQ[:, :].rearrange("p (h k a) -> p h k a", h=PEER_HEADS, k=TOPK)
                eq2 = EQ2[:, :].rearrange("p (h k a) -> p h k a", h=PEER_HEADS, k=TOPK)
                dve.wait_ge(pk_tr, t + 1)
                for a in range(2):
                    tile = bass.ds(t * P, P)
                    link(dve.tensor_tensor(EQ[:, :].rearrange("p (k a) -> p k a", a=TOPK), spread(AB[a][:, tile], 2, TOPK),
                                           spread(iota16, 1, P), ALU.is_equal))
                    keys = I12[:, a, tile].rearrange("p (h a) -> p h a", a=TOPK)
                    link(dve.tensor_tensor(eq2, eq, spread(keys, 2, TOPK), ALU.mult))
                    ins = dve.reduce_sum(PK[:, a, :], EQ2[:, :].rearrange("p (k a) -> p k a", a=TOPK), AX_X)
                dve.tensor_copy(PK[:, 2, :], CS[:, tile]).then_inc(pk_ready, 1)
                link.end(TT)
            stage_end(dve, 8)
            with dve.Fori(0, T // 8) as i:
                for p in range(2):
                    dve.wait_ge(quad_done, i * 2 + p + 1)
                    for j in range(4):
                        tok = bass.ds(i * 8 + 4 * p + j, 1)
                        dve.tensor_scalar(OH[p][j][:, :], iota, PT[:, 1, tok], None, ALU.is_equal)
                        ins = dve.tensor_scalar(OG[p][j][:, :], iota, PT[:, 0, tok], PT[:, 2, tok], ALU.is_equal, ALU.mult)
                    ins.then_inc(oh_ready, 1)
            stage_end(dve, 9)
            for half in range(2):
                c0 = half * KEYS

                def u_lo(c, j):
                    dve.wait_ge(uh, c0 + c + 1)
                    dve.tensor_tensor(UL[j % 2][:, :, :], UR[j % 2][:, :, :], UH[j % 2][:, :, :].bitcast(F32),
                                      ALU.subtract).then_inc(ul, 1)

                def gated(c, j):
                    dve.wait_ge(gelu, c0 + c + 3)
                    dve.wait_ge(g_in[j % 2], (c - j % 2 + c0) * 8 + 16)
                    dve.tensor_tensor(AF[j % 2][:, :], AF[j % 2][:, :], GT[j % 2][:, :], ALU.mult).then_inc(prod, 1)

                def a_lo(c, j):
                    dve.wait_ge(ah, c0 + c + 1)
                    dve.tensor_tensor(AL[j % 4][:, :], AF[j % 2][:, :], AH[j % 4][:, :].bitcast(F32),
                                      ALU.subtract).then_inc(al, 1)

                def add(g, t):
                    tt, dh = divmod(t, 2)
                    y = ACC[:, tt, dh * 512:(dh + 1) * 512]
                    dve.wait_ge(s2, (c0 // 2) * 8 + g * 8 + t + 17)
                    dve.tensor_tensor(y, bank(2 + t % 4), y, ALU.add).then_inc(acc_add, 1)

                def period(c, j, g=None, more_u=True):
                    gated(c, j)
                    a_lo(c, j)
                    gated(c + 1, j + 1)
                    if g is not None:
                        add(g, 0)
                    a_lo(c + 1, j + 1)
                    for q in range(2):
                        if g is not None:
                            add(g, 3 * q + 1)
                            add(g, 3 * q + 2)
                        if more_u:
                            u_lo(c + 2 + q, j + q)
                        if g is not None:
                            add(g, 3 * q + 3)
                    if g is not None:
                        add(g, 7)

                u_lo(0, 0)
                u_lo(1, 1)
                period(0, 0)
                dve.wait_ge(acc_in, 16 * (half + 1))
                with dve.Fori(0, KEYS // 4 - 1) as i:
                    period(i * 4 + 2, 2, i * 2)
                    period(i * 4 + 4, 0, i * 2 + 1)
                period(KEYS - 2, 2, KEYS // 2 - 2, more_u=False)
                for t in range(8):
                    add(KEYS // 2 - 1, t)
                dve.wait_ge(y_root, half + 1)
                dve.wait_ge(consts_in, 16 * 9)
                link(dve.reciprocal(norm_r[:, 0:4], norm_ss[:, 0:4]))
                for t in range(4):
                    dve.scalar_tensor_tensor(out=ACC[:, t, :], in0=ACC[:, t, :], scalar=norm_r[:, t:t + 1], in1=fin_w[:, :],
                                             op0=ALU.mult, op1=ALU.mult).then_inc(y_ready, 1)

        @block.gpsimd
        def _(pool):
            pool.sem_inc(hg_k, 2)
            pool.sem_inc(vl, 2)
            stage_end(pool, 1)
            stage_end(pool, 2)
            pool.wait_ge(ready, 2 + HEADS)
            with pool.Fori(0, TT) as n:
                for h in range(HEADS):
                    p = h % 2
                    k = K[:, h, bass.ds(n * P, P)]
                    pool.wait_ge(hg_pe, n * 4 + h + 1)
                    pool.wait_ge(hg_exp, n * 4 + h + 1)
                    pool.tensor_copy(KL[p][:, 8, :], k)
                    pool.tensor_tensor(KL[p][:, 0:8, :], E[p][:, 1:9, :], spread(k, 1, 8), ALU.mult).then_inc(hg_k, 1)
            stage_end(pool, 3)
            stage_end(pool, 4)
            for t in range(TT):
                g = GATE[:, t, :].rearrange("p (h e) -> p h e", h=4)
                pool.tensor_tensor(g, g, spread(hg_gain[:, :], 1, 4), ALU.mult).then_inc(gate_gain, 1)
            stage_end(pool, 5)
            stage_end(pool, 6)
            if stop == 6:
                return
            for n in (7, 8, 9):
                stage_end(pool, n)
            for half in range(2):
                c0 = half * KEYS

                def v_lo(c, j):
                    pool.wait_ge(vh, c0 + c + 1)
                    pool.tensor_tensor(VL[j % 4][:, :], VR[j % 2][:, :], VH[j % 4][:, :].bitcast(F32),
                                       ALU.subtract).then_inc(vl, 1)

                with pool.Fori(0, KEYS // 4) as i:
                    for j in range(4):
                        v_lo(i * 4 + j, j)


def kernel(x, norm_mix_w, w_in, hgrn_lb_param, hgrn_norm_w, diff_lambda, diff_norm_w, w_out, norm_ffn_w,
           peer_w_query, peer_sub_keys, peer_u, peer_v, norm_final_w):
    import concourse.bacc as bacc
    from concourse.bass_utils import run_bass_kernel_spmd

    def rows(a):
        return np.ascontiguousarray(np.asarray(a).reshape(-1, P, a.shape[-1]).transpose(1, 0, 2))

    def everywhere(a):
        return np.ascontiguousarray(np.broadcast_to(np.asarray(a), (P,) + a.shape))

    t = np.arange(P)
    level_masks = np.zeros((P, 8, P), np.float32)
    for l in range(LEVELS):
        m = 64 >> l
        same = t[:, None] // (2 * m) == t[None, :] // (2 * m)
        level_masks[:, l] = same & (t[None, :] % (2 * m) >= m) & (t[:, None] % (2 * m) < m)
    level_masks[:, 7] = np.eye(P)
    cst = np.concatenate([np.eye(P), np.ones((P, P)), np.broadcast_to(t, (P, P)),
                          np.broadcast_to(np.arange(16), (P, 16))], axis=1).astype(np.float32)
    x = np.asarray(x)
    ins = {
        "x_t": rows(x[0].T), "x_n": np.ascontiguousarray(x[0].reshape(TT, P, D)),
        "w_in": rows(w_in[0]), "w_out": rows(w_out[0]), "w_q": rows(peer_w_query[0]),
        "sub_t": np.ascontiguousarray(np.asarray(peer_sub_keys)[0].reshape(16, KEYS, P).transpose(2, 0, 1)),
        "u_t": np.ascontiguousarray(np.asarray(peer_u)[0].reshape(KEYS, P, KD, P).transpose(0, 3, 2, 1)),
        "v": np.ascontiguousarray(np.asarray(peer_v)[0].reshape(KEYS, P, D)),
        "norm_mix": np.ascontiguousarray(np.asarray(norm_mix_w)[0].reshape(KD, P).T),
        "norm_ffn": everywhere(norm_ffn_w[0]), "norm_fin": everywhere(norm_final_w),
        "lb": np.ascontiguousarray(np.asarray(hgrn_lb_param).reshape(2, HEADS, P).transpose(2, 0, 1)),
        "hg_norm": everywhere(hgrn_norm_w[0]), "da_norm": everywhere(diff_norm_w[0]),
        "lam": everywhere(diff_lambda[0]), "cst": cst, "level_masks": level_masks,
    }
    nc = bacc.Bacc("TRN2", target_bir_lowering=False, num_devices=1)
    args = {n: nc.dram_tensor(n, a.shape, F32, kind="ExternalInput").ap() for n, a in ins.items()}
    out = nc.dram_tensor("out", (TT, P, D), F32, kind="ExternalOutput").ap()
    h_dram = nc.dram_tensor("h_dram", (TT, P, D), F32, kind="Internal").ap()
    s_dram = nc.dram_tensor("s_dram", (TT, PEER_HEADS, P, 2 * KEYS), F32, kind="Internal").ap()
    gates_dram = nc.dram_tensor("gates_dram", (KEYS, KEYS, T), F32, kind="Internal").ap()
    build(nc, **args, out=out, h_dram=h_dram, s_dram=s_dram, gates_dram=gates_dram)
    r = run_bass_kernel_spmd(nc, [ins], core_ids=[0])
    return r.results[0]["out"].reshape(1, T, D)
```

```python
from contextlib import ExitStack

import concourse.bass as bass
import numpy as np
from concourse import mybir

F32 = mybir.dt.float32
F32R = mybir.dt.float32r
U32 = mybir.dt.uint32
ALU = mybir.AluOpType
ACT = mybir.ActivationFunctionType
AX_X = mybir.AxisListType.X

P = 128
T = 1024
D = 1024
KD = D // P
TT = T // P
HEADS = 4
SECTIONS = 7
CHUNK = 64
PEER_HEADS = 8
TOPK = 16
KEYS = 128
UNITS = TT * PEER_HEADS
HALF_T = T // 2
LEVELS = 7
EPS = 1e-6
LAMBDA_INIT = 0.2
LOWEST = -3.0e38


class Links:

    def __init__(self, eng, sem):
        self.eng, self.sem, self.n, self.shift = eng, sem, 0, 0

    def __call__(self, ins):
        self.n += 1
        ins.then_inc(self.sem, 1)
        self.eng.wait_ge(self.sem, self.shift + self.n)

    def mark(self, ins):
        self.n += 1
        ins.then_inc(self.sem, 1)
        return self.n

    def wait(self, n):
        self.eng.wait_ge(self.sem, self.shift + n)

    def loop(self, i, per_turn):
        self.start, self.per_turn, self.shift = self.n, per_turn, i * per_turn

    def end(self, turns):
        assert self.n - self.start == self.per_turn, (self.n - self.start, self.per_turn)
        self.n, self.shift = self.start + turns * self.per_turn, 0


def spread(ap, axis, n):
    ap = ap.unsqueeze(axis)
    shape = list(ap.shape)
    shape[axis] = n
    return ap.broadcast_to(shape)


def build(nc, x_t, x_n, w_in, w_out, w_q, sub_t, u_t, v, norm_mix, norm_ffn, norm_fin, lb, hg_norm,
          da_norm, lam, cst, level_masks, out, h_dram, s_dram, gates_dram, n2_dram, stop=99):
    with ExitStack() as ctx:
        base = (nc.sbuf_base + 127) // 128 * 128
        KB = 1024

        def at(name, kb, shape, dt=F32):
            return nc.alloc_sbuf_tensor_at(name, shape, dt, offset=base + int(kb * KB))

        def sem(name):
            return ctx.enter_context(nc.semaphore(name))

        PS = ctx.enter_context(nc.psum_tensor("PS", [P, 8, 512], F32))

        def bank(b, n=1):
            return PS[:, b, :] if n == 1 else PS[:, b:b + n, :]

        def bank_tiles(b, n=1):
            return PS[:, b:b + n, :].rearrange("p a (b c) -> p (a b) c", c=128)

        consts = at("consts", 0, [P, 400])
        ident, ones, iota, iota16 = consts[:, 0:128], consts[:, 128:256], consts[:, 256:384], consts[:, 384:400]
        masks = at("masks", 2, [P, 8, 128])
        hg_gain = at("hg_gain", 6, [P, 128])
        da_gain = at("da_gain", 6.5, [P, 128])
        lam_in = at("lam_in", 7, [P, 4, 64])
        mix_w = at("mix_w", 8, [P, KD])
        lb_in = at("lb_in", 8.0625, [P, 2, HEADS])
        small = at("small", 8.125, [P, 96])
        eps = small[:, 0:1]
        lbs, one_lb, lb_t = small[:, 4:8], small[:, 8:12], small[:, 12:20]
        lams, lam_t = small[:, 20:21], small[:, 24:26]
        zero_col = small[:, 28:29]
        norm_ss, norm_r = at("norm_ss", 8.5, [P, 32]), at("norm_r", 8.625, [P, 32])
        l_sum, l_rec, mx, nmx = (at(n, 8.75 + i / 16, [P, 2, 2]) for i, n in enumerate(("l_sum", "l_rec", "mx", "nmx")))
        zeros = at("zeros", 9, [P, 128])

        X = at("X", 10, [P, KD, T])
        W = [at(f"W{i}", 42 + 16 * i, [P, KD, 512]) for i in range(2)]
        sq = [at(f"sq{i}", 74 + 4 * i, [P, T]) for i in range(2)]
        rstd = at("rstd", 82, [P, T])
        Q = at("Q", 74, [P, HEADS, T])
        F = at("F", 90, [P, HEADS, T])
        K = at("K", 106, [P, HEADS, T])
        INP = at("INP", 122, [P, TT, 512])
        GATE = at("GATE", 138, [P, TT, 512])
        DQ = at("DQ", 154, [P, HEADS, T])
        DK = at("DK", 170, [P, HEADS, T])
        DV = at("DV", 186, [P, TT, 512])
        E = [at(f"E{i}", 10 + 4.5 * i, [P, 9, 128]) for i in range(2)]
        QL = [at(f"QL{i}", 19 + 4.5 * i, [P, 9, 128]) for i in range(2)]
        KL = [at(f"KL{i}", 28 + 4.5 * i, [P, 9, 128]) for i in range(2)]
        M = [at(f"M{i}", 42 + 4 * i, [P, 8, 128]) for i in range(2)]
        KN = [at(f"KN{i}", 50 + i / 2, [P, 128]) for i in range(2)]
        STATE = at("STATE", 51, [P, HEADS, 128])
        BL = [at(f"BL{i}", 53 + i / 16, [P, 1]) for i in range(2)]
        PR = [[at(f"PR{i}{c}", 74 + 8 * i + 4 * c, [P, T]) for c in range(2)] for i in range(2)]
        AT = [at(f"AT{i}", 90 + 4 * i, [P, TT, 128]) for i in range(2)]
        DA = at("DA", 106, [P, TT, 512])
        SQN = [at(f"SQN{i}", 98 + 2 * i, [P, 512]) for i in range(2)]
        MT = at("MT", 10, [P, KD, T])
        WO = at("WO", 42, [P, KD, D])
        N2H = [at(f"N2H{i}", kb, [P, KD, HALF_T], F32R) for i, kb in enumerate((154, 74))]
        N2L = [at(f"N2L{i}", kb, [P, KD, HALF_T], F32R) for i, kb in enumerate((170, 90))]
        XN = [at(f"XN{i}", 138 + 4 * i, [P, D]) for i in range(2)]
        H = [at(f"H{i}", 146 + 4 * i, [P, D]) for i in range(2)]
        N2 = [at(f"N2{i}", 186 + 4 * i, [P, D]) for i in range(2)]
        ffn_w = at("ffn_w", 194, [P, D])
        junk = at("junk", 198, [P, D])
        WQ = [at(f"WQ{i}", 10 + 16 * i, [P, KD, 512]) for i in range(2)]
        WQH = [at(f"WQH{i}", 42 + 4 * i, [P, KD, 128], F32R) for i in range(2)]
        WQL = [at(f"WQL{i}", 50 + 4 * i, [P, KD, 128], F32R) for i in range(2)]
        QH = [at(f"QH{i}", 58 + 2 * i, [P, HALF_T]) for i in range(2)]
        SUB = at("SUB", 106, [P, 16, 128])
        SS = [at(f"SS{i}", 114 + 2 * i, [P, TT // 2, 128]) for i in range(2)]
        SU = [at(f"SU{i}", 186 + i, [P, 2, 128]) for i in range(2)]
        ABS = at("ABS", 188, [P, 4, 128])
        SU2 = at("SU2", 190, [P, 2, 128])
        TOPV = at("TOPV", 191, [P, 2, TOPK])
        TOPI = at("TOPI", 191.25, [P, 2, TOPK], U32)
        TOPC = at("TOPC", 191.5, [P, TOPK])
        TOPP = at("TOPP", 191.625, [P, TOPK], U32)
        su_seen = at("su_seen", 191.75, [P, 1])
        CAND = at("CAND", 192, [P, TOPK * TOPK])
        CAND2 = at("CAND2", 193, [P, TOPK * TOPK])
        I12 = at("I12", 194, [P, 2, P])
        CS = at("CS", 195, [P, P])
        POS = at("POS", 195.5, [P, P], U32)
        AB = [at(f"AB{i}", 196 + i / 2, [P, P]) for i in range(2)]
        ABU = at("ABU", 197, [P, P], U32)
        gsum, grec, gmax = (at(n, 197.5 + i / 8, [P, PEER_HEADS]) for i, n in enumerate(("gsum", "grec", "gmax")))
        EQ = at("EQ", 66, [P, P * TOPK // 2])
        EQ2 = at("EQ2", 70, [P, P * TOPK // 2])
        PT = [at(f"PT{i}", 2 + 1.5 * i, [P, 3, P]) for i in range(3)]
        PK = at("PK", 6.5, [P, 3, P])
        OH = [at(f"OH{i}", 198 + 2 * i, [P, 4, 128]) for i in range(2)]
        OG = [at(f"OG{i}", 202 + 2 * i, [P, 4, 128]) for i in range(2)]
        GS = [at(f"GS{i}", 74 + 32 * i, [P, KEYS, 64]) for i in range(2)]
        UR = [at(f"UR{i}", 10 + 4 * i, [P, KD, 128]) for i in range(2)]
        VR = [at(f"VR{i}", 18 + 4 * i, [P, D]) for i in range(2)]
        UH = [at(f"UH{i}", 26 + 4 * i, [P, KD, 128], F32R) for i in range(2)]
        UL = [at(f"UL{i}", 34 + 4 * i, [P, KD, 128], F32R) for i in range(2)]
        GT = [at(f"GT{i}", 42 + 2 * i, [P, HALF_T]) for i in range(2)]
        AF = [at(f"AF{i}", 46 + 2 * i, [P, HALF_T]) for i in range(2)]
        AH = [at(f"AH{i}", 50 + 2 * i, [P, HALF_T], F32R) for i in range(4)]
        AL = [at(f"AL{i}", 58 + 2 * i, [P, HALF_T], F32R) for i in range(4)]
        VH = [at(f"VH{i}", 106 + 4 * i, [P, D], F32R) for i in range(4)]
        VL = [at(f"VL{i}", 122 + 4 * i, [P, D], F32R) for i in range(4)]
        ACC = at("ACC", 138, [P, TT // 2, D])
        FSQ = at("FSQ", 66, [P, D])
        fin_w = at("fin_w", 70, [P, D])

        consts_in, x_in = sem("consts_in"), [sem(f"x_in{k}") for k in range(KD)]
        w_in_sem = [sem(f"w_in{i}") for i in range(2)]
        stage_done = sem("stage_done")
        sq_ready, sq_used, root_ready, n1_ready = sem("sq_ready"), sem("sq_used"), sem("root_ready"), sem("n1_ready")
        proj_done = sem("proj_done")
        proj_out = {"act": sem("proj_out_act"), "dve": sem("proj_out_dve")}
        ready = sem("ready")
        log_f = sem("log_f")
        hg_diff, hg_exp, hg_q, hg_k, hg_scores, hg_mask, hg_kn, hg_pe, hg_state, hg_out = (
            sem("hg_" + n) for n in ("diff", "exp", "q", "k", "scores", "mask", "kn", "pe", "state", "out"))
        at_s, at_max, at_exp, at_comb, at_tr, at_t, at_o, at_oe = (
            sem("at_" + n) for n in ("s", "max", "exp", "comb", "tr", "t", "o", "oe"))
        nrm_sq, nrm_ss, nrm_root, nrm_r = sem("nrm_sq"), sem("nrm_ss"), sem("nrm_root"), sem("nrm_r")
        mt_tr, mt_act, mt_dve, wo_in, wo_done, h_ready, h_ss, n2_ready, n2_tr, n2_hi, n2_lo = (
            sem(n) for n in ("mt_tr", "mt_act", "mt_dve", "wo_in", "wo_done", "h_ready", "h_ss", "n2_ready", "n2_tr", "n2_hi", "n2_lo"))
        xn_in = [sem(f"xn_in{i}") for i in range(2)]
        h_out = [sem(f"h_out{i}") for i in range(2)]
        wq_in = [sem(f"wq_in{i}") for i in range(2)]
        wq_hi, wq_lo, qh_done, qh_out, sc_done, sc_out = (sem(n) for n in ("wq_hi", "wq_lo", "qh_done", "qh_out", "sc_done", "sc_out"))
        ss_out = [sem(f"ss_out{i}") for i in range(2)]
        su_in = [sem(f"su_in{i}") for i in range(2)]
        su_used, pk_ready, pk_tr, pt_ready, g_exp, g_shift = (sem(n) for n in ("su_used", "pk_ready", "pk_tr", "pt_ready", "g_exp", "g_shift"))
        og_ready, oh_ready, quad_done, quad_out, n2_kept, n2_in = (sem(n) for n in ("og_ready", "oh_ready", "quad_done", "quad_out", "n2_kept", "n2_in"))
        gs_out = [sem(f"gs_out{i}") for i in range(2)]
        gate_gain = sem("gate_gain")
        u_in, v_in, g_in = ([sem(f"{n}_in{i}") for i in range(2)] for n in "uvg")
        uh, ul, vh, vl, s1, gelu, prod, ah, al, s2, acc_add = (
            sem("p_" + n) for n in ("uh", "ul", "vh", "vl", "s1", "gelu", "prod", "ah", "al", "s2", "acc"))
        acc_in, y_ss, y_root, y_ready, y_out = (sem(n) for n in ("acc_in", "y_ss", "y_root", "y_ready", "y_out"))
        act_own, dve_own, pool_own = sem("act_own"), sem("dve_own"), sem("pool_own")

        def stage_end(eng, n):
            eng.drain().then_inc(stage_done, 1)
            eng.wait_ge(stage_done, 5 * n)

        def taker(G):
            return "act" if G // 8 in (1, 3) or G % 2 == 0 else "dve"

        def taken(G):
            return taker(G), sum(taker(g) == taker(G) for g in range(G + 1))

        def proj_dst(G):
            s, g = divmod(G, 8)
            dst = (Q, F, INP, GATE, DQ, DK, DV)[s]
            if s in (2, 3, 6):
                return dst[:, g, :]
            return dst[:, g // 2, (g % 2) * 512:(g % 2) * 512 + 512]

        att = [(h, b) for h in range(HEADS) for b in range(TT)]

        SEGMENTS = 8
        BEFORE = 5

        TURN_AT = [16 + 8, 16 + 14]
        BETWEEN = [("route", 2), ("gates", 0), ("route", 3), ("gates", 1), ("route", 4), ("gates", 2), ("gates", 3)]

        def quads_before(t):
            return 32 * max(0, t - 2 if t < BEFORE else t)

        def turned_before(t):
            return min(t + 3, BEFORE) if t < 4 else t + 1

        def turns_in(seg):
            return 4 if seg < SEGMENTS - 1 else 3

        block = ctx.enter_context(nc.Block())

        @block.sync
        def _(sp):
            for dst, src in ((consts[:, :], cst), (masks[:, :, :], level_masks), (mix_w[:, :], norm_mix),
                             (lb_in[:, :, :], lb)):
                sp.dma_start(dst, src).then_inc(consts_in, 16)
            for k in range(KD):
                sp.dma_start(X[:, k, :], x_t[:, k, :]).then_inc(x_in[k], 16)
            for dst, src in ((hg_gain[:, :], hg_norm), (da_gain[:, :], da_norm), (lam_in[:, :, :], lam)):
                sp.dma_start(dst, src).then_inc(consts_in, 16)
            for s in range(SECTIONS):
                if s == 2:
                    stage_end(sp, 1)
                if s >= 2:
                    sp.wait_ge(proj_done, 8 * (s - 1))
                sp.dma_start(W[s % 2][:, :, :], w_in[:, :, s * 512:(s + 1) * 512]).then_inc(w_in_sem[s % 2], 16)
            for n in (2, 3):
                stage_end(sp, n)
            sp.dma_start(WO[:, :, :], w_out).then_inc(wo_in, 16)
            for n in (4, 5):
                stage_end(sp, n)
            sp.dma_start(XN[0][:, :], x_n[0]).then_inc(xn_in[0], 16)
            sp.dma_start(ffn_w[:, :], norm_ffn).then_inc(wo_in, 16)
            for t in range(TT):
                if t + 1 < TT:
                    if t >= 1:
                        sp.wait_ge(h_ready, t)
                    sp.dma_start(XN[(t + 1) % 2][:, :], x_n[t + 1]).then_inc(xn_in[(t + 1) % 2], 16)
                sp.wait_ge(h_ready, t + 1)
                sp.dma_start(h_dram[t], H[t % 2][:, :]).then_inc(h_out[t % 2], 16)
            sp.wait_ge(h_out[0], 16 * TT // 2)
            sp.wait_ge(h_out[1], 16 * TT // 2)
            stage_end(sp, 6)
            if stop == 6:
                sp.dma_start(out, h_dram).then_inc(y_out, 16)
                sp.wait_ge(y_out, 16)
                return
            sp.dma_start(SUB[:, :, :], sub_t).then_inc(consts_in, 16)
            s_units = s_dram.rearrange("a h p n -> (a h) p n")

            def load_unit(u, slot):
                src = s_units[bass.ds(u, 1), :, :].rearrange("o p (a n) -> p (o a) n", a=2)
                sp.dma_start(SU[slot][:, :, :], src).then_inc(su_in[slot], 16)

            for t in range(BEFORE):
                if t in (0, 4):
                    for q in ss_out:
                        sp.wait_ge(q, 16 * 8 * (t // 4 + 1))
                with sp.Fori(0, PEER_HEADS // 2) as i:
                    for j in range(2):
                        sp.wait_ge(su_used, i * 2 + (8 * t + j + 1))
                        load_unit(i * 2 + (8 * t + j), j)
            stage_end(sp, 7)
            for half in range(2):
                c0 = half * KEYS

                def load_u(c, j):
                    sp.wait_ge(ul, c0 + c + 1)
                    sp.dma_start(UR[j % 2][:, :, :], u_t[bass.ds(c, 1)].rearrange("o p k n -> p (o k) n")
                                 ).then_inc(u_in[j % 2], 16)

                def load_vg(c, j):
                    sp.wait_ge(prod, c0 + c + 1)
                    sp.dma_start(GT[j % 2][:, :], gates_dram[bass.ds(c, 1), :, half * HALF_T:(half + 1) * HALF_T]
                                 .rearrange("o p t -> p (o t)")).then_inc(g_in[j % 2], 16)
                    sp.wait_ge(stage_done, 5 * 7)
                    sp.wait_ge(vl, c0 + c + 1)
                    sp.dma_start(VR[j % 2][:, :], v[bass.ds(c, 1)].rearrange("o p d -> p (o d)")).then_inc(v_in[j % 2], 16)

                def step(c):
                    for j in range(4):
                        load_vg(c + j, j)
                        load_u(c + (2 + j), j)

                if half:
                    sp.wait_ge(s1, KEYS + 2)
                    sp.dma_start(N2H[0][:, :, :].bitcast(F32), n2_dram[0]).then_inc(n2_in, 16)
                    sp.dma_start(N2L[0][:, :, :].bitcast(F32), n2_dram[1]).then_inc(n2_in, 16)
                    sp.wait_ge(y_out, 16 * 4)
                sp.dma_start(ACC[:, :, :], h_dram[half * 4:half * 4 + 4].rearrange("a p d -> p a d")).then_inc(acc_in, 16)
                sp.wait_ge(gs_out[0], 16 * (4 if half == 0 else 12))
                sp.wait_ge(gs_out[1], 16 * 4)
                load_u(0, 0)
                load_u(1, 1)
                for j in range(2):
                    load_vg(j, j)
                    load_u(j + 2, j)
                if half == 0:
                    for seg in range(SEGMENTS):
                        with sp.Fori(0, turns_in(seg)) as i:
                            if seg < 6:
                                u = 8 * BEFORE + 4 * seg
                                sp.wait_ge(su_used, i + (u + 2))
                                load_unit(i + u, 0)
                            step(i * 4 + (16 * seg + 2))
                else:
                    with sp.Fori(0, KEYS // 4 - 1) as i:
                        step(i * 4 + 2)
                for j in range(2):
                    load_vg(KEYS - 2 + j, j)
                if half == 0:
                    sp.wait_ge(pk_ready, TT)
                    sp.dma_start(fin_w[:, :], norm_fin).then_inc(consts_in, 16)
                for t in range(4):
                    sp.wait_ge(y_ready, half * 4 + t + 1)
                    sp.dma_start(out[half * 4 + t], ACC[:, t, :]).then_inc(y_out, 16)
            sp.wait_ge(y_out, 16 * TT)

        @block.tensor
        def _(pe):
            pe.sem_inc(hg_pe, 2)
            pe.sem_inc(s1, 2)
            pe.sem_inc(s2, 16)
            pe.sem_inc(quad_done, 2)
            pe.sem_inc(pk_tr, 1)
            pe.wait_ge(consts_in, 16 * 7)
            for k in range(KD):
                pe.wait_ge(sq_ready, k + 1)
                for th in range(2):
                    mm = pe.matmul(bank(th), ones, sq[k % 2][:, th * 512:(th + 1) * 512], start=k == 0, stop=k == KD - 1)
                mm.then_inc(sq_used, 1)
            stage_end(pe, 1)
            for G in range(8 * SECTIONS):
                s, g = divmod(G, 8)
                if g == 0:
                    pe.wait_ge(w_in_sem[s % 2], 16 * (s // 2 + 1))
                if G >= 4:
                    who, n = taken(G - 4)
                    pe.wait_ge(proj_out[who], n)
                for k in range(KD):
                    if s in (2, 3, 6):
                        l, r = X[:, k, g * P:(g + 1) * P], W[s % 2][:, k, :]
                    else:
                        l, r = W[s % 2][:, k, (g // 2) * P:(g // 2 + 1) * P], X[:, k, (g % 2) * 512:(g % 2 + 1) * 512]
                    mm = pe.matmul(bank(G % 4), l, r, start=k == 0, stop=k == KD - 1)
                mm.then_inc(proj_done, 1)
            stage_end(pe, 2)
            with pe.Fori(0, TT) as n:
                def scores(h):
                    p = h % 2
                    pe.wait_ge(hg_q, n * 4 + h + 3)
                    pe.wait_ge(hg_k, n * 4 + h + 3)
                    pe.wait_ge(hg_mask, n * 4 + h + 1)
                    for l in range(8):
                        pe.matmul(bank_tiles(2 * p, 2)[:, l, :], KL[p][:, l if l < 7 else 8, :],
                                  QL[p][:, l + 1, :], start=True, stop=True)
                    pe.wait_ge(hg_state, n * 4 + h + 1)
                    pe.transpose(PS[:, 6 + p, 0:128], KL[p][:, 7, :], ident).then_inc(hg_scores, 1)

                def outputs(h):
                    p = h % 2
                    vals = INP[:, bass.ds(n, 1), h * 128:(h + 1) * 128].rearrange("p o e -> p (o e)")
                    pe.wait_ge(hg_mask, n * 4 + h + 3)
                    pe.wait_ge(hg_out, n * 4 + h + 1)
                    for l in range(8):
                        pe.matmul(PS[:, 4 + p, 0:128], M[p][:, l, :], vals, start=l == 0, stop=False)
                    pe.matmul(PS[:, 4 + p, 0:128], QL[p][:, 0, :], STATE[:, h, :], start=False, stop=True)
                    pe.wait_ge(hg_kn, n * 4 + h + 1)
                    pe.matmul(PS[:, 6 + p, 0:128], KN[p][:, :], vals, start=True, stop=True).then_inc(hg_pe, 1)

                scores(0)
                scores(1)
                outputs(0)
                scores(2)
                outputs(1)
                scores(3)
                outputs(2)
                outputs(3)
            stage_end(pe, 3)
            def att_scores(u):
                h, b = att[u]
                if u >= 1:
                    pe.wait_ge(at_exp, 2 * u)
                for c in range(2):
                    for n0 in range(0, (b + 1) * P, 512):
                        n1 = min((b + 1) * P, n0 + 512)
                        mm = pe.matmul(PS[:, 2 * c + n0 // 512, 0:n1 - n0],
                                       DQ[64 * c:64 * c + 64, h, b * P:(b + 1) * P],
                                       DK[64 * c:64 * c + 64, h, n0:n1], start=True, stop=True)
                    mm.then_inc(at_s, 1)

            def att_turn(u):
                h, b = att[u]
                pe.wait_ge(at_comb, u + 1)
                if u >= 1:
                    pe.wait_ge(at_t, u)
                for j in range(b + 1):
                    mm = pe.transpose(PS[:, 4 + j // 4, (j % 4) * P:(j % 4 + 1) * P],
                                      PR[u % 2][0][:, j * P:(j + 1) * P], ident)
                mm.then_inc(at_tr, 1)

            def att_out(u):
                h, b = att[u]
                pe.wait_ge(at_t, u + 1)
                if u >= 2:
                    pe.wait_ge(at_oe, u - 1)
                for j in range(b + 1):
                    mm = pe.matmul(PS[:, 6 + u % 2, 0:128], AT[u % 2][:, j, :], DV[:, j, h * 128:(h + 1) * 128],
                                   start=j == 0, stop=j == b)
                mm.then_inc(at_o, 1)

            for u in range(len(att) + 2):
                if u < len(att):
                    att_scores(u)
                if u >= 2:
                    att_out(u - 2)
                if 1 <= u <= len(att):
                    att_turn(u - 1)
            stage_end(pe, 4)
            stage_end(pe, 5)
            def turn_mixed(t):
                if t >= 1:
                    pe.wait_ge(mt_act, t)
                    pe.wait_ge(mt_dve, t)
                for k in range(KD):
                    src = INP if k < 4 else DA
                    mm = pe.transpose(PS[:, k // 4, (k % 4) * P:(k % 4 + 1) * P], src[:, t, (k % 4) * P:(k % 4 + 1) * P], ident)
                mm.then_inc(mt_tr, 1)

            def project_out(t):
                pe.wait_ge(mt_act, t + 1)
                pe.wait_ge(mt_dve, t + 1)
                if t >= 1:
                    pe.wait_ge(h_ready, t)
                for dh in range(2):
                    for k in range(KD):
                        mm = pe.matmul(bank(2 + dh), MT[:, k, t * P:(t + 1) * P], WO[:, k, dh * 512:(dh + 1) * 512],
                                       start=k == 0, stop=k == KD - 1)
                mm.then_inc(wo_done, 1)

            def turn_n2(t):
                pe.wait_ge(n2_ready, t + 1)
                if t >= 2:
                    pe.wait_ge(n2_lo, t - 1)
                for k in range(KD):
                    mm = pe.transpose(PS[:, 4 + 2 * (t % 2) + k // 4, (k % 4) * P:(k % 4 + 1) * P],
                                      N2[t % 2][:, k * P:(k + 1) * P], ident)
                mm.then_inc(n2_tr, 1)

            pe.wait_ge(wo_in, 32)
            turn_mixed(0)
            for t in range(TT + 1):
                if t + 1 < TT:
                    turn_mixed(t + 1)
                if t < TT:
                    project_out(t)
                if t >= 1:
                    turn_n2(t - 1)
            stage_end(pe, 6)
            if stop == 6:
                return
            pe.wait_ge(consts_in, 16 * 8)

            def queries(M):
                half, m = divmod(M, 16)
                pe.wait_ge(wq_lo, M + 1)
                if M >= 2:
                    pe.wait_ge(qh_out, M - 1)
                for k in range(KD):
                    for j, (a, b) in enumerate(((WQH, N2H), (WQH, N2L), (WQL, N2H))):
                        mm = pe.matmul(bank(M % 2), a[M % 2][:, k, :], b[half][:, k, :], start=k == 0 and j == 0,
                                       stop=k == KD - 1 and j == 2)
                mm.then_inc(qh_done, 1)

            def key_scores(M):
                pe.wait_ge(qh_out, M + 1)
                if M >= 2:
                    pe.wait_ge(sc_out, M - 1)
                for t in range(TT // 2):
                    mm = pe.matmul(PS[:, 2 + M % 2, t * P:(t + 1) * P], QH[M % 2][:, t * P:(t + 1) * P],
                                   SUB[:, M % 16, :], start=True, stop=True)
                mm.then_inc(sc_done, 1)

            def turn_picks(t):
                pe.wait_ge(pk_ready, t + 1)
                pe.wait_ge(quad_out, quads_before(t) + 2)
                if t >= 1:
                    pe.wait_ge(pt_ready, t)
                for j in range(3):
                    mm = pe.transpose(PS[:, 7, j * P:(j + 1) * P], PK[:, j, :], ident)
                mm.then_inc(pk_tr, 1)

            def quad(B, qd, t):
                p = qd % 2
                pe.wait_ge(og_ready, B * 4 + (qd + 1))
                if p:
                    pe.wait_ge(oh_ready, B * 2 + (qd // 2 + 2))
                    pe.wait_ge(pt_ready, turned_before(t))
                pe.wait_ge(quad_out, B * 4 + (qd + 1))
                for j in range(4):
                    mm = pe.matmul(PS[:, 6 + p, j * P:(j + 1) * P], OH[p][:, j, :], OG[p][:, j, :], start=True, stop=True)
                mm.then_inc(quad_done, 1)

            for n in range(33):
                if n < 32:
                    queries(n)
                if n >= 1:
                    key_scores(n - 1)
                if n in TURN_AT:
                    turn_picks(TURN_AT.index(n))
            for what, t in BETWEEN:
                if what == "route":
                    turn_picks(t)
                else:
                    with pe.Fori(0, 8) as i:
                        for qd in range(4):
                            quad(i + 8 * t, qd, t)
            stage_end(pe, 7)
            for half in range(2):
                c0 = half * KEYS

                def first(c, j):
                    pe.wait_ge(ul, c0 + c + 3)
                    pe.wait_ge(gelu, c0 + c + 1)
                    for k in range(KD):
                        for q, (a, b) in enumerate(((UH, N2H), (UH, N2L), (UL, N2H))):
                            mm = pe.matmul(bank(j % 2), a[j % 2][:, k, :], b[0][:, k, :], start=k == 0 and q == 0,
                                           stop=k == KD - 1 and q == 2)
                    mm.then_inc(s1, 1)

                def second(g, j, quads=None):
                    pe.wait_ge(al, c0 + g * 2 + 4)
                    pe.wait_ge(vl, c0 + g * 2 + 4)
                    for t in range(8):
                        tt, dh = divmod(t, 2)
                        pe.wait_ge(acc_add, (c0 // 2) * 8 + g * 8 + t + 1)
                        for c in (2 * j, 2 * j + 1):
                            for q, (a, b) in enumerate(((AH, VH), (AH, VL), (AL, VH))):
                                mm = pe.matmul(bank(2 + t % 4), a[c][:, tt * P:(tt + 1) * P], b[c][:, dh * 512:(dh + 1) * 512],
                                               start=c == 2 * j and q == 0, stop=c == 2 * j + 1 and q == 2)
                        mm.then_inc(s2, 1)
                        if quads and t % 2:
                            quad(quads[0], t // 2, quads[1])

                def step(c, g, quads=None):
                    for j in range(2):
                        first(c + 2 * j, 0)
                        first(c + (2 * j + 1), 1)
                        second(g + j, j, quads if j else None)

                if half:
                    pe.wait_ge(n2_in, 32)
                first(0, 0)
                first(1, 1)
                if half == 0:
                    for seg in range(SEGMENTS):
                        t = 4 + seg // 2
                        with pe.Fori(0, turns_in(seg)) as i:
                            step(i * 4 + (16 * seg + 2), i * 2 + 8 * seg, (i + (32 + 4 * seg), t))
                        if seg in (1, 3, 5):
                            turn_picks(t + 1)
                else:
                    with pe.Fori(0, KEYS // 4 - 1) as i:
                        step(i * 4 + 2, i * 2)
                first(KEYS - 2, 0)
                first(KEYS - 1, 1)
                second(KEYS // 2 - 2, 0)
                second(KEYS // 2 - 1, 1, (63, 7) if half == 0 else None)

        @block.scalar
        def _(act):
            link = Links(act, act_own)
            act.sem_inc(hg_out, 2)
            act.sem_inc(gelu, 2)
            act.sem_inc(quad_out, 2)
            act.sem_inc(oh_ready, 1)
            for k in range(KD):
                act.wait_ge(x_in[k], 16)
                if k >= 2:
                    act.wait_ge(sq_used, k - 1)
                act.activation(sq[k % 2][:, :], X[:, k, :], ACT.Square).then_inc(sq_ready, 1)
            act.wait_ge(sq_used, KD)
            act.wait_ge(ready, 1)
            act.activation(rstd[:, :].rearrange("p (a b) -> p a b", a=2), bank(0, 2), ACT.Sqrt, bias=eps,
                           scale=1.0 / D).then_inc(root_ready, 1)
            act.wait_ge(ready, 2)
            link(act.activation(lb_t, lb_t, ACT.Exp))
            act.activation(lam_t, lam_t, ACT.Exp).then_inc(root_ready, 1)
            stage_end(act, 1)
            for G in range(8 * SECTIONS):
                if taker(G) != "act":
                    continue
                act.wait_ge(proj_done, G + 1)
                func = {1: ACT.Sigmoid, 3: ACT.Silu}.get(G // 8, ACT.Copy)
                act.activation(proj_dst(G), bank(G % 4), func, scale=P ** -0.5 if G // 8 == 0 else 1.0
                               ).then_inc(proj_out["act"], 1)
            stage_end(act, 2)
            for h in range(HEADS):
                act.wait_ge(log_f, h + 1)
                act.activation(F[:, h, :], F[:, h, :], ACT.Ln).then_inc(ready, 1)
            with act.Fori(0, TT) as n:
                def decay(h):
                    act.wait_ge(hg_diff, n * 4 + h + 1)
                    act.activation(E[h % 2][:, :, :], E[h % 2][:, :, :], ACT.Exp).then_inc(hg_exp, 1)

                def turned(h):
                    act.wait_ge(hg_scores, n * 4 + h + 1)
                    act.wait_ge(hg_pe, n * 4 + h + 1)
                    act.copy(KN[h % 2][:, :], PS[:, 6 + h % 2, 0:128]).then_inc(hg_kn, 1)

                def result(h):
                    act.wait_ge(hg_pe, n * 4 + h + 3)
                    act.copy(INP[:, bass.ds(n, 1), h * 128:(h + 1) * 128].rearrange("p o e -> p (o e)"),
                             PS[:, 4 + h % 2, 0:128]).then_inc(hg_out, 1)

                decay(0)
                decay(1)
                turned(0)
                decay(2)
                turned(1)
                result(0)
                decay(3)
                turned(2)
                result(1)
                turned(3)
                result(2)
                result(3)
            stage_end(act, 3)
            def att_exp(u):
                h, b = att[u]
                nk = (b + 1) * P
                for c in range(2):
                    act.wait_ge(at_max, 2 * u + c + 1)
                    if u >= 2 and c == 0:
                        act.wait_ge(at_tr, u - 1)
                    act.activation(PR[u % 2][c][:, 0:nk], PS[:, 2 * c:2 * c + 2, :].rearrange("p a b -> p (a b)")[:, 0:nk],
                                   ACT.Exp, bias=nmx[:, u % 2, c:c + 1], scale=0.125,
                                   accum_out=l_sum[:, u % 2, c:c + 1]).then_inc(at_exp, 1)

            for u in range(len(att) + 2):
                if u < len(att):
                    att_exp(u)
                if 1 <= u <= len(att):
                    h, b = att[u - 1]
                    act.wait_ge(at_tr, u)
                    if u >= 3:
                        act.wait_ge(at_o, u - 2)
                    act.copy(AT[(u - 1) % 2][:, 0:b + 1, :], bank_tiles(4, 2)[:, 0:b + 1, :]).then_inc(at_t, 1)
                if u >= 2:
                    h, b = att[u - 2]
                    act.wait_ge(at_o, u - 1)
                    act.copy(DA[:, b, h * 128:(h + 1) * 128], PS[:, 6 + u % 2, 0:128]).then_inc(at_oe, 1)
            stage_end(act, 4)
            for i in range(2 * TT):
                t, da = i % TT, i // TT
                if i >= 2:
                    act.wait_ge(nrm_ss, i - 1)
                act.activation(SQN[i % 2][:, :], (DA if da else INP)[:, t, :], ACT.Square).then_inc(nrm_sq, 1)
                if i % TT == TT - 1:
                    act.wait_ge(nrm_ss, i + 1)
                    act.activation(norm_r[:, :], norm_ss[:, :], ACT.Sqrt, bias=eps, scale=1.0 / P).then_inc(nrm_root, 1)
                    act.wait_ge(nrm_r, da + 1)
            stage_end(act, 5)
            for t in range(TT + 1):
                if t < TT:
                    act.wait_ge(mt_tr, t + 1)
                    act.copy(MT[:, 0:4, t * P:(t + 1) * P], bank_tiles(0)).then_inc(mt_act, 1)
                if t >= 1:
                    act.wait_ge(n2_tr, t)
                    b = 4 + 2 * ((t - 1) % 2)
                    act.copy(N2H[(t - 1) // 4][:, :, (t - 1) % 4 * P:((t - 1) % 4 + 1) * P], bank_tiles(b, 2)).then_inc(n2_hi, 1)
                if t < TT:
                    act.wait_ge(h_ready, t + 1)
                    link(act.activation(junk[:, :], H[t % 2][:, :], ACT.Square, accum_out=norm_ss[:, t:t + 1]))
                    act.activation(norm_ss[:, t:t + 1], norm_ss[:, t:t + 1], ACT.Sqrt, bias=eps, scale=1.0 / D).then_inc(h_ss, 1)
            stage_end(act, 6)
            if stop == 6:
                return
            act.dma_start(WQ[0][:, :, :], w_q[:, :, 0:512]).then_inc(wq_in[0], 16)
            act.dma_start(WQ[1][:, :, :], w_q[:, :, 512:1024]).then_inc(wq_in[1], 16)

            def wq_split(M):
                if M % 4 == 0:
                    act.wait_ge(wq_in[(M // 4) % 2], 16 * (M // 8 + 1))
                if M >= 2:
                    act.wait_ge(qh_done, M - 1)
                act.copy(WQH[M % 2][:, :, :], WQ[(M // 4) % 2][:, :, (M % 4) * P:(M % 4 + 1) * P]).then_inc(wq_hi, 1)

            def gate_exp(t):
                act.wait_ge(g_shift, t + 1)
                act.activation(CS[:, :], CS[:, :], ACT.Exp).then_inc(g_exp, 1)
                act.wait_ge(pk_tr, t + 2)
                act.copy(PT[t % 3][:, :, :], bank_tiles(7)[:, 0:3, :]).then_inc(pt_ready, 1)

            def abs_quad(B, qd, t, x, links):
                act.wait_ge(quad_done, B * 4 + (qd + 1))
                act.wait_ge(oh_ready, B * 2 + (qd // 2 + 1))
                act.wait_ge(pt_ready, t + 1)
                for j in range(4):
                    ins = act.activation(ABS[:, j, :], iota, ACT.Abs, bias=PT[t % 3][:, 1, bass.ds(x + (4 * qd + j), 1)],
                                         scale=-1.0)
                links(ins)
                act.activation(OH[1][:, :, :], ABS[:, :, :], ACT.Relu, bias=ones[:, 0:1], scale=-1.0).then_inc(oh_ready, 1)

            def take_quad(B, qd, x, buf):
                act.wait_ge(quad_done, B * 4 + (qd + 3))
                act.copy(GS[buf][:, :, bass.ds(x + 4 * qd, 4)].rearrange("p a t -> p t a"),
                         bank_tiles(6 + qd % 2)).then_inc(quad_out, 1)

            def store_gates(b, buf):
                act.wait_ge(quad_out, 16 * (b + 1) + 2)
                act.dma_start(gates_dram[:, :, b * 64:(b + 1) * 64].rearrange("a p t -> p a t"),
                              GS[buf][:, :, :]).then_inc(gs_out[buf], 16)

            wq_split(0)
            wq_split(1)
            for M in range(33):
                if M < 32:
                    if M in TURN_AT:
                        gate_exp(TURN_AT.index(M))
                    act.wait_ge(qh_done, M + 1)
                    if M >= 2:
                        act.wait_ge(sc_done, M - 1)
                    act.copy(QH[M % 2][:, :], bank(M % 2)).then_inc(qh_out, 1)
                    if M + 2 < 32:
                        wq_split(M + 2)
                if M == 31:
                    act.dma_start(n2_dram[0], N2H[1][:, :, :].bitcast(F32)).then_inc(n2_kept, 16)
                    act.dma_start(n2_dram[1], N2L[1][:, :, :].bitcast(F32)).then_inc(n2_kept, 16)
                if M >= 1:
                    S = M - 1
                    half, m = divmod(S, 16)
                    act.wait_ge(sc_done, S + 1)
                    if S >= 2:
                        act.wait_ge(ss_out[S % 2], 16 * (S // 2))
                    act.copy(SS[S % 2][:, :, :], bank_tiles(2 + S % 2)).then_inc(sc_out, 1)
                    act.wait_ge(sc_out, S + 1)
                    dst = s_dram[4 * half:4 * half + 4, m // 2, :, (m % 2) * 128:(m % 2) * 128 + 128].rearrange("a p n -> p a n")
                    act.dma_start(dst, SS[S % 2][:, :, :]).then_inc(ss_out[S % 2], 16)
                if M % 4 == 2 and M < 24:
                    S = M // 4 + 2
                    act.wait_ge(wq_lo, 4 * (S - 1))
                    act.dma_start(WQ[S % 2][:, :, :], w_q[:, :, (S % 4) * 512:(S % 4 + 1) * 512]).then_inc(wq_in[S % 2], 16)
            act.wait_ge(n2_kept, 32)
            for q in ss_out:
                act.wait_ge(q, 16 * 16)
            for what, t in BETWEEN:
                if what == "route":
                    gate_exp(t)
                    continue
                for b in range(2):
                    if t >= 1:
                        act.wait_ge(gs_out[b], 16 * t)
                    with act.Fori(0, 4) as i:
                        B, x = i + (8 * t + 4 * b), i * 16
                        link.loop(i, 2)
                        abs_quad(B, 1, t, x + 64 * b, link)
                        take_quad(B, 0, x, b)
                        abs_quad(B, 3, t, x + 64 * b, link)
                        for qd in (1, 2, 3):
                            take_quad(B, qd, x, b)
                        link.end(4)
                    store_gates(2 * t + b, b)
            stage_end(act, 7)
            act.preload_act_table(ACT.Gelu_apprx_tanh)
            for half in range(2):
                c0 = half * KEYS

                def u_hi(c, j):
                    act.wait_ge(s1, c0 + c + 1)
                    act.wait_ge(u_in[j % 2], turns(c, j))
                    act.copy(UH[j % 2][:, :, :], UR[j % 2][:, :, :]).then_inc(uh, 1)

                def v_hi(c, j):
                    act.wait_ge(s2, buffers_free(c, j))
                    act.wait_ge(v_in[j % 2], turns(c, j))
                    act.copy(VH[j % 4][:, :], VR[j % 2][:, :]).then_inc(vh, 1)

                def turns(c, j):
                    return (c - j % 2 + c0) * 8 + 16

                def buffers_free(c, j):
                    return (c - j % 2 + c0) * 4 + 8

                def act_gelu(c, j):
                    act.wait_ge(al, c0 + c + 1)
                    act.wait_ge(s1, c0 + c + 3)
                    act.activation(AF[j % 2][:, :], bank(j % 2), ACT.Gelu_apprx_tanh).then_inc(gelu, 1)

                def a_hi(c, j):
                    act.wait_ge(s2, buffers_free(c, j))
                    act.wait_ge(prod, c0 + c + 3)
                    act.copy(AH[j % 4][:, :], AF[j % 2][:, :]).then_inc(ah, 1)

                def period(c, j, more_u=True, quads=None):
                    act_gelu(c, j)
                    if more_u:
                        u_hi(c + 2, j)
                    a_hi(c, j)
                    if quads:
                        B, t, x, y = quads
                        abs_quad(B, 1, t, x, link)
                    act_gelu(c + 1, j + 1)
                    a_hi(c + 1, j + 1)
                    if more_u:
                        u_hi(c + 3, j + 1)
                    v_hi(c, j)
                    v_hi(c + 1, j + 1)
                    if quads:
                        take_quad(B, 0, y, 0)
                        take_quad(B, 1, y, 0)
                        abs_quad(B, 3, t, x, link)
                        take_quad(B, 2, y, 0)
                        take_quad(B, 3, y, 0)

                u_hi(0, 0)
                u_hi(1, 1)
                period(0, 0)
                if half == 0:
                    for seg in range(SEGMENTS):
                        t = 4 + seg // 2
                        if seg >= 1:
                            act.wait_ge(gs_out[0], 16 * (4 + seg))
                        with act.Fori(0, turns_in(seg)) as i:
                            link.loop(i, 2)
                            period(i * 4 + (16 * seg + 2), 2)
                            period(i * 4 + (16 * seg + 4), 0,
                                   quads=(i + (32 + 4 * seg), t, i * 16 + (seg % 2) * 64, i * 16))
                            link.end(turns_in(seg))
                        if seg < SEGMENTS - 1:
                            store_gates(8 + seg, 0)
                        if seg in (1, 3, 5):
                            gate_exp(t + 1)
                    period(KEYS - 2, 2, more_u=False)
                    for q in range(2):
                        abs_quad(63, 2 * q + 1, 7, 112, link)
                        take_quad(63, 2 * q, 48, 0)
                        take_quad(63, 2 * q + 1, 48, 0)
                    store_gates(15, 0)
                else:
                    with act.Fori(0, KEYS // 4 - 1) as i:
                        period(i * 4 + 2, 2)
                        period(i * 4 + 4, 0)
                    period(KEYS - 2, 2, more_u=False)
                act.wait_ge(acc_add, (half + 1) * KEYS * 4 + 4)
                act.wait_ge(acc_in, 16 * (half + 1))
                act.wait_ge(pk_ready, TT)
                for t in range(4):
                    link(act.activation(FSQ[:, :], ACC[:, t, :], ACT.Square, accum_out=norm_ss[:, t:t + 1]))
                act.activation(norm_ss[:, 0:4], norm_ss[:, 0:4], ACT.Sqrt, bias=eps, scale=1.0 / D).then_inc(y_root, 1)

        @block.vector
        def _(dve):
            link = Links(dve, dve_own)
            dve.sem_inc(hg_mask, 2)
            dve.sem_inc(hg_q, 2)
            dve.sem_inc(hg_state, 2)
            dve.sem_inc(su_used, 2)
            dve.sem_inc(ul, 2)
            dve.sem_inc(prod, 2)
            dve.sem_inc(al, 2)
            dve.sem_inc(acc_add, 4)
            link(dve.memset(zeros[:, :], 0.0))
            dve.memset(eps, EPS).then_inc(ready, 1)
            dve.wait_ge(consts_in, 16 * 7)
            link(dve.tensor_tensor(lb_t[:, 0:4], lb_in[:, 0, :], lb_in[:, 1, :], ALU.max))
            link(dve.tensor_tensor(lb_t[:, 4:8], lb_in[:, 1, :], lb_t[:, 0:4], ALU.subtract))
            link(dve.tensor_tensor(lb_t[:, 0:4], lb_in[:, 0, :], lb_t[:, 0:4], ALU.subtract))
            for r in range(2):
                link(dve.tensor_tensor(lam_in[:, 2 * r, :], lam_in[:, 2 * r, :], lam_in[:, 2 * r + 1, :], ALU.mult))
                ins = dve.reduce_sum(lam_t[:, r:r + 1], lam_in[:, 2 * r, :], AX_X)
                if r == 0:
                    link(ins)
                else:
                    ins.then_inc(ready, 1)
            dve.wait_ge(root_ready, 1)
            link(dve.reciprocal(rstd[:, :], rstd[:, :]))
            for k in range(KD):
                link(dve.scalar_tensor_tensor(out=X[:, k, :], in0=X[:, k, :], scalar=mix_w[:, k:k + 1], in1=rstd[:, :],
                                              op0=ALU.mult, op1=ALU.mult))
            dve.wait_ge(root_ready, 2)
            link(dve.tensor_tensor(one_lb, lb_t[:, 0:4], lb_t[:, 4:8], ALU.add))
            link(dve.reciprocal(one_lb, one_lb))
            link(dve.tensor_tensor(lbs, lb_t[:, 0:4], one_lb, ALU.mult))
            link(dve.tensor_scalar(one_lb, lbs, -1.0, 1.0, ALU.mult, ALU.add))
            link(dve.tensor_tensor(lams, lam_t[:, 0:1], lam_t[:, 1:2], ALU.subtract))
            link(dve.tensor_scalar(lams, lams, LAMBDA_INIT, None, ALU.add))
            stage_end(dve, 1)
            for G in range(8 * SECTIONS):
                if taker(G) != "dve":
                    continue
                dve.wait_ge(proj_done, G + 1)
                dve.tensor_scalar(proj_dst(G), bank(G % 4), P ** -0.5 if G // 8 == 0 else 1.0, None, ALU.mult
                                  ).then_inc(proj_out["dve"], 1)
            stage_end(dve, 2)
            for h in range(HEADS):
                link(dve.tensor_scalar(F[:, h, :], F[:, h, :], one_lb[:, h:h + 1], lbs[:, h:h + 1], ALU.mult, ALU.add))
                dve.tensor_scalar(K[:, h, :], F[:, h, :], -1.0, 1.0, ALU.mult, ALU.add).then_inc(log_f, 1)
            link(dve.memset(STATE[:, :, :], 0.0))
            dve.wait_ge(ready, 2 + HEADS)
            with dve.Fori(0, TT) as n:
                link.loop(n, 3 * HEADS)

                def differences(h):
                    d = E[h % 2]
                    dve.wait_ge(hg_q, n * 4 + h + 1)
                    dve.wait_ge(hg_k, n * 4 + h + 1)
                    b = d[:, 0, :]
                    link(dve.tensor_tensor_scan(b, F[:, h, bass.ds(n * P, P)], zeros[:, :], 0.0, ALU.add, ALU.add))
                    for l in range(LEVELS):
                        m = 64 >> l
                        view = b.rearrange("p (a m) -> p a m", m=2 * m)
                        dve.tensor_tensor(d[:, 1 + l, :].rearrange("p (a m) -> p a m", m=2 * m), view,
                                          view[:, :, m - 1:m].broadcast_to([P, P // (2 * m), 2 * m]), ALU.subtract)
                    link(dve.tensor_scalar(d[:, 8, :], b, b[:, P - 1:P], None, ALU.subtract))
                    dve.scalar_tensor_tensor(out=d[:, :, :], in0=d[:, :, :], scalar=-1.0, in1=d[:, :, :],
                                             op0=ALU.mult, op1=ALU.min).then_inc(hg_diff, 1)

                def queries(h):
                    p = h % 2
                    q = Q[:, h, bass.ds(n * P, P)]
                    dve.wait_ge(hg_pe, n * 4 + h + 1)
                    dve.wait_ge(hg_exp, n * 4 + h + 1)
                    dve.wait_ge(hg_state, n * 4 + h + 1)
                    dve.tensor_copy(QL[p][:, 8, :], q)
                    link(dve.tensor_copy(BL[p][:, :], E[p][:, 0, P - 1:P]))
                    dve.tensor_tensor(QL[p][:, 0:8, :], E[p][:, 0:8, :], spread(q, 1, 8), ALU.mult).then_inc(hg_q, 1)

                def mask(h):
                    p = h % 2
                    dve.wait_ge(hg_scores, n * 4 + h + 1)
                    dve.wait_ge(hg_pe, n * 4 + h + 1)
                    dve.tensor_tensor(M[p][:, :, :], bank_tiles(2 * p, 2), masks[:, :, :], ALU.mult).then_inc(hg_mask, 1)

                def state(h):
                    dve.wait_ge(hg_pe, n * 4 + h + 3)
                    dve.scalar_tensor_tensor(out=STATE[:, h, :], in0=STATE[:, h, :], scalar=BL[h % 2][:, :],
                                             in1=PS[:, 6 + h % 2, 0:128], op0=ALU.mult, op1=ALU.add).then_inc(hg_state, 1)

                differences(0)
                differences(1)
                queries(0)
                differences(2)
                queries(1)
                mask(0)
                differences(3)
                state(0)
                queries(2)
                mask(1)
                state(1)
                queries(3)
                mask(2)
                state(2)
                mask(3)
                state(3)
                link.end(TT)
            stage_end(dve, 3)
            for u in range(len(att) + 1):
                if u >= 1:
                    h, b = att[u - 1]
                    p, nk = (u - 1) % 2, (b + 1) * P
                    dve.wait_ge(at_exp, 2 * u)
                    link(dve.reciprocal(l_rec[:, p, :], l_sum[:, p, :]))
                    link(dve.tensor_scalar(l_rec[:, p, 1:2], l_rec[:, p, 1:2], lams, None, ALU.mult))
                    link(dve.tensor_scalar(PR[p][1][:, 0:nk], PR[p][1][:, 0:nk], l_rec[:, p, 1:2], None, ALU.mult))
                    dve.scalar_tensor_tensor(out=PR[p][0][:, 0:nk], in0=PR[p][0][:, 0:nk], scalar=l_rec[:, p, 0:1],
                                             in1=PR[p][1][:, 0:nk], op0=ALU.mult, op1=ALU.subtract).then_inc(at_comb, 1)
                if u < len(att):
                    h, b = att[u]
                    nk = (b + 1) * P
                    for c in range(2):
                        s = PS[:, 2 * c:2 * c + 2, :].rearrange("p a b -> p (a b)")
                        dve.wait_ge(at_s, 2 * u + c + 1)
                        link(dve.memset(s[0:CHUNK, nk - CHUNK:nk], -1.0e30))
                        link(dve.reduce_max(mx[:, u % 2, c:c + 1], s[:, 0:nk], AX_X))
                        dve.tensor_scalar(nmx[:, u % 2, c:c + 1], mx[:, u % 2, c:c + 1], -0.125, None, ALU.mult
                                          ).then_inc(at_max, 1)
            stage_end(dve, 4)
            link(dve.tensor_scalar(da_gain[:, :], da_gain[:, :], 1.0 - LAMBDA_INIT, None, ALU.mult))
            for da in range(2):
                buf = DA if da else INP
                for t in range(TT):
                    i = da * TT + t
                    dve.wait_ge(nrm_sq, i + 1)
                    dve.reduce_sum(norm_ss[:, t * 4:t * 4 + 4], SQN[i % 2][:, :].rearrange("p (h e) -> p h e", h=4), AX_X
                                   ).then_inc(nrm_ss, 1)
                dve.wait_ge(nrm_root, da + 1)
                link(dve.reciprocal(norm_r[:, :], norm_r[:, :]))
                if not da:
                    dve.wait_ge(gate_gain, TT)
                for t in range(TT):
                    o = buf[:, t, :].rearrange("p (h e) -> p h e", h=4)
                    link(dve.tensor_tensor(o, o, spread(norm_r[:, t * 4:t * 4 + 4], 2, P), ALU.mult))
                    by = spread(da_gain[:, :], 1, 4) if da else GATE[:, t, :].rearrange("p (h e) -> p h e", h=4)
                    ins = dve.tensor_tensor(o, o, by, ALU.mult)
                    if t == TT - 1:
                        ins.then_inc(nrm_r, 1)
            stage_end(dve, 5)
            dve.wait_ge(wo_in, 32)
            for t in range(TT + 1):
                if t < TT:
                    dve.wait_ge(mt_tr, t + 1)
                    dve.tensor_copy(MT[:, 4:8, t * P:(t + 1) * P], bank_tiles(1)).then_inc(mt_dve, 1)
                if t >= 1:
                    dve.wait_ge(n2_hi, t)
                    b = 4 + 2 * ((t - 1) % 2)
                    half, ts = (t - 1) // 4, slice((t - 1) % 4 * P, ((t - 1) % 4 + 1) * P)
                    dve.tensor_tensor(N2L[half][:, :, ts], bank_tiles(b, 2), N2H[half][:, :, ts].bitcast(F32),
                                      ALU.subtract).then_inc(n2_lo, 1)
                if t < TT:
                    dve.wait_ge(wo_done, t + 1)
                    dve.wait_ge(xn_in[t % 2], 16 * (t // 2 + 1))
                    if t >= 2:
                        dve.wait_ge(h_out[t % 2], 16 * (t // 2))
                    dve.tensor_tensor(H[t % 2][:, :].rearrange("p (a b) -> p a b", a=2), bank(2, 2),
                                      XN[t % 2][:, :].rearrange("p (a b) -> p a b", a=2), ALU.add).then_inc(h_ready, 1)
                    dve.wait_ge(h_ss, t + 1)
                    link(dve.reciprocal(norm_r[:, t:t + 1], norm_ss[:, t:t + 1]))
                    if t >= 2:
                        dve.wait_ge(n2_tr, t - 1)
                    dve.scalar_tensor_tensor(out=N2[t % 2][:, :], in0=H[t % 2][:, :], scalar=norm_r[:, t:t + 1],
                                             in1=ffn_w[:, :], op0=ALU.mult, op1=ALU.mult).then_inc(n2_ready, 1)
            stage_end(dve, 6)
            if stop == 6:
                return
            def top16(src, src2, vals, idx):
                for s, v in zip(src, vals):
                    dve.max(v[:, 0:8], s)
                dve.drain()
                for s, v, i in zip(src, vals, idx):
                    dve.max_index(i[:, 0:8], v[:, 0:8], s)
                for s, s2, v in zip(src, src2, vals):
                    dve.match_replace(s2, v[:, 0:8], s, LOWEST)
                dve.drain()
                for s2, v in zip(src2, vals):
                    dve.max(v[:, 8:16], s2)
                dve.drain()
                for s2, v, i in zip(src2, vals, idx):
                    dve.max_index(i[:, 8:16], v[:, 8:16], s2)
                dve.drain()

            def unit_halves(slot, loads, col):
                dve.wait_ge(su_in[slot], loads)
                dve.tensor_copy(su_seen[:, :], SU[slot][:, 0, 0:1])
                dve.drain()
                top16([SU[slot][:, a, :] for a in range(2)], [SU2[:, a, :] for a in range(2)],
                      [TOPV[:, a, :] for a in range(2)], [TOPI[:, a, :] for a in range(2)])
                dve.tensor_copy(I12[:, :, col], TOPI[:, :, :]).then_inc(su_used, 1)
                dve.tensor_tensor(CAND[:, :].rearrange("p (a b) -> p a b", a=TOPK), spread(TOPV[:, 0, :], 2, TOPK),
                                  spread(TOPV[:, 1, :], 1, TOPK), ALU.add)
                dve.drain()

            def unit_sums(col):
                top16([CAND[:, :]], [CAND2[:, :]], [TOPC], [TOPP])
                dve.tensor_copy(CS[:, col], TOPC[:, :])
                dve.tensor_copy(POS[:, col], TOPP[:, :])
                dve.drain()

            def tile_picks(t):
                cs = CS[:, :].rearrange("p (u k) -> p u k", k=TOPK)
                link(dve.tensor_copy(gmax[:, :], cs[:, :, 0]))
                dve.tensor_tensor(cs, cs, spread(gmax[:, :], 2, TOPK), ALU.subtract).then_inc(g_shift, 1)
                link(dve.tensor_scalar(ABU[:, :], POS[:, :], 4, None, ALU.logical_shift_right))
                link(dve.tensor_copy(AB[0][:, :], ABU[:, :]))
                link(dve.tensor_scalar(ABU[:, :], POS[:, :], 15, None, ALU.bitwise_and))
                link(dve.tensor_copy(AB[1][:, :], ABU[:, :]))
                dve.wait_ge(pk_tr, t + 1)
                for a in range(2):
                    for part in range(2):
                        ks = slice(64 * part, 64 * part + 64)
                        link(dve.tensor_tensor(EQ[:, :].rearrange("p (k a) -> p k a", a=TOPK), spread(AB[a][:, ks], 2, TOPK),
                                               spread(iota16, 1, 64), ALU.is_equal))
                        keys = I12[:, a, ks].rearrange("p (h a) -> p h a", a=TOPK)
                        link(dve.tensor_tensor(EQ2[:, :].rearrange("p (h k a) -> p h k a", h=4, k=TOPK),
                                               EQ[:, :].rearrange("p (h k a) -> p h k a", h=4, k=TOPK),
                                               spread(keys, 2, TOPK), ALU.mult))
                        link(dve.reduce_sum(PK[:, a, ks], EQ2[:, :].rearrange("p (k a) -> p k a", a=TOPK), AX_X))
                dve.wait_ge(g_exp, t + 1)
                link(dve.reduce_sum(gsum[:, :], cs, AX_X))
                link(dve.reciprocal(grec[:, :], gsum[:, :]))
                dve.tensor_tensor(PK[:, 2, :].rearrange("p (u k) -> p u k", k=TOPK), cs, spread(grec[:, :], 2, TOPK),
                                  ALU.mult).then_inc(pk_ready, 1)

            def route(t):
                with dve.Fori(0, PEER_HEADS // 2) as i:
                    for j in range(2):
                        col = bass.ds(i * 2 * TOPK + j * TOPK, TOPK)
                        unit_halves(j, i * 16 + 16 * (4 * t + 1), col)
                        unit_sums(col)
                tile_picks(t)

            def rows(B, qd, t, x):
                p = qd % 2
                dve.wait_ge(quad_done, B * 4 + (qd + 1))
                dve.wait_ge(pt_ready, t + 1)
                if not p:
                    dve.tensor_tensor(OH[0][:, :, :], spread(iota, 1, 4),
                                      spread(PT[t % 3][:, 1, bass.ds(x + 4 * qd, 4)], 2, P), ALU.is_equal)
                for j in range(4):
                    tok = bass.ds(x + (4 * qd + j), 1)
                    ins = dve.tensor_scalar(OG[p][:, j, :], iota, PT[t % 3][:, 0, tok], PT[t % 3][:, 2, tok],
                                            ALU.is_equal, ALU.mult)
                ins.then_inc(og_ready, 1)

            route(0)
            route(1)
            for what, t in BETWEEN:
                if what == "route":
                    route(t)
                else:
                    with dve.Fori(0, 8) as i:
                        for qd in range(4):
                            rows(i + 8 * t, qd, t, i * 16)
            stage_end(dve, 7)
            for half in range(2):
                c0 = half * KEYS

                def u_lo(c, j):
                    dve.wait_ge(uh, c0 + c + 1)
                    dve.tensor_tensor(UL[j % 2][:, :, :], UR[j % 2][:, :, :], UH[j % 2][:, :, :].bitcast(F32),
                                      ALU.subtract).then_inc(ul, 1)

                def gated(c, j):
                    dve.wait_ge(gelu, c0 + c + 3)
                    dve.wait_ge(g_in[j % 2], (c - j % 2 + c0) * 8 + 16)
                    dve.tensor_tensor(AF[j % 2][:, :], AF[j % 2][:, :], GT[j % 2][:, :], ALU.mult).then_inc(prod, 1)

                def a_lo(c, j):
                    dve.wait_ge(ah, c0 + c + 1)
                    dve.tensor_tensor(AL[j % 4][:, :], AF[j % 2][:, :], AH[j % 4][:, :].bitcast(F32),
                                      ALU.subtract).then_inc(al, 1)

                def add(g, t):
                    tt, dh = divmod(t, 2)
                    y = ACC[:, tt, dh * 512:(dh + 1) * 512]
                    dve.wait_ge(s2, (c0 // 2) * 8 + g * 8 + t + 17)
                    dve.tensor_tensor(y, bank(2 + t % 4), y, ALU.add).then_inc(acc_add, 1)

                def nothing():
                    pass

                def period(c, j, g=None, more_u=True, extra=(nothing,) * 4):
                    def adds(*ts):
                        for t in ts:
                            if g is not None:
                                add(g, t)

                    extra[0]()
                    gated(c, j)
                    a_lo(c, j)
                    if more_u:
                        u_lo(c + 2, j)
                    extra[1]()
                    gated(c + 1, j + 1)
                    adds(0)
                    a_lo(c + 1, j + 1)
                    adds(1, 2)
                    if more_u:
                        u_lo(c + 3, j + 1)
                    extra[2]()
                    adds(3, 4)
                    extra[3]()
                    adds(5, 6, 7)

                u_lo(0, 0)
                u_lo(1, 1)
                period(0, 0)
                dve.wait_ge(acc_in, 16 * (half + 1))
                if half == 0:
                    for seg in range(SEGMENTS):
                        t = 4 + seg // 2
                        with dve.Fori(0, turns_in(seg)) as i:
                            col = bass.ds(i * TOPK + (seg % 2) * 64, TOPK)
                            loads = i * 16 + 16 * (4 * BEFORE + 4 * seg + 1)
                            routing = (lambda: unit_halves(0, loads, col), lambda: unit_sums(col), nothing, nothing)
                            period(i * 4 + (16 * seg + 2), 2, i * 2 + 8 * seg, extra=routing if seg < 6 else (nothing,) * 4)
                            made = [lambda qd=qd: rows(i + (32 + 4 * seg), qd, t, i * 16 + (seg % 2) * 64) for qd in range(4)]
                            period(i * 4 + (16 * seg + 4), 0, i * 2 + (8 * seg + 1), extra=made)
                        if seg in (1, 3, 5):
                            tile_picks(t + 1)
                    period(KEYS - 2, 2, KEYS // 2 - 2, more_u=False)
                    for t in range(8):
                        if t % 2 == 0:
                            rows(63, t // 2, 7, 112)
                        add(KEYS // 2 - 1, t)
                else:
                    with dve.Fori(0, KEYS // 4 - 1) as i:
                        period(i * 4 + 2, 2, i * 2)
                        period(i * 4 + 4, 0, i * 2 + 1)
                    period(KEYS - 2, 2, KEYS // 2 - 2, more_u=False)
                    for t in range(8):
                        add(KEYS // 2 - 1, t)
                dve.wait_ge(y_root, half + 1)
                dve.wait_ge(consts_in, 16 * 9)
                link(dve.reciprocal(norm_r[:, 0:4], norm_ss[:, 0:4]))
                for t in range(4):
                    dve.scalar_tensor_tensor(out=ACC[:, t, :], in0=ACC[:, t, :], scalar=norm_r[:, t:t + 1], in1=fin_w[:, :],
                                             op0=ALU.mult, op1=ALU.mult).then_inc(y_ready, 1)

        @block.gpsimd
        def _(pool):
            pool.sem_inc(hg_k, 2)
            pool.sem_inc(vl, 2)
            stage_end(pool, 1)
            stage_end(pool, 2)
            pool.wait_ge(ready, 2 + HEADS)
            with pool.Fori(0, TT) as n:
                for h in range(HEADS):
                    p = h % 2
                    k = K[:, h, bass.ds(n * P, P)]
                    pool.wait_ge(hg_pe, n * 4 + h + 1)
                    pool.wait_ge(hg_exp, n * 4 + h + 1)
                    pool.tensor_copy(KL[p][:, 8, :], k)
                    pool.tensor_tensor(KL[p][:, 0:8, :], E[p][:, 1:9, :], spread(k, 1, 8), ALU.mult).then_inc(hg_k, 1)
            stage_end(pool, 3)
            stage_end(pool, 4)
            for t in range(TT):
                g = GATE[:, t, :].rearrange("p (h e) -> p h e", h=4)
                pool.tensor_tensor(g, g, spread(hg_gain[:, :], 1, 4), ALU.mult).then_inc(gate_gain, 1)
            stage_end(pool, 5)
            stage_end(pool, 6)
            if stop == 6:
                return
            for M in range(32):
                pool.wait_ge(wq_hi, M + 1)
                pool.tensor_tensor(WQL[M % 2][:, :, :], WQ[(M // 4) % 2][:, :, (M % 4) * P:(M % 4 + 1) * P],
                                   WQH[M % 2][:, :, :].bitcast(F32), ALU.subtract).then_inc(wq_lo, 1)
            stage_end(pool, 7)
            for half in range(2):
                c0 = half * KEYS

                def v_lo(c, j):
                    pool.wait_ge(vh, c0 + c + 1)
                    pool.tensor_tensor(VL[j % 4][:, :], VR[j % 2][:, :], VH[j % 4][:, :].bitcast(F32),
                                       ALU.subtract).then_inc(vl, 1)

                with pool.Fori(0, KEYS // 4) as i:
                    for j in range(4):
                        v_lo(i * 4 + j, j)


def kernel(x, norm_mix_w, w_in, hgrn_lb_param, hgrn_norm_w, diff_lambda, diff_norm_w, w_out, norm_ffn_w,
           peer_w_query, peer_sub_keys, peer_u, peer_v, norm_final_w):
    import concourse.bacc as bacc
    from concourse.bass_utils import run_bass_kernel_spmd

    def rows(a):
        return np.ascontiguousarray(np.asarray(a).reshape(-1, P, a.shape[-1]).transpose(1, 0, 2))

    def everywhere(a):
        return np.ascontiguousarray(np.broadcast_to(np.asarray(a), (P,) + a.shape))

    t = np.arange(P)
    level_masks = np.zeros((P, 8, P), np.float32)
    for l in range(LEVELS):
        m = 64 >> l
        same = t[:, None] // (2 * m) == t[None, :] // (2 * m)
        level_masks[:, l] = same & (t[None, :] % (2 * m) >= m) & (t[:, None] % (2 * m) < m)
    level_masks[:, 7] = np.eye(P)
    cst = np.concatenate([np.eye(P), np.ones((P, P)), np.broadcast_to(t, (P, P)),
                          np.broadcast_to(np.arange(16), (P, 16))], axis=1).astype(np.float32)
    x = np.asarray(x)
    ins = {
        "x_t": rows(x[0].T), "x_n": np.ascontiguousarray(x[0].reshape(TT, P, D)),
        "w_in": rows(w_in[0]), "w_out": rows(w_out[0]), "w_q": rows(peer_w_query[0]),
        "sub_t": np.ascontiguousarray(np.asarray(peer_sub_keys)[0].reshape(16, KEYS, P).transpose(2, 0, 1)),
        "u_t": np.ascontiguousarray(np.asarray(peer_u)[0].reshape(KEYS, P, KD, P).transpose(0, 3, 2, 1)),
        "v": np.ascontiguousarray(np.asarray(peer_v)[0].reshape(KEYS, P, D)),
        "norm_mix": np.ascontiguousarray(np.asarray(norm_mix_w)[0].reshape(KD, P).T),
        "norm_ffn": everywhere(norm_ffn_w[0]), "norm_fin": everywhere(norm_final_w),
        "lb": np.ascontiguousarray(np.asarray(hgrn_lb_param).reshape(2, HEADS, P).transpose(2, 0, 1)),
        "hg_norm": everywhere(hgrn_norm_w[0]), "da_norm": everywhere(diff_norm_w[0]),
        "lam": everywhere(diff_lambda[0]), "cst": cst, "level_masks": level_masks,
    }
    nc = bacc.Bacc("TRN2", target_bir_lowering=False, num_devices=1)
    args = {n: nc.dram_tensor(n, a.shape, F32, kind="ExternalInput").ap() for n, a in ins.items()}
    out = nc.dram_tensor("out", (TT, P, D), F32, kind="ExternalOutput").ap()
    h_dram = nc.dram_tensor("h_dram", (TT, P, D), F32, kind="Internal").ap()
    s_dram = nc.dram_tensor("s_dram", (TT, PEER_HEADS, P, 2 * KEYS), F32, kind="Internal").ap()
    gates_dram = nc.dram_tensor("gates_dram", (KEYS, KEYS, T), F32, kind="Internal").ap()
    n2_dram = nc.dram_tensor("n2_dram", (2, P, KD, HALF_T), F32, kind="Internal").ap()
    build(nc, **args, out=out, h_dram=h_dram, s_dram=s_dram, gates_dram=gates_dram, n2_dram=n2_dram)
    r = run_bass_kernel_spmd(nc, [ins], core_ids=[0])
    return r.results[0]["out"].reshape(1, T, D)
```

```python
from contextlib import ExitStack

import concourse.bass as bass
import numpy as np
from concourse import mybir

F32 = mybir.dt.float32
F32R = mybir.dt.float32r
U32 = mybir.dt.uint32
ALU = mybir.AluOpType
ACT = mybir.ActivationFunctionType
AX_X = mybir.AxisListType.X

P = 128
T = 1024
D = 1024
KD = D // P
TT = T // P
HEADS = 4
SECTIONS = 7
CHUNK = 64
PEER_HEADS = 8
TOPK = 16
KEYS = 128
UNITS = TT * PEER_HEADS
HALF_T = T // 2
LEVELS = 7
EPS = 1e-6
LAMBDA_INIT = 0.2
LOWEST = -3.0e38


class Links:

    def __init__(self, eng, sem):
        self.eng, self.sem, self.n, self.shift = eng, sem, 0, 0

    def __call__(self, ins):
        self.n += 1
        ins.then_inc(self.sem, 1)
        self.eng.wait_ge(self.sem, self.shift + self.n)

    def mark(self, ins):
        self.n += 1
        ins.then_inc(self.sem, 1)
        return self.n

    def wait(self, n):
        self.eng.wait_ge(self.sem, self.shift + n)

    def loop(self, i, per_turn):
        self.start, self.per_turn, self.shift = self.n, per_turn, i * per_turn

    def end(self, turns):
        assert self.n - self.start == self.per_turn, (self.n - self.start, self.per_turn)
        self.n, self.shift = self.start + turns * self.per_turn, 0


def spread(ap, axis, n):
    ap = ap.unsqueeze(axis)
    shape = list(ap.shape)
    shape[axis] = n
    return ap.broadcast_to(shape)


def build(nc, x_t, x_n, w_in, w_out, w_q, sub_t, u_t, v, norm_mix, norm_ffn, norm_fin, lb, hg_norm,
          da_norm, lam, cst, level_masks, out, h_dram, s_dram, gates_dram, n2_dram, a_dram):
    with ExitStack() as ctx:
        base = (nc.sbuf_base + 127) // 128 * 128
        KB = 1024

        def at(name, kb, shape, dt=F32):
            return nc.alloc_sbuf_tensor_at(name, shape, dt, offset=base + int(kb * KB))

        def sem(name):
            return ctx.enter_context(nc.semaphore(name))

        PS = ctx.enter_context(nc.psum_tensor("PS", [P, 8, 512], F32))

        def bank(b, n=1):
            return PS[:, b, :] if n == 1 else PS[:, b:b + n, :]

        def bank_tiles(b, n=1):
            return PS[:, b:b + n, :].rearrange("p a (b c) -> p (a b) c", c=128)

        consts = at("consts", 0, [P, 400])
        ident, ones, iota, iota16 = consts[:, 0:128], consts[:, 128:256], consts[:, 256:384], consts[:, 384:400]
        masks = at("masks", 2, [P, 8, 128])
        hg_gain = at("hg_gain", 6, [P, 128])
        da_gain = at("da_gain", 6.5, [P, 128])
        lam_in = at("lam_in", 7, [P, 4, 64])
        mix_w = at("mix_w", 8, [P, KD])
        lb_in = at("lb_in", 8.0625, [P, 2, HEADS])
        small = at("small", 8.125, [P, 96])
        eps = small[:, 0:1]
        lbs, one_lb, lb_t = small[:, 4:8], small[:, 8:12], small[:, 12:20]
        lams, lam_t = small[:, 20:21], small[:, 24:26]
        zero_col = small[:, 28:29]
        norm_ss, norm_r = at("norm_ss", 8.5, [P, 32]), at("norm_r", 8.625, [P, 32])
        l_sum, l_rec, mx, nmx = (at(n, 8.75 + i / 16, [P, 2, 2]) for i, n in enumerate(("l_sum", "l_rec", "mx", "nmx")))
        zeros = at("zeros", 9, [P, 128])

        X = at("X", 10, [P, KD, T])
        W = [at(f"W{i}", 42 + 16 * i, [P, KD, 512]) for i in range(2)]
        sq = [at(f"sq{i}", 74 + 4 * i, [P, T]) for i in range(2)]
        rstd = at("rstd", 82, [P, T])
        Q = at("Q", 74, [P, HEADS, T])
        F = at("F", 90, [P, HEADS, T])
        K = at("K", 106, [P, HEADS, T])
        INP = at("INP", 122, [P, TT, 512])
        GATE = at("GATE", 138, [P, TT, 512])
        DQ = at("DQ", 154, [P, HEADS, T])
        DK = at("DK", 170, [P, HEADS, T])
        DV = at("DV", 186, [P, TT, 512])
        E = [at(f"E{i}", 10 + 4.5 * i, [P, 9, 128]) for i in range(2)]
        QL = [at(f"QL{i}", 19 + 4.5 * i, [P, 9, 128]) for i in range(2)]
        KL = [at(f"KL{i}", 28 + 4.5 * i, [P, 9, 128]) for i in range(2)]
        M = [at(f"M{i}", 42 + 4 * i, [P, 8, 128]) for i in range(2)]
        KN = [at(f"KN{i}", 50 + i / 2, [P, 128]) for i in range(2)]
        STATE = at("STATE", 51, [P, HEADS, 128])
        BL = [at(f"BL{i}", 53 + i / 16, [P, 1]) for i in range(2)]
        PR = [[at(f"PR{i}{c}", 74 + 8 * i + 4 * c, [P, T]) for c in range(2)] for i in range(2)]
        AT = [at(f"AT{i}", 90 + 4 * i, [P, TT, 128]) for i in range(2)]
        DA = at("DA", 106, [P, TT, 512])
        SQN = [at(f"SQN{i}", 98 + 2 * i, [P, 512]) for i in range(2)]
        MT = at("MT", 10, [P, KD, T])
        WO = at("WO", 42, [P, KD, D])
        N2H = [at(f"N2H{i}", kb, [P, KD, HALF_T], F32R) for i, kb in enumerate((154, 74))]
        N2L = [at(f"N2L{i}", kb, [P, KD, HALF_T], F32R) for i, kb in enumerate((170, 90))]
        XN = [at(f"XN{i}", 138 + 4 * i, [P, D]) for i in range(2)]
        H = [at(f"H{i}", 146 + 4 * i, [P, D]) for i in range(2)]
        N2 = [at(f"N2{i}", 186 + 4 * i, [P, D]) for i in range(2)]
        ffn_w = at("ffn_w", 194, [P, D])
        junk = at("junk", 198, [P, D])
        WQ = [at(f"WQ{i}", 10 + 16 * i, [P, KD, 512]) for i in range(2)]
        WQH = [at(f"WQH{i}", 42 + 4 * i, [P, KD, 128], F32R) for i in range(2)]
        WQL = [at(f"WQL{i}", 50 + 4 * i, [P, KD, 128], F32R) for i in range(2)]
        QH = [at(f"QH{i}", 58 + 2 * i, [P, HALF_T]) for i in range(2)]
        SUB = at("SUB", 106, [P, 16, 128])
        SS = [at(f"SS{i}", 114 + 2 * i, [P, TT // 2, 128]) for i in range(2)]
        SU = [at(f"SU{i}", 186 + i, [P, 2, 128]) for i in range(2)]
        ABS = at("ABS", 188, [P, 4, 128])
        SU2 = at("SU2", 190, [P, 2, 128])
        TOPV = at("TOPV", 191, [P, 2, TOPK])
        TOPI = at("TOPI", 191.25, [P, 2, TOPK], U32)
        TOPC = at("TOPC", 191.5, [P, TOPK])
        TOPP = at("TOPP", 191.625, [P, TOPK], U32)
        su_seen = at("su_seen", 191.75, [P, 1])
        CAND = at("CAND", 192, [P, TOPK * TOPK])
        CAND2 = at("CAND2", 193, [P, TOPK * TOPK])
        I12 = [at(f"I12{i}", kb, [P, 2, P]) for i, kb in enumerate((194, 70))]
        CS = at("CS", 195, [P, P])
        POS = at("POS", 195.5, [P, P], U32)
        AB = [at(f"AB{i}", kb, [P, 2, P]) for i, kb in enumerate((196, 71))]
        ABU = at("ABU", 197, [P, P], U32)
        gsum, grec, gmax = (at(n, 197.5 + i / 8, [P, PEER_HEADS]) for i, n in enumerate(("gsum", "grec", "gmax")))
        EQ = at("EQ", 66, [P, 2 * TOPK * TOPK])
        EQ2 = at("EQ2", 68, [P, 2 * TOPK * TOPK])
        PT = [at(f"PT{i}", 2 + 1.5 * i, [P, 3, P]) for i in range(3)]
        PK = at("PK", 6.5, [P, 3, P])
        DIFF = at("DIFF", 72, [P, 4, 128])
        OH = [at(f"OH{i}", 198 + 2 * i, [P, 4, 128]) for i in range(2)]
        OG = [at(f"OG{i}", 202 + 2 * i, [P, 4, 128]) for i in range(2)]
        GS = [at(f"GS{i}", 74 + 32 * i, [P, KEYS, 64]) for i in range(2)]
        UR = [at(f"UR{i}", 10 + 4 * i, [P, KD, 128]) for i in range(2)]
        VR = [at(f"VR{i}", 18 + 4 * i, [P, D]) for i in range(2)]
        UH = [at(f"UH{i}", 26 + 4 * i, [P, KD, 128], F32R) for i in range(2)]
        UL = [at(f"UL{i}", 34 + 4 * i, [P, KD, 128], F32R) for i in range(2)]
        GT = [at(f"GT{i}", 42 + 2 * i, [P, HALF_T]) for i in range(2)]
        AF = [at(f"AF{i}", 46 + 2 * i, [P, HALF_T]) for i in range(2)]
        AH = [at(f"AH{i}", 50 + 2 * i, [P, HALF_T], F32R) for i in range(4)]
        AL = [at(f"AL{i}", 58 + 2 * i, [P, HALF_T], F32R) for i in range(4)]
        VH = [at(f"VH{i}", 106 + 4 * i, [P, D], F32R) for i in range(4)]
        VL = [at(f"VL{i}", 122 + 4 * i, [P, D], F32R) for i in range(4)]
        ACC = [at(f"ACC{i}", kb, [P, TT // 2, D]) for i, kb in enumerate((138, 74))]
        FSQ = at("FSQ", 66, [P, D])
        fin_w = at("fin_w", 70, [P, D])

        consts_in, x_in = sem("consts_in"), [sem(f"x_in{k}") for k in range(KD)]
        w_in_sem = [sem(f"w_in{i}") for i in range(2)]
        stage_done = sem("stage_done")
        sq_ready, sq_used, root_ready, n1_ready = sem("sq_ready"), sem("sq_used"), sem("root_ready"), sem("n1_ready")
        proj_done = sem("proj_done")
        proj_out = {"act": sem("proj_out_act"), "dve": sem("proj_out_dve")}
        ready = sem("ready")
        log_f = sem("log_f")
        hg_diff, hg_exp, hg_q, hg_k, hg_scores, hg_mask, hg_kn, hg_pe, hg_state, hg_out = (
            sem("hg_" + n) for n in ("diff", "exp", "q", "k", "scores", "mask", "kn", "pe", "state", "out"))
        at_s, at_max, at_exp, at_comb, at_tr, at_t, at_o, at_oe = (
            sem("at_" + n) for n in ("s", "max", "exp", "comb", "tr", "t", "o", "oe"))
        nrm_sq, nrm_ss, nrm_root, nrm_r = sem("nrm_sq"), sem("nrm_ss"), sem("nrm_root"), sem("nrm_r")
        mt_tr, mt_act, mt_dve, wo_in, wo_done, h_ready, h_ss, n2_ready, n2_tr, n2_hi, n2_lo = (
            sem(n) for n in ("mt_tr", "mt_act", "mt_dve", "wo_in", "wo_done", "h_ready", "h_ss", "n2_ready", "n2_tr", "n2_hi", "n2_lo"))
        xn_in = [sem(f"xn_in{i}") for i in range(2)]
        h_out = [sem(f"h_out{i}") for i in range(2)]
        wq_in = [sem(f"wq_in{i}") for i in range(2)]
        wq_hi, wq_lo, qh_done, qh_out, sc_done, sc_out = (sem(n) for n in ("wq_hi", "wq_lo", "qh_done", "qh_out", "sc_done", "sc_out"))
        ss_out = [sem(f"ss_out{i}") for i in range(2)]
        su_in = [sem(f"su_in{i}") for i in range(2)]
        su_used, pk_ready, pk_tr, pt_ready, g_exp, g_shift = (sem(n) for n in ("su_used", "pk_ready", "pk_tr", "pt_ready", "g_exp", "g_shift"))
        og_ready, oh_even, oh_odd, quad_done, quad_out, n2_kept, n2_in = (sem(n) for n in ("og_ready", "oh_even", "oh_odd", "quad_done", "quad_out", "n2_kept", "n2_in"))
        gs_out = [sem(f"gs_out{i}") for i in range(2)]
        gate_gain = sem("gate_gain")
        u_in, v_in, g_in = ([sem(f"{n}_in{i}") for i in range(2)] for n in "uvg")
        uh, ul, vh, vl, s1, gelu, prod, ah, al, s2, acc_add = (
            sem("p_" + n) for n in ("uh", "ul", "vh", "vl", "s1", "gelu", "prod", "ah", "al", "s2", "acc"))
        acc_in = [sem(f"acc_in{i}") for i in range(2)]
        af_out, af_in = ([sem(f"af_{n}{i}") for i in range(2)] for n in ("out", "in"))
        y_root, y_ready, y_out = (sem(n) for n in ("y_root", "y_ready", "y_out"))
        act_own, dve_own, pool_own = sem("act_own"), sem("dve_own"), sem("pool_own")

        def stage_end(eng, n):
            eng.drain().then_inc(stage_done, 1)
            eng.wait_ge(stage_done, 5 * n)

        def taker(G):
            return "act" if G // 8 in (1, 3) or G % 2 == 0 else "dve"

        def taken(G):
            return taker(G), sum(taker(g) == taker(G) for g in range(G + 1))

        def proj_dst(G):
            s, g = divmod(G, 8)
            dst = (Q, F, INP, GATE, DQ, DK, DV)[s]
            if s in (2, 3, 6):
                return dst[:, g, :]
            return dst[:, g // 2, (g % 2) * 512:(g % 2) * 512 + 512]

        att = [(h, b) for h in range(HEADS) for b in range(TT)]

        PERIODS = TT
        AHEAD = KEYS // 2

        def segment(k, b):
            return 1 if (k, b) == (PERIODS - 1, 1) else 2

        block = ctx.enter_context(nc.Block())

        @block.sync
        def _(sp):
            for dst, src in ((consts[:, :], cst), (masks[:, :, :], level_masks), (mix_w[:, :], norm_mix),
                             (lb_in[:, :, :], lb)):
                sp.dma_start(dst, src).then_inc(consts_in, 16)
            for k in range(KD):
                sp.dma_start(X[:, k, :], x_t[:, k, :]).then_inc(x_in[k], 16)
            for dst, src in ((hg_gain[:, :], hg_norm), (da_gain[:, :], da_norm), (lam_in[:, :, :], lam)):
                sp.dma_start(dst, src).then_inc(consts_in, 16)
            for s in range(SECTIONS):
                if s == 2:
                    stage_end(sp, 1)
                if s >= 2:
                    sp.wait_ge(proj_done, 8 * (s - 1))
                sp.dma_start(W[s % 2][:, :, :], w_in[:, :, s * 512:(s + 1) * 512]).then_inc(w_in_sem[s % 2], 16)
            for n in (2, 3):
                stage_end(sp, n)
            sp.dma_start(WO[:, :, :], w_out).then_inc(wo_in, 16)
            for n in (4, 5):
                stage_end(sp, n)
            sp.dma_start(XN[0][:, :], x_n[0]).then_inc(xn_in[0], 16)
            sp.dma_start(ffn_w[:, :], norm_ffn).then_inc(wo_in, 16)
            for t in range(TT):
                if t + 1 < TT:
                    if t >= 1:
                        sp.wait_ge(h_ready, t)
                    sp.dma_start(XN[(t + 1) % 2][:, :], x_n[t + 1]).then_inc(xn_in[(t + 1) % 2], 16)
                sp.wait_ge(h_ready, t + 1)
                sp.dma_start(h_dram[t], H[t % 2][:, :]).then_inc(h_out[t % 2], 16)
            sp.wait_ge(h_out[0], 16 * TT // 2)
            sp.wait_ge(h_out[1], 16 * TT // 2)
            stage_end(sp, 6)
            sp.dma_start(SUB[:, :, :], sub_t).then_inc(consts_in, 16)
            s_units = s_dram.rearrange("a h p n -> (a h) p n")

            def load_unit(u, slot):
                src = s_units[bass.ds(u, 1), :, :].rearrange("o p (a n) -> p (o a) n", a=2)
                sp.dma_start(SU[slot][:, :, :], src).then_inc(su_in[slot], 16)

            for u in range(PEER_HEADS):
                for q in ss_out:
                    sp.wait_ge(q, 16 * (u + 1))
                if u >= 2:
                    sp.wait_ge(su_used, u + 1)
                load_unit(u, u % 2)
            with sp.Fori(0, PEER_HEADS // 2) as i:
                for j in range(2):
                    sp.wait_ge(su_used, i * 2 + (PEER_HEADS + j + 1))
                    load_unit(i * 2 + (PEER_HEADS + j), j)
            def load_u(U, c, j):
                sp.wait_ge(ul, U + 1)
                sp.dma_start(UR[j % 2][:, :, :], u_t[bass.ds(c, 1)].rearrange("o p k n -> p (o k) n")
                             ).then_inc(u_in[j % 2], 16)

            sp.wait_ge(wq_lo, 28)
            load_u(0, 0, 0)
            load_u(1, 1, 1)
            stage_end(sp, 7)
            sp.dma_start(ACC[0][:, :, :], h_dram[0:4].rearrange("a p d -> p a d")).then_inc(acc_in[0], 16)

            def load_vg(place, c, j, half):
                sp.wait_ge(prod, place + 1)
                sp.dma_start(GT[j % 2][:, :], gates_dram[bass.ds(c, 1), :, half * HALF_T:(half + 1) * HALF_T]
                             .rearrange("o p t -> p (o t)")).then_inc(g_in[j % 2], 16)
                sp.wait_ge(stage_done, 5 * 7)
                sp.wait_ge(vl, place + 1)
                sp.dma_start(VR[j % 2][:, :], v[bass.ds(c, 1)].rearrange("o p d -> p (o d)")).then_inc(v_in[j % 2], 16)

            def load_unit_of(k, b, i, j):
                u = 8 * (k + 2) + 4 * b + j
                sp.wait_ge(su_used, i * 2 + (u + 1))
                load_unit(i * 2 + u, j)

            def store_gates(b, n):
                sp.wait_ge(quad_out, 16 * (b + 1) + 2)
                sp.dma_start(gates_dram[bass.ds(n, 16), :, b * 64:(b + 1) * 64].rearrange("a p t -> p a t"),
                             GS[b % 2 if b < 8 else 0][:, bass.ds(n, 16), :]).then_inc(gs_out[b % 2 if b < 8 else 0], 16)

            for q in ss_out:
                sp.wait_ge(q, 16 * 16)
            for k in range(4):
                for b in range(2):
                    with sp.Fori(0, 2) as i:
                        for j in range(4):
                            c = 16 * k + 8 * b + j
                            if j % 2 == 0:
                                load_unit_of(k, b, i, j // 2)
                            load_u(i * 4 + (c + 2), i * 4 + (c + 2), j)
                            if (k, b) != (0, 0):
                                store_gates(2 * k + b - 1, i * 64 + 16 * j)
                            sp.wait_ge(stage_done, 5 * 7)
                            sp.wait_ge(gelu, i * 4 + (c + 3))
                            sp.dma_start(a_dram[bass.ds(i * 4 + c, 1)].rearrange("o p t -> p (o t)"), AF[j % 2][:, :]
                                         ).then_inc(af_out[j % 2], 16)
            for n in range(8):
                store_gates(7, 16 * n)
            sp.wait_ge(gs_out[0], 128 * 4)
            sp.wait_ge(gs_out[1], 128 * 4)
            for j in range(2):
                load_vg(j, AHEAD + j, j, 0)
                load_u(AHEAD + 2 + j, AHEAD + 2 + j, j)
            for k in range(4, PERIODS):
                for b in range(2):
                    for i in range(segment(k, b)):
                        place = 16 * (k - 4) + 8 * b + 2 + 4 * i
                        for j in range(4):
                            if k + 2 < PERIODS and j % 2 == 0:
                                load_unit_of(k, b, i, j // 2)
                            load_vg(place + j, AHEAD + place + j, j, 0)
                            load_u(AHEAD + place + 2 + j, AHEAD + place + 2 + j, j)
                            if i == 0 and (k, b) != (4, 0) and j in (1, 3):
                                for n in range(4):
                                    store_gates(2 * k + b - 1, 32 * (j - 1) + 16 * n)
            for j in range(2):
                load_vg(AHEAD - 2 + j, KEYS - 2 + j, j, 0)
            sp.wait_ge(s1, KEYS + 2)
            sp.wait_ge(n2_kept, 32)
            sp.dma_start(N2H[0][:, :, :].bitcast(F32), n2_dram[0]).then_inc(n2_in, 16)
            sp.dma_start(N2L[0][:, :, :].bitcast(F32), n2_dram[1]).then_inc(n2_in, 16)
            for q in af_out:
                sp.wait_ge(q, 16 * AHEAD // 2)
            load_u(KEYS, 0, 0)
            load_u(KEYS + 1, 1, 1)

            def load_places(i):
                for j in range(4):
                    load_vg(i * 4 + (AHEAD + j), i * 4 + j, j, 0)
                    sp.wait_ge(stage_done, 5 * 7)
                    sp.wait_ge(al, i * 4 + (AHEAD + j + 1))
                    sp.dma_start(AF[j % 2][:, :], a_dram[bass.ds(i * 4 + j, 1)].rearrange("o p t -> p (o t)")
                                 ).then_inc(af_in[j % 2], 16)

            for i in range(4):
                load_places(i)
                for n in range(2):
                    store_gates(15, 32 * i + 16 * n)
            with sp.Fori(0, AHEAD // 4 - 4) as i:
                load_places(i + 4)
            sp.wait_ge(gs_out[0], 128 * 12)
            sp.dma_start(ACC[1][:, :, :], h_dram[4:8].rearrange("a p d -> p a d")).then_inc(acc_in[1], 16)
            sp.wait_ge(pk_ready, 8 * TT)
            sp.dma_start(fin_w[:, :], norm_fin).then_inc(consts_in, 16)
            for j in range(2):
                load_vg(KEYS + j, j, j, 1)
                load_u(KEYS + 2 + j, 2 + j, j)
            for t in range(4):
                sp.wait_ge(y_ready, t + 1)
                sp.dma_start(out[t], ACC[0][:, t, :]).then_inc(y_out, 16)
            with sp.Fori(0, KEYS // 4 - 1) as i:
                for j in range(4):
                    load_vg(i * 4 + (KEYS + 2 + j), i * 4 + (2 + j), j, 1)
                    load_u(i * 4 + (KEYS + 4 + j), i * 4 + (4 + j), j)
            for j in range(2):
                load_vg(2 * KEYS - 2 + j, KEYS - 2 + j, j, 1)
            for t in range(4, TT):
                sp.wait_ge(y_ready, t + 1)
                sp.dma_start(out[t], ACC[1][:, t - 4, :]).then_inc(y_out, 16)
            sp.wait_ge(y_out, 16 * TT)

        @block.tensor
        def _(pe):
            pe.sem_inc(hg_pe, 2)
            pe.sem_inc(s1, 2)
            pe.sem_inc(s2, 16)
            pe.sem_inc(quad_done, 2)
            pe.sem_inc(pk_tr, 1)
            pe.wait_ge(consts_in, 16 * 7)
            for k in range(KD):
                pe.wait_ge(sq_ready, k + 1)
                for th in range(2):
                    mm = pe.matmul(bank(th), ones, sq[k % 2][:, th * 512:(th + 1) * 512], start=k == 0, stop=k == KD - 1)
                mm.then_inc(sq_used, 1)
            stage_end(pe, 1)
            for G in range(8 * SECTIONS):
                s, g = divmod(G, 8)
                if g == 0:
                    pe.wait_ge(w_in_sem[s % 2], 16 * (s // 2 + 1))
                if G >= 4:
                    who, n = taken(G - 4)
                    pe.wait_ge(proj_out[who], n)
                for k in range(KD):
                    if s in (2, 3, 6):
                        l, r = X[:, k, g * P:(g + 1) * P], W[s % 2][:, k, :]
                    else:
                        l, r = W[s % 2][:, k, (g // 2) * P:(g // 2 + 1) * P], X[:, k, (g % 2) * 512:(g % 2 + 1) * 512]
                    mm = pe.matmul(bank(G % 4), l, r, start=k == 0, stop=k == KD - 1)
                mm.then_inc(proj_done, 1)
            stage_end(pe, 2)
            with pe.Fori(0, TT) as n:
                def scores(h):
                    p = h % 2
                    pe.wait_ge(hg_q, n * 4 + h + 3)
                    pe.wait_ge(hg_k, n * 4 + h + 3)
                    pe.wait_ge(hg_mask, n * 4 + h + 1)
                    for l in range(8):
                        pe.matmul(bank_tiles(2 * p, 2)[:, l, :], KL[p][:, l if l < 7 else 8, :],
                                  QL[p][:, l + 1, :], start=True, stop=True)
                    pe.wait_ge(hg_state, n * 4 + h + 1)
                    pe.transpose(PS[:, 6 + p, 0:128], KL[p][:, 7, :], ident).then_inc(hg_scores, 1)

                def outputs(h):
                    p = h % 2
                    vals = INP[:, bass.ds(n, 1), h * 128:(h + 1) * 128].rearrange("p o e -> p (o e)")
                    pe.wait_ge(hg_mask, n * 4 + h + 3)
                    pe.wait_ge(hg_out, n * 4 + h + 1)
                    for l in range(8):
                        pe.matmul(PS[:, 4 + p, 0:128], M[p][:, l, :], vals, start=l == 0, stop=False)
                    pe.matmul(PS[:, 4 + p, 0:128], QL[p][:, 0, :], STATE[:, h, :], start=False, stop=True)
                    pe.wait_ge(hg_kn, n * 4 + h + 1)
                    pe.matmul(PS[:, 6 + p, 0:128], KN[p][:, :], vals, start=True, stop=True).then_inc(hg_pe, 1)

                scores(0)
                scores(1)
                outputs(0)
                scores(2)
                outputs(1)
                scores(3)
                outputs(2)
                outputs(3)
            stage_end(pe, 3)
            def att_scores(u):
                h, b = att[u]
                if u >= 1:
                    pe.wait_ge(at_exp, 2 * u)
                for c in range(2):
                    for n0 in range(0, (b + 1) * P, 512):
                        n1 = min((b + 1) * P, n0 + 512)
                        mm = pe.matmul(PS[:, 2 * c + n0 // 512, 0:n1 - n0],
                                       DQ[64 * c:64 * c + 64, h, b * P:(b + 1) * P],
                                       DK[64 * c:64 * c + 64, h, n0:n1], start=True, stop=True)
                    mm.then_inc(at_s, 1)

            def att_turn(u):
                h, b = att[u]
                pe.wait_ge(at_comb, u + 1)
                if u >= 1:
                    pe.wait_ge(at_t, u)
                for j in range(b + 1):
                    mm = pe.transpose(PS[:, 4 + j // 4, (j % 4) * P:(j % 4 + 1) * P],
                                      PR[u % 2][0][:, j * P:(j + 1) * P], ident)
                mm.then_inc(at_tr, 1)

            def att_out(u):
                h, b = att[u]
                pe.wait_ge(at_t, u + 1)
                if u >= 2:
                    pe.wait_ge(at_oe, u - 1)
                for j in range(b + 1):
                    mm = pe.matmul(PS[:, 6 + u % 2, 0:128], AT[u % 2][:, j, :], DV[:, j, h * 128:(h + 1) * 128],
                                   start=j == 0, stop=j == b)
                mm.then_inc(at_o, 1)

            for u in range(len(att) + 2):
                if u < len(att):
                    att_scores(u)
                if u >= 2:
                    att_out(u - 2)
                if 1 <= u <= len(att):
                    att_turn(u - 1)
            stage_end(pe, 4)
            stage_end(pe, 5)
            def turn_mixed(t):
                if t >= 1:
                    pe.wait_ge(mt_act, t)
                    pe.wait_ge(mt_dve, t)
                for k in range(KD):
                    src = INP if k < 4 else DA
                    mm = pe.transpose(PS[:, k // 4, (k % 4) * P:(k % 4 + 1) * P], src[:, t, (k % 4) * P:(k % 4 + 1) * P], ident)
                mm.then_inc(mt_tr, 1)

            def project_out(t):
                pe.wait_ge(mt_act, t + 1)
                pe.wait_ge(mt_dve, t + 1)
                if t >= 1:
                    pe.wait_ge(h_ready, t)
                for dh in range(2):
                    for k in range(KD):
                        mm = pe.matmul(bank(2 + dh), MT[:, k, t * P:(t + 1) * P], WO[:, k, dh * 512:(dh + 1) * 512],
                                       start=k == 0, stop=k == KD - 1)
                mm.then_inc(wo_done, 1)

            def turn_n2(t):
                pe.wait_ge(n2_ready, t + 1)
                if t >= 2:
                    pe.wait_ge(n2_lo, t - 1)
                for k in range(KD):
                    mm = pe.transpose(PS[:, 4 + 2 * (t % 2) + k // 4, (k % 4) * P:(k % 4 + 1) * P],
                                      N2[t % 2][:, k * P:(k + 1) * P], ident)
                mm.then_inc(n2_tr, 1)

            pe.wait_ge(wo_in, 32)
            turn_mixed(0)
            for t in range(TT + 1):
                if t + 1 < TT:
                    turn_mixed(t + 1)
                if t < TT:
                    project_out(t)
                if t >= 1:
                    turn_n2(t - 1)
            stage_end(pe, 6)
            pe.wait_ge(consts_in, 16 * 8)

            def queries(M):
                half, m = divmod(M, 16)
                pe.wait_ge(wq_lo, M + 1)
                if M >= 2:
                    pe.wait_ge(qh_out, M - 1)
                for k in range(KD):
                    for j, (a, b) in enumerate(((WQH, N2H), (WQH, N2L), (WQL, N2H))):
                        mm = pe.matmul(bank(M % 2), a[M % 2][:, k, :], b[half][:, k, :], start=k == 0 and j == 0,
                                       stop=k == KD - 1 and j == 2)
                mm.then_inc(qh_done, 1)

            def key_scores(M):
                pe.wait_ge(qh_out, M + 1)
                if M >= 2:
                    pe.wait_ge(sc_out, M - 1)
                for t in range(TT // 2):
                    mm = pe.matmul(PS[:, 2 + M % 2, t * P:(t + 1) * P], QH[M % 2][:, t * P:(t + 1) * P],
                                   SUB[:, M % 16, :], start=True, stop=True)
                mm.then_inc(sc_done, 1)

            def turn_picks(t):
                pe.wait_ge(pk_ready, 8 * (t + 1))
                pe.wait_ge(quad_out, 32 * t + 2)
                if t >= 1:
                    pe.wait_ge(pt_ready, t)
                for j in range(3):
                    mm = pe.transpose(PS[:, 7, j * P:(j + 1) * P], PK[:, j, :], ident)
                mm.then_inc(pk_tr, 1)

            def quad(B, qd, t):
                p = qd % 2
                pe.wait_ge(og_ready, B * 4 + (qd + 1))
                pe.wait_ge(oh_odd if p else oh_even, B * 2 + (qd // 2 + (2 if p else 1)))
                if p:
                    pe.wait_ge(pt_ready, t + 1)
                pe.wait_ge(quad_out, B * 4 + (qd + 1))
                for j in range(4):
                    mm = pe.matmul(PS[:, 6 + p, j * P:(j + 1) * P], OH[p][:, j, :], OG[p][:, j, :], start=True, stop=True)
                mm.then_inc(quad_done, 1)

            for n in range(33):
                if n < 32:
                    queries(n)
                if n >= 1:
                    key_scores(n - 1)
            stage_end(pe, 7)

            def first(U, j):
                pe.wait_ge(ul, U + 3)
                pe.wait_ge(gelu, U + 1)
                for k in range(KD):
                    for q, (a, b) in enumerate(((UH, N2H), (UH, N2L), (UL, N2H))):
                        mm = pe.matmul(bank(j % 2), a[j % 2][:, k, :], b[0][:, k, :], start=k == 0 and q == 0,
                                       stop=k == KD - 1 and q == 2)
                mm.then_inc(s1, 1)

            def second(g, j, quads=None):
                pe.wait_ge(al, g * 2 + 4)
                pe.wait_ge(vl, g * 2 + 4)
                for t in range(8):
                    tt, dh = divmod(t, 2)
                    pe.wait_ge(acc_add, g * 8 + t + 1)
                    for c in (2 * j, 2 * j + 1):
                        for q, (a, b) in enumerate(((AH, VH), (AH, VL), (AL, VH))):
                            mm = pe.matmul(bank(2 + t % 4), a[c][:, tt * P:(tt + 1) * P], b[c][:, dh * 512:(dh + 1) * 512],
                                           start=c == 2 * j and q == 0, stop=c == 2 * j + 1 and q == 2)
                    mm.then_inc(s2, 1)
                    if quads:
                        quad(quads[0], t, quads[1])

            for k in range(4):
                turn_picks(k)
                for b in range(2):
                    with pe.Fori(0, 2) as i:
                        for j in range(4):
                            first(i * 4 + (16 * k + 8 * b + j), j)
                            for qd in (2 * (j % 2), 2 * (j % 2) + 1):
                                quad(i * 2 + (8 * k + 4 * b + j // 2), qd, k)
            turn_picks(4)
            first(AHEAD, 0)
            first(AHEAD + 1, 1)
            for k in range(4, PERIODS):
                if k > 4:
                    turn_picks(k)
                for b in range(2):
                    with pe.Fori(0, segment(k, b)) as i:
                        place = 16 * (k - 4) + 8 * b + 2
                        for j in range(2):
                            first(i * 4 + (AHEAD + place + 2 * j), 0)
                            first(i * 4 + (AHEAD + place + 2 * j + 1), 1)
                            second(i * 2 + (place // 2 - 1 + j), j, (i * 2 + (8 * k + 4 * b), k) if j else None)
            first(KEYS - 2, 0)
            first(KEYS - 1, 1)
            second(AHEAD // 2 - 2, 0)
            second(AHEAD // 2 - 1, 1, (62, 7))
            with pe.Fori(0, AHEAD // 4 - 1) as i:
                second(i * 2 + AHEAD // 2, 0)
                second(i * 2 + (AHEAD // 2 + 1), 1)
            second(KEYS // 2 - 2, 0)
            pe.wait_ge(n2_in, 32)
            first(KEYS, 0)
            first(KEYS + 1, 1)
            second(KEYS // 2 - 1, 1)
            with pe.Fori(0, KEYS // 4 - 1) as i:
                for j in range(2):
                    first(i * 4 + (KEYS + 2 + 2 * j), 0)
                    first(i * 4 + (KEYS + 3 + 2 * j), 1)
                    second(i * 2 + (KEYS // 2 + j), j)
            first(2 * KEYS - 2, 0)
            first(2 * KEYS - 1, 1)
            second(KEYS - 2, 0)
            second(KEYS - 1, 1)

        @block.scalar
        def _(act):
            link = Links(act, act_own)
            act.sem_inc(hg_out, 2)
            act.sem_inc(gelu, 2)
            act.sem_inc(quad_out, 2)
            act.sem_inc(oh_odd, 1)
            for k in range(KD):
                act.wait_ge(x_in[k], 16)
                if k >= 2:
                    act.wait_ge(sq_used, k - 1)
                act.activation(sq[k % 2][:, :], X[:, k, :], ACT.Square).then_inc(sq_ready, 1)
            act.wait_ge(sq_used, KD)
            act.wait_ge(ready, 1)
            act.activation(rstd[:, :].rearrange("p (a b) -> p a b", a=2), bank(0, 2), ACT.Sqrt, bias=eps,
                           scale=1.0 / D).then_inc(root_ready, 1)
            act.wait_ge(ready, 2)
            link(act.activation(lb_t, lb_t, ACT.Exp))
            act.activation(lam_t, lam_t, ACT.Exp).then_inc(root_ready, 1)
            stage_end(act, 1)
            for G in range(8 * SECTIONS):
                if taker(G) != "act":
                    continue
                act.wait_ge(proj_done, G + 1)
                func = {1: ACT.Sigmoid, 3: ACT.Silu}.get(G // 8, ACT.Copy)
                act.activation(proj_dst(G), bank(G % 4), func, scale=P ** -0.5 if G // 8 == 0 else 1.0
                               ).then_inc(proj_out["act"], 1)
            stage_end(act, 2)
            for h in range(HEADS):
                act.wait_ge(log_f, h + 1)
                act.activation(F[:, h, :], F[:, h, :], ACT.Ln).then_inc(ready, 1)
            with act.Fori(0, TT) as n:
                def decay(h):
                    act.wait_ge(hg_diff, n * 4 + h + 1)
                    act.activation(E[h % 2][:, :, :], E[h % 2][:, :, :], ACT.Exp).then_inc(hg_exp, 1)

                def turned(h):
                    act.wait_ge(hg_scores, n * 4 + h + 1)
                    act.wait_ge(hg_pe, n * 4 + h + 1)
                    act.copy(KN[h % 2][:, :], PS[:, 6 + h % 2, 0:128]).then_inc(hg_kn, 1)

                def result(h):
                    act.wait_ge(hg_pe, n * 4 + h + 3)
                    act.copy(INP[:, bass.ds(n, 1), h * 128:(h + 1) * 128].rearrange("p o e -> p (o e)"),
                             PS[:, 4 + h % 2, 0:128]).then_inc(hg_out, 1)

                decay(0)
                decay(1)
                turned(0)
                decay(2)
                turned(1)
                result(0)
                decay(3)
                turned(2)
                result(1)
                turned(3)
                result(2)
                result(3)
            stage_end(act, 3)
            def att_exp(u):
                h, b = att[u]
                nk = (b + 1) * P
                for c in range(2):
                    act.wait_ge(at_max, 2 * u + c + 1)
                    if u >= 2 and c == 0:
                        act.wait_ge(at_tr, u - 1)
                    act.activation(PR[u % 2][c][:, 0:nk], PS[:, 2 * c:2 * c + 2, :].rearrange("p a b -> p (a b)")[:, 0:nk],
                                   ACT.Exp, bias=nmx[:, u % 2, c:c + 1], scale=0.125,
                                   accum_out=l_sum[:, u % 2, c:c + 1]).then_inc(at_exp, 1)

            for u in range(len(att) + 2):
                if u < len(att):
                    att_exp(u)
                if 1 <= u <= len(att):
                    h, b = att[u - 1]
                    act.wait_ge(at_tr, u)
                    if u >= 3:
                        act.wait_ge(at_o, u - 2)
                    act.copy(AT[(u - 1) % 2][:, 0:b + 1, :], bank_tiles(4, 2)[:, 0:b + 1, :]).then_inc(at_t, 1)
                if u >= 2:
                    h, b = att[u - 2]
                    act.wait_ge(at_o, u - 1)
                    act.copy(DA[:, b, h * 128:(h + 1) * 128], PS[:, 6 + u % 2, 0:128]).then_inc(at_oe, 1)
            stage_end(act, 4)
            for i in range(2 * TT):
                t, da = i % TT, i // TT
                if i >= 2:
                    act.wait_ge(nrm_ss, i - 1)
                act.activation(SQN[i % 2][:, :], (DA if da else INP)[:, t, :], ACT.Square).then_inc(nrm_sq, 1)
                if i % TT == TT - 1:
                    act.wait_ge(nrm_ss, i + 1)
                    act.activation(norm_r[:, :], norm_ss[:, :], ACT.Sqrt, bias=eps, scale=1.0 / P).then_inc(nrm_root, 1)
                    act.wait_ge(nrm_r, da + 1)
            stage_end(act, 5)
            for t in range(TT + 1):
                if t < TT:
                    act.wait_ge(mt_tr, t + 1)
                    act.copy(MT[:, 0:4, t * P:(t + 1) * P], bank_tiles(0)).then_inc(mt_act, 1)
                if t >= 1:
                    act.wait_ge(n2_tr, t)
                    b = 4 + 2 * ((t - 1) % 2)
                    act.copy(N2H[(t - 1) // 4][:, :, (t - 1) % 4 * P:((t - 1) % 4 + 1) * P], bank_tiles(b, 2)).then_inc(n2_hi, 1)
                if t < TT:
                    act.wait_ge(h_ready, t + 1)
                    link(act.activation(junk[:, :], H[t % 2][:, :], ACT.Square, accum_out=norm_ss[:, t:t + 1]))
                    act.activation(norm_ss[:, t:t + 1], norm_ss[:, t:t + 1], ACT.Sqrt, bias=eps, scale=1.0 / D).then_inc(h_ss, 1)
            stage_end(act, 6)
            act.dma_start(WQ[0][:, :, :], w_q[:, :, 0:512]).then_inc(wq_in[0], 16)
            act.dma_start(WQ[1][:, :, :], w_q[:, :, 512:1024]).then_inc(wq_in[1], 16)

            def wq_split(M):
                if M % 4 == 0:
                    act.wait_ge(wq_in[(M // 4) % 2], 16 * (M // 8 + 1))
                if M >= 2:
                    act.wait_ge(qh_done, M - 1)
                act.copy(WQH[M % 2][:, :, :], WQ[(M // 4) % 2][:, :, (M % 4) * P:(M % 4 + 1) * P]).then_inc(wq_hi, 1)

            def gate_exp(t):
                act.wait_ge(g_shift, t + 1)
                act.activation(CS[:, :], CS[:, :], ACT.Exp).then_inc(g_exp, 1)

            def take_picks(t):
                act.wait_ge(pk_tr, t + 2)
                act.copy(PT[t % 3][:, :, :], bank_tiles(7)[:, 0:3, :]).then_inc(pt_ready, 1)

            def abs_quad(B, qd, t, x):
                act.wait_ge(quad_done, B * 4 + (qd + 1))
                act.wait_ge(oh_odd, B * 2 + (qd // 2 + 1))
                act.wait_ge(pt_ready, t + 1)
                for j in range(4):
                    ins = act.activation(ABS[:, j, :], iota, ACT.Abs, bias=PT[t % 3][:, 1, bass.ds(x + (4 * qd + j), 1)],
                                         scale=-1.0)
                link(ins)
                act.activation(OH[1][:, :, :], ABS[:, :, :], ACT.Relu, bias=ones[:, 0:1], scale=-1.0).then_inc(oh_odd, 1)

            def take_quad(B, qd, x, buf):
                act.wait_ge(quad_done, B * 4 + (qd + 3))
                act.copy(GS[buf][:, :, bass.ds(x + 4 * qd, 4)].rearrange("p a t -> p t a"),
                         bank_tiles(6 + qd % 2)).then_inc(quad_out, 1)

            wq_split(0)
            wq_split(1)
            for M in range(33):
                if M < 32:
                    if M in (18, 28):
                        gate_exp(M // 10 - 1)
                    act.wait_ge(qh_done, M + 1)
                    if M >= 2:
                        act.wait_ge(sc_done, M - 1)
                    act.copy(QH[M % 2][:, :], bank(M % 2)).then_inc(qh_out, 1)
                    if M + 2 < 32:
                        wq_split(M + 2)
                if M == 31:
                    act.dma_start(n2_dram[0], N2H[1][:, :, :].bitcast(F32)).then_inc(n2_kept, 16)
                    act.dma_start(n2_dram[1], N2L[1][:, :, :].bitcast(F32)).then_inc(n2_kept, 16)
                if M >= 1:
                    S = M - 1
                    half, m = divmod(S, 16)
                    act.wait_ge(sc_done, S + 1)
                    if S >= 2:
                        act.wait_ge(ss_out[S % 2], 16 * (S // 2))
                    act.copy(SS[S % 2][:, :, :], bank_tiles(2 + S % 2)).then_inc(sc_out, 1)
                    act.wait_ge(sc_out, S + 1)
                    dst = s_dram[4 * half:4 * half + 4, m // 2, :, (m % 2) * 128:(m % 2) * 128 + 128].rearrange("a p n -> p a n")
                    act.dma_start(dst, SS[S % 2][:, :, :]).then_inc(ss_out[S % 2], 16)
                if M % 4 == 2 and M < 24:
                    S = M // 4 + 2
                    act.wait_ge(wq_lo, 4 * (S - 1))
                    act.dma_start(WQ[S % 2][:, :, :], w_q[:, :, (S % 4) * 512:(S % 4 + 1) * 512]).then_inc(wq_in[S % 2], 16)
            stage_end(act, 7)

            def u_hi(U, j):
                act.wait_ge(s1, U + 1)
                act.wait_ge(u_in[j % 2], turns(U, j))
                act.copy(UH[j % 2][:, :, :], UR[j % 2][:, :, :]).then_inc(uh, 1)

            def v_hi(place, j):
                act.wait_ge(s2, buffers_free(place, j))
                act.wait_ge(v_in[j % 2], turns(place, j))
                act.copy(VH[j % 4][:, :], VR[j % 2][:, :]).then_inc(vh, 1)

            def turns(n, j):
                return (n - j % 2) * 8 + 16

            def buffers_free(place, j):
                return (place - j % 2) * 4 + 8

            def act_gelu(U, j, free=None):
                if free is not None:
                    act.wait_ge(*free)
                act.wait_ge(s1, U + 3)
                act.activation(AF[j % 2][:, :], bank(j % 2), ACT.Gelu_apprx_tanh).then_inc(gelu, 1)

            def a_hi(place, j):
                act.wait_ge(s2, buffers_free(place, j))
                act.wait_ge(prod, place + 3)
                act.copy(AH[j % 4][:, :], AF[j % 2][:, :]).then_inc(ah, 1)

            def period(place, j, U, more_u=True, quads=None):
                act_gelu(U, j, (al, place + 1))
                if more_u:
                    u_hi(U + 2, j)
                a_hi(place, j)
                if quads:
                    abs_quad(quads[0], 1, quads[1], quads[2])
                act_gelu(U + 1, j + 1, (al, place + 2))
                a_hi(place + 1, j + 1)
                if more_u:
                    u_hi(U + 3, j + 1)
                if quads:
                    take_quads(*quads)
                v_hi(place, j)
                v_hi(place + 1, j + 1)

            def take_quads(B, t, x, y, stored):
                act.wait_ge(gs_out[0], 128 * (4 + stored))
                take_quad(B, 0, y, 0)
                for qd in (1, 3, 5):
                    take_quad(B, qd, y, 0)
                    abs_quad(B, qd + 2, t, x)
                    take_quad(B, qd + 1, y, 0)
                take_quad(B, 7, y, 0)

            def half_period(place, j):
                for q in range(2):
                    a_hi(place + q, j + q)
                for q in range(2):
                    v_hi(place + q, j + q)

            def final_squares(half):
                act.wait_ge(acc_add, (half + 1) * KEYS * 4 + 4)
                if half:
                    act.wait_ge(y_ready, 1)
                act.wait_ge(pk_ready, 8 * TT)
                for t in range(4):
                    link(act.activation(FSQ[:, :], ACC[half][:, t, :], ACT.Square, accum_out=norm_ss[:, t:t + 1]))
                act.activation(norm_ss[:, 0:4], norm_ss[:, 0:4], ACT.Sqrt, bias=eps, scale=1.0 / D).then_inc(y_root, 1)

            def early_step(k, b, i):
                for j in range(4):
                    c = 16 * k + 8 * b + j
                    B, x, qd = i * 2 + (8 * k + 4 * b + j // 2), i * 32 + 16 * (j // 2), 2 * (j % 2)
                    abs_quad(B, qd + 1, k, x + 64 * b)
                    n = 16 * k + 8 * b + 4 * i + j if isinstance(i, int) else 2
                    act_gelu(i * 4 + c, j, (af_out[j % 2], i * 32 + 16 * (8 * k + 4 * b + j // 2)) if n >= 2 else None)
                    u_hi(i * 4 + (c + 2), j)
                    if k == 0 and j == 0:
                        act.wait_ge(n2_kept, 32)
                        act.wait_ge(ss_out[0], 16 * 16)
                        act.wait_ge(ss_out[1], 16 * 16)
                    elif j == 0:
                        act.wait_ge(gs_out[b], 128 * k)
                    take_quad(B, qd, x, b)
                    take_quad(B, qd + 1, x, b)

            u_hi(0, 0)
            u_hi(1, 1)
            for k in range(4):
                take_picks(k)
                if k:
                    gate_exp(k + 1)
                act.preload_act_table(ACT.Gelu_apprx_tanh)
                for b in range(2):
                    if k == 0 and b == 0:
                        for i in range(2):
                            early_step(k, b, i)
                    else:
                        with act.Fori(0, 2) as i:
                            link.loop(i, 4)
                            early_step(k, b, i)
                            link.end(2)
            take_picks(4)
            gate_exp(5)
            act.preload_act_table(ACT.Gelu_apprx_tanh)
            act.wait_ge(gs_out[1], 128 * 4)
            for q in af_out:
                act.wait_ge(q, 16 * AHEAD // 2)
            period(0, 0, AHEAD)
            for k in range(4, PERIODS):
                if k > 4:
                    take_picks(k)
                    if k + 1 < TT:
                        gate_exp(k + 1)
                        act.preload_act_table(ACT.Gelu_apprx_tanh)
                for b in range(2):
                    with act.Fori(0, segment(k, b)) as i:
                        link.loop(i, 4)
                        for j in range(2):
                            place = 16 * (k - 4) + 8 * b + 2 + 2 * j
                            period(i * 4 + place, 2 - 2 * j, i * 4 + (AHEAD + place),
                                   quads=(i * 2 + (8 * k + 4 * b), k, i * 32 + 64 * b, i * 32, 2 * (k - 4) + b) if j else None)
                        link.end(segment(k, b))
            period(AHEAD - 2, 2, KEYS - 2, more_u=False)
            abs_quad(62, 1, 7, 96)
            for q in range(2):
                a_hi(AHEAD + q, q)
            take_quads(62, 7, 96, 32, 7)
            for q in range(2):
                v_hi(AHEAD + q, q)
            with act.Fori(0, AHEAD // 4 - 1) as i:
                half_period(i * 4 + (AHEAD + 2), 2)
                half_period(i * 4 + (AHEAD + 4), 0)
            u_hi(KEYS, 0)
            u_hi(KEYS + 1, 1)
            half_period(KEYS - 2, 2)
            period(KEYS, 0, KEYS)
            final_squares(0)
            act.preload_act_table(ACT.Gelu_apprx_tanh)
            with act.Fori(0, KEYS // 4 - 1) as i:
                period(i * 4 + (KEYS + 2), 2, i * 4 + (KEYS + 2))
                period(i * 4 + (KEYS + 4), 0, i * 4 + (KEYS + 4))
            period(2 * KEYS - 2, 2, 2 * KEYS - 2, more_u=False)
            final_squares(1)

        @block.vector
        def _(dve):
            link = Links(dve, dve_own)
            dve.sem_inc(hg_mask, 2)
            dve.sem_inc(hg_q, 2)
            dve.sem_inc(hg_state, 2)
            dve.sem_inc(su_used, 2)
            dve.sem_inc(prod, 2)
            dve.sem_inc(al, 2)
            dve.sem_inc(acc_add, 4)
            link(dve.memset(zeros[:, :], 0.0))
            dve.memset(eps, EPS).then_inc(ready, 1)
            dve.wait_ge(consts_in, 16 * 7)
            link(dve.tensor_tensor(lb_t[:, 0:4], lb_in[:, 0, :], lb_in[:, 1, :], ALU.max))
            link(dve.tensor_tensor(lb_t[:, 4:8], lb_in[:, 1, :], lb_t[:, 0:4], ALU.subtract))
            link(dve.tensor_tensor(lb_t[:, 0:4], lb_in[:, 0, :], lb_t[:, 0:4], ALU.subtract))
            for r in range(2):
                link(dve.tensor_tensor(lam_in[:, 2 * r, :], lam_in[:, 2 * r, :], lam_in[:, 2 * r + 1, :], ALU.mult))
                ins = dve.reduce_sum(lam_t[:, r:r + 1], lam_in[:, 2 * r, :], AX_X)
                if r == 0:
                    link(ins)
                else:
                    ins.then_inc(ready, 1)
            dve.wait_ge(root_ready, 1)
            link(dve.reciprocal(rstd[:, :], rstd[:, :]))
            for k in range(KD):
                link(dve.scalar_tensor_tensor(out=X[:, k, :], in0=X[:, k, :], scalar=mix_w[:, k:k + 1], in1=rstd[:, :],
                                              op0=ALU.mult, op1=ALU.mult))
            dve.wait_ge(root_ready, 2)
            link(dve.tensor_tensor(one_lb, lb_t[:, 0:4], lb_t[:, 4:8], ALU.add))
            link(dve.reciprocal(one_lb, one_lb))
            link(dve.tensor_tensor(lbs, lb_t[:, 0:4], one_lb, ALU.mult))
            link(dve.tensor_scalar(one_lb, lbs, -1.0, 1.0, ALU.mult, ALU.add))
            link(dve.tensor_tensor(lams, lam_t[:, 0:1], lam_t[:, 1:2], ALU.subtract))
            link(dve.tensor_scalar(lams, lams, LAMBDA_INIT, None, ALU.add))
            stage_end(dve, 1)
            for G in range(8 * SECTIONS):
                if taker(G) != "dve":
                    continue
                dve.wait_ge(proj_done, G + 1)
                dve.tensor_scalar(proj_dst(G), bank(G % 4), P ** -0.5 if G // 8 == 0 else 1.0, None, ALU.mult
                                  ).then_inc(proj_out["dve"], 1)
            stage_end(dve, 2)
            for h in range(HEADS):
                link(dve.tensor_scalar(F[:, h, :], F[:, h, :], one_lb[:, h:h + 1], lbs[:, h:h + 1], ALU.mult, ALU.add))
                dve.tensor_scalar(K[:, h, :], F[:, h, :], -1.0, 1.0, ALU.mult, ALU.add).then_inc(log_f, 1)
            link(dve.memset(STATE[:, :, :], 0.0))
            dve.wait_ge(ready, 2 + HEADS)
            with dve.Fori(0, TT) as n:
                link.loop(n, 3 * HEADS)

                def differences(h):
                    d = E[h % 2]
                    dve.wait_ge(hg_q, n * 4 + h + 1)
                    dve.wait_ge(hg_k, n * 4 + h + 1)
                    b = d[:, 0, :]
                    link(dve.tensor_tensor_scan(b, F[:, h, bass.ds(n * P, P)], zeros[:, :], 0.0, ALU.add, ALU.add))
                    for l in range(LEVELS):
                        m = 64 >> l
                        view = b.rearrange("p (a m) -> p a m", m=2 * m)
                        dve.tensor_tensor(d[:, 1 + l, :].rearrange("p (a m) -> p a m", m=2 * m), view,
                                          view[:, :, m - 1:m].broadcast_to([P, P // (2 * m), 2 * m]), ALU.subtract)
                    link(dve.tensor_scalar(d[:, 8, :], b, b[:, P - 1:P], None, ALU.subtract))
                    dve.scalar_tensor_tensor(out=d[:, :, :], in0=d[:, :, :], scalar=-1.0, in1=d[:, :, :],
                                             op0=ALU.mult, op1=ALU.min).then_inc(hg_diff, 1)

                def queries(h):
                    p = h % 2
                    q = Q[:, h, bass.ds(n * P, P)]
                    dve.wait_ge(hg_pe, n * 4 + h + 1)
                    dve.wait_ge(hg_exp, n * 4 + h + 1)
                    dve.wait_ge(hg_state, n * 4 + h + 1)
                    dve.tensor_copy(QL[p][:, 8, :], q)
                    link(dve.tensor_copy(BL[p][:, :], E[p][:, 0, P - 1:P]))
                    dve.tensor_tensor(QL[p][:, 0:8, :], E[p][:, 0:8, :], spread(q, 1, 8), ALU.mult).then_inc(hg_q, 1)

                def mask(h):
                    p = h % 2
                    dve.wait_ge(hg_scores, n * 4 + h + 1)
                    dve.wait_ge(hg_pe, n * 4 + h + 1)
                    dve.tensor_tensor(M[p][:, :, :], bank_tiles(2 * p, 2), masks[:, :, :], ALU.mult).then_inc(hg_mask, 1)

                def state(h):
                    dve.wait_ge(hg_pe, n * 4 + h + 3)
                    dve.scalar_tensor_tensor(out=STATE[:, h, :], in0=STATE[:, h, :], scalar=BL[h % 2][:, :],
                                             in1=PS[:, 6 + h % 2, 0:128], op0=ALU.mult, op1=ALU.add).then_inc(hg_state, 1)

                differences(0)
                differences(1)
                queries(0)
                differences(2)
                queries(1)
                mask(0)
                differences(3)
                state(0)
                queries(2)
                mask(1)
                state(1)
                queries(3)
                mask(2)
                state(2)
                mask(3)
                state(3)
                link.end(TT)
            stage_end(dve, 3)
            for u in range(len(att) + 1):
                if u >= 1:
                    h, b = att[u - 1]
                    p, nk = (u - 1) % 2, (b + 1) * P
                    dve.wait_ge(at_exp, 2 * u)
                    link(dve.reciprocal(l_rec[:, p, :], l_sum[:, p, :]))
                    link(dve.tensor_scalar(l_rec[:, p, 1:2], l_rec[:, p, 1:2], lams, None, ALU.mult))
                    link(dve.tensor_scalar(PR[p][1][:, 0:nk], PR[p][1][:, 0:nk], l_rec[:, p, 1:2], None, ALU.mult))
                    dve.scalar_tensor_tensor(out=PR[p][0][:, 0:nk], in0=PR[p][0][:, 0:nk], scalar=l_rec[:, p, 0:1],
                                             in1=PR[p][1][:, 0:nk], op0=ALU.mult, op1=ALU.subtract).then_inc(at_comb, 1)
                if u < len(att):
                    h, b = att[u]
                    nk = (b + 1) * P
                    for c in range(2):
                        s = PS[:, 2 * c:2 * c + 2, :].rearrange("p a b -> p (a b)")
                        dve.wait_ge(at_s, 2 * u + c + 1)
                        link(dve.memset(s[0:CHUNK, nk - CHUNK:nk], -1.0e30))
                        link(dve.reduce_max(mx[:, u % 2, c:c + 1], s[:, 0:nk], AX_X))
                        dve.tensor_scalar(nmx[:, u % 2, c:c + 1], mx[:, u % 2, c:c + 1], -0.125, None, ALU.mult
                                          ).then_inc(at_max, 1)
            stage_end(dve, 4)
            link(dve.tensor_scalar(da_gain[:, :], da_gain[:, :], 1.0 - LAMBDA_INIT, None, ALU.mult))
            for da in range(2):
                buf = DA if da else INP
                for t in range(TT):
                    i = da * TT + t
                    dve.wait_ge(nrm_sq, i + 1)
                    dve.reduce_sum(norm_ss[:, t * 4:t * 4 + 4], SQN[i % 2][:, :].rearrange("p (h e) -> p h e", h=4), AX_X
                                   ).then_inc(nrm_ss, 1)
                dve.wait_ge(nrm_root, da + 1)
                link(dve.reciprocal(norm_r[:, :], norm_r[:, :]))
                if not da:
                    dve.wait_ge(gate_gain, TT)
                for t in range(TT):
                    o = buf[:, t, :].rearrange("p (h e) -> p h e", h=4)
                    link(dve.tensor_tensor(o, o, spread(norm_r[:, t * 4:t * 4 + 4], 2, P), ALU.mult))
                    by = spread(da_gain[:, :], 1, 4) if da else GATE[:, t, :].rearrange("p (h e) -> p h e", h=4)
                    ins = dve.tensor_tensor(o, o, by, ALU.mult)
                    if t == TT - 1:
                        ins.then_inc(nrm_r, 1)
            stage_end(dve, 5)
            dve.wait_ge(wo_in, 32)
            for t in range(TT + 1):
                if t < TT:
                    dve.wait_ge(mt_tr, t + 1)
                    dve.tensor_copy(MT[:, 4:8, t * P:(t + 1) * P], bank_tiles(1)).then_inc(mt_dve, 1)
                if t >= 1:
                    dve.wait_ge(n2_hi, t)
                    b = 4 + 2 * ((t - 1) % 2)
                    half, ts = (t - 1) // 4, slice((t - 1) % 4 * P, ((t - 1) % 4 + 1) * P)
                    dve.tensor_tensor(N2L[half][:, :, ts], bank_tiles(b, 2), N2H[half][:, :, ts].bitcast(F32),
                                      ALU.subtract).then_inc(n2_lo, 1)
                if t < TT:
                    dve.wait_ge(wo_done, t + 1)
                    dve.wait_ge(xn_in[t % 2], 16 * (t // 2 + 1))
                    if t >= 2:
                        dve.wait_ge(h_out[t % 2], 16 * (t // 2))
                    dve.tensor_tensor(H[t % 2][:, :].rearrange("p (a b) -> p a b", a=2), bank(2, 2),
                                      XN[t % 2][:, :].rearrange("p (a b) -> p a b", a=2), ALU.add).then_inc(h_ready, 1)
                    dve.wait_ge(h_ss, t + 1)
                    link(dve.reciprocal(norm_r[:, t:t + 1], norm_ss[:, t:t + 1]))
                    if t >= 2:
                        dve.wait_ge(n2_tr, t - 1)
                    dve.scalar_tensor_tensor(out=N2[t % 2][:, :], in0=H[t % 2][:, :], scalar=norm_r[:, t:t + 1],
                                             in1=ffn_w[:, :], op0=ALU.mult, op1=ALU.mult).then_inc(n2_ready, 1)
            stage_end(dve, 6)
            def top16(src, src2, vals, idx):
                for s, v in zip(src, vals):
                    dve.max(v[:, 0:8], s)
                dve.drain()
                for s, v, i in zip(src, vals, idx):
                    dve.max_index(i[:, 0:8], v[:, 0:8], s)
                for s, s2, v in zip(src, src2, vals):
                    dve.match_replace(s2, v[:, 0:8], s, LOWEST)
                dve.drain()
                for s2, v in zip(src2, vals):
                    dve.max(v[:, 8:16], s2)
                dve.drain()
                for s2, v, i in zip(src2, vals, idx):
                    dve.max_index(i[:, 8:16], v[:, 8:16], s2)
                dve.drain()

            def unit_halves(t, slot, loads, col):
                dve.wait_ge(su_in[slot], loads)
                dve.tensor_copy(su_seen[:, :], SU[slot][:, 0, 0:1])
                dve.drain()
                top16([SU[slot][:, a, :] for a in range(2)], [SU2[:, a, :] for a in range(2)],
                      [TOPV[:, a, :] for a in range(2)], [TOPI[:, a, :] for a in range(2)])
                dve.tensor_copy(I12[t % 2][:, :, col], TOPI[:, :, :]).then_inc(su_used, 1)
                dve.tensor_tensor(CAND[:, :].rearrange("p (a b) -> p a b", a=TOPK), spread(TOPV[:, 0, :], 2, TOPK),
                                  spread(TOPV[:, 1, :], 1, TOPK), ALU.add)
                dve.drain()

            def unit_sums(col):
                top16([CAND[:, :]], [CAND2[:, :]], [TOPC], [TOPP])
                dve.tensor_copy(CS[:, col], TOPC[:, :])
                dve.tensor_copy(POS[:, col], TOPP[:, :])
                dve.drain()

            def shift(t):
                cs = CS[:, :].rearrange("p (u k) -> p u k", k=TOPK)
                link(dve.tensor_copy(gmax[:, :], cs[:, :, 0]))
                dve.tensor_tensor(cs, cs, spread(gmax[:, :], 2, TOPK), ALU.subtract).then_inc(g_shift, 1)
                link(dve.tensor_scalar(ABU[:, :], POS[:, :], 4, None, ALU.logical_shift_right))
                link(dve.tensor_copy(AB[t % 2][:, 0, :], ABU[:, :]))
                link(dve.tensor_scalar(ABU[:, :], POS[:, :], 15, None, ALU.bitwise_and))
                link(dve.tensor_copy(AB[t % 2][:, 1, :], ABU[:, :]))

            def gates(t):
                cs = CS[:, :].rearrange("p (u k) -> p u k", k=TOPK)
                dve.wait_ge(g_exp, t + 1)
                link(dve.reduce_sum(gsum[:, :], cs, AX_X))
                link(dve.reciprocal(grec[:, :], gsum[:, :]))
                dve.wait_ge(pk_tr, t + 1)
                link(dve.tensor_tensor(PK[:, 2, :].rearrange("p (u k) -> p u k", k=TOPK), cs, spread(grec[:, :], 2, TOPK),
                                       ALU.mult))

            def keys_of(t, a, x):
                ks = bass.ds(x, 2 * TOPK)
                dve.tensor_tensor(EQ[:, :].rearrange("p (k a) -> p k a", a=TOPK), spread(AB[t % 2][:, a, ks], 2, TOPK),
                                  spread(iota16, 1, 2 * TOPK), ALU.is_equal)
                dve.drain()
                keys = I12[t % 2][:, a, ks].rearrange("p (h a) -> p h a", a=TOPK)
                dve.tensor_tensor(EQ2[:, :].rearrange("p (h k a) -> p h k a", h=2, k=TOPK),
                                  EQ[:, :].rearrange("p (h k a) -> p h k a", h=2, k=TOPK), spread(keys, 2, TOPK), ALU.mult)
                dve.drain()
                dve.reduce_sum(PK[:, a, ks], EQ2[:, :].rearrange("p (k a) -> p k a", a=TOPK), AX_X).then_inc(pk_ready, 1)

            def unit(t, b, i, j):
                return j, i * 16 + 16 * (4 * t + 2 * b + 1), bass.ds(i * 32 + (64 * b + 16 * j), TOPK)

            def rows(B, qd, t, x):
                p = qd % 2
                dve.wait_ge(quad_done, B * 4 + (qd + 1))
                dve.wait_ge(pt_ready, t + 1)
                for j in range(4):
                    tok = bass.ds(x + (4 * qd + j), 1)
                    ins = dve.tensor_scalar(OG[p][:, j, :], iota, PT[t % 3][:, 0, tok], PT[t % 3][:, 2, tok],
                                            ALU.is_equal, ALU.mult)
                ins.then_inc(og_ready, 1)

            dve.drain().then_inc(stage_done, 1)
            for t in range(2):
                for b in range(2):
                    with dve.Fori(0, 2) as i:
                        for j in range(2):
                            slot, loads, col = unit(t, b, i, j)
                            unit_halves(t, slot, loads, col)
                            unit_sums(col)
                shift(t)
                gates(t)
                if t == 0:
                    for a in range(2):
                        with dve.Fori(0, 2) as i:
                            for j in range(2):
                                keys_of(0, a, i * 64 + 32 * j)

            def gated(place, j, U):
                if U is None:
                    dve.wait_ge(af_in[j % 2], (place - j % 2) * 8 + (16 - 8 * AHEAD))
                else:
                    dve.wait_ge(gelu, U + 3)
                dve.wait_ge(g_in[j % 2], (place - j % 2) * 8 + 16)
                dve.tensor_tensor(AF[j % 2][:, :], AF[j % 2][:, :], GT[j % 2][:, :], ALU.mult).then_inc(prod, 1)

            def a_lo(place, j):
                dve.wait_ge(ah, place + 1)
                dve.tensor_tensor(AL[j % 4][:, :], AF[j % 2][:, :], AH[j % 4][:, :].bitcast(F32),
                                  ALU.subtract).then_inc(al, 1)

            def add(g, t, half):
                tt, dh = divmod(t, 2)
                y = ACC[half][:, tt, dh * 512:(dh + 1) * 512]
                dve.wait_ge(s2, g * 8 + t + 17)
                dve.tensor_tensor(y, bank(2 + t % 4), y, ALU.add).then_inc(acc_add, 1)

            def nothing():
                pass

            def period(place, j, U, g=None, half=0, extra=(nothing,) * 3, made=None):
                def add_and_rows(t):
                    if g is not None:
                        add(g, t, half)
                    if made and t + 2 < 8:
                        made(t + 2)

                extra[0]()
                if made:
                    made(0)
                gated(place, j, U)
                a_lo(place, j)
                extra[1]()
                if made:
                    made(1)
                gated(place + 1, j + 1, None if U is None else U + 1)
                add_and_rows(0)
                a_lo(place + 1, j + 1)
                for t in range(1, 4):
                    add_and_rows(t)
                extra[2]()
                for t in range(4, 8):
                    add_and_rows(t)

            def final_norm(half):
                dve.wait_ge(y_root, half + 1)
                dve.wait_ge(consts_in, 16 * 9)
                link(dve.reciprocal(norm_r[:, 0:4], norm_ss[:, 0:4]))
                for t in range(4):
                    dve.scalar_tensor_tensor(out=ACC[half][:, t, :], in0=ACC[half][:, t, :], scalar=norm_r[:, t:t + 1],
                                             in1=fin_w[:, :], op0=ALU.mult, op1=ALU.mult).then_inc(y_ready, 1)

            for k in range(4):
                for b in range(2):
                    with dve.Fori(0, 2) as i:
                        for j in range(2):
                            B, x = i * 2 + (8 * k + 4 * b + j), i * 32 + (64 * b + 16 * j)
                            slot, loads, col = unit(k + 2, b, i, j)
                            rows(B, 0, k, x)
                            rows(B, 1, k, x)
                            unit_halves(k + 2, slot, loads, col)
                            rows(B, 2, k, x)
                            rows(B, 3, k, x)
                            unit_sums(col)
                            keys_of(k + 1, b, i * 64 + 32 * j)
                shift(k + 2)
                gates(k + 2)
            period(0, 0, AHEAD)
            dve.wait_ge(acc_in[0], 16)
            for k in range(4, PERIODS):
                for b in range(2):
                    with dve.Fori(0, segment(k, b)) as i:
                        place = 16 * (k - 4) + 8 * b + 2
                        early, late = [[nothing, nothing, nothing] for _ in range(2)]
                        if k + 2 < TT:
                            (slot0, loads0, col0), (slot1, loads1, col1) = (unit(k + 2, b, i, j) for j in range(2))
                            early[0] = lambda: unit_halves(k + 2, slot0, loads0, col0)
                            early[1] = lambda: unit_sums(col0)
                            early[2] = lambda: unit_halves(k + 2, slot1, loads1, col1)
                            late[0] = lambda: unit_sums(col1)
                        if k + 1 < TT:
                            halves = early[2]
                            early[2] = lambda: (halves(), keys_of(k + 1, b, i * 64), keys_of(k + 1, b, i * 64 + 32))
                        made = lambda qd: rows(i * 2 + (8 * k + 4 * b), qd, k, i * 32 + 64 * b)
                        period(i * 4 + place, 2, i * 4 + (AHEAD + place), i * 2 + (place // 2 - 1), extra=early)
                        period(i * 4 + (place + 2), 0, i * 4 + (AHEAD + place + 2), i * 2 + place // 2, extra=late, made=made)
                if k + 2 < TT:
                    shift(k + 2)
                    gates(k + 2)
            period(AHEAD - 2, 2, KEYS - 2, AHEAD // 2 - 2)
            period(AHEAD, 0, None, AHEAD // 2 - 1, made=lambda qd: rows(62, qd, 7, 96))
            with dve.Fori(0, AHEAD // 4 - 1) as i:
                period(i * 4 + (AHEAD + 2), 2, None, i * 2 + AHEAD // 2)
                period(i * 4 + (AHEAD + 4), 0, None, i * 2 + (AHEAD // 2 + 1))
            period(KEYS - 2, 2, None, KEYS // 2 - 2)
            period(KEYS, 0, KEYS, KEYS // 2 - 1)
            final_norm(0)
            dve.wait_ge(acc_in[1], 16)
            with dve.Fori(0, KEYS // 4 - 1) as i:
                for j in range(2):
                    place = KEYS + 2 + 2 * j
                    period(i * 4 + place, 2 - 2 * j, i * 4 + place, i * 2 + (place // 2 - 1), 1)
            period(2 * KEYS - 2, 2, 2 * KEYS - 2, KEYS - 2, 1)
            for t in range(8):
                add(KEYS - 1, t, 1)
            final_norm(1)

        @block.gpsimd
        def _(pool):
            pool.sem_inc(hg_k, 2)
            pool.sem_inc(vl, 2)
            pool.sem_inc(ul, 2)
            stage_end(pool, 1)
            stage_end(pool, 2)
            pool.wait_ge(ready, 2 + HEADS)
            with pool.Fori(0, TT) as n:
                for h in range(HEADS):
                    p = h % 2
                    k = K[:, h, bass.ds(n * P, P)]
                    pool.wait_ge(hg_pe, n * 4 + h + 1)
                    pool.wait_ge(hg_exp, n * 4 + h + 1)
                    pool.tensor_copy(KL[p][:, 8, :], k)
                    pool.tensor_tensor(KL[p][:, 0:8, :], E[p][:, 1:9, :], spread(k, 1, 8), ALU.mult).then_inc(hg_k, 1)
            stage_end(pool, 3)
            stage_end(pool, 4)
            for t in range(TT):
                g = GATE[:, t, :].rearrange("p (h e) -> p h e", h=4)
                pool.tensor_tensor(g, g, spread(hg_gain[:, :], 1, 4), ALU.mult).then_inc(gate_gain, 1)
            stage_end(pool, 5)
            stage_end(pool, 6)
            for M in range(32):
                pool.wait_ge(wq_hi, M + 1)
                pool.tensor_tensor(WQL[M % 2][:, :, :], WQ[(M // 4) % 2][:, :, (M % 4) * P:(M % 4 + 1) * P],
                                   WQH[M % 2][:, :, :].bitcast(F32), ALU.subtract).then_inc(wq_lo, 1)
            stage_end(pool, 7)

            def rows(B, qd, t, x):
                pool.drain()
                pool.wait_ge(pt_ready, t + 1)
                pool.wait_ge(quad_done, B * 4 + (qd + 1))
                pool.tensor_tensor(DIFF[:, :, :], spread(iota, 1, 4), spread(PT[t % 3][:, 1, bass.ds(x + 4 * qd, 4)], 2, P),
                                   ALU.subtract)
                pool.drain()
                pool.tensor_scalar(OH[0][:, :, :], DIFF[:, :, :], 0.0, None, ALU.is_equal).then_inc(oh_even, 1)

            def u_lo(U, j):
                pool.wait_ge(uh, U + 1)
                pool.tensor_tensor(UL[j % 2][:, :, :], UR[j % 2][:, :, :], UH[j % 2][:, :, :].bitcast(F32),
                                   ALU.subtract).then_inc(ul, 1)

            def v_lo(place, j):
                pool.wait_ge(vh, place + 1)
                pool.tensor_tensor(VL[j % 4][:, :], VR[j % 2][:, :], VH[j % 4][:, :].bitcast(F32),
                                   ALU.subtract).then_inc(vl, 1)

            u_lo(0, 0)
            u_lo(1, 1)
            for k in range(4):
                for b in range(2):
                    with pool.Fori(0, 2) as i:
                        for j in range(4):
                            if j % 2 == 0:
                                rows(i * 2 + (8 * k + 4 * b + j // 2), 0, k, i * 32 + (64 * b + 8 * j))
                            else:
                                rows(i * 2 + (8 * k + 4 * b + j // 2), 2, k, i * 32 + (64 * b + 8 * (j - 1)))
                            u_lo(i * 4 + (16 * k + 8 * b + j + 2), j)
            for q in range(2):
                u_lo(AHEAD + 2 + q, q)
            for q in range(2):
                v_lo(q, q)
            for k in range(4, PERIODS):
                for b in range(2):
                    with pool.Fori(0, segment(k, b)) as i:
                        place = 16 * (k - 4) + 8 * b + 2
                        for q in range(2):
                            u_lo(i * 4 + (AHEAD + place + 2 + q), q)
                        for q in range(2):
                            v_lo(i * 4 + (place + q), 2 + q)
                        rows(i * 2 + (8 * k + 4 * b), 0, k, i * 32 + 64 * b)
                        u_lo(i * 4 + (AHEAD + place + 4), 0)
                        for qd in (2, 4, 6):
                            rows(i * 2 + (8 * k + 4 * b), qd, k, i * 32 + 64 * b)
                        u_lo(i * 4 + (AHEAD + place + 5), 1)
                        for q in range(2):
                            v_lo(i * 4 + (place + 2 + q), q)
            for q in range(2):
                v_lo(AHEAD - 2 + q, 2 + q)
            for qd in (0, 2, 4, 6):
                rows(62, qd, 7, 96)
            for q in range(2):
                v_lo(AHEAD + q, q)
            with pool.Fori(0, AHEAD // 4 - 1) as i:
                for j in range(4):
                    v_lo(i * 4 + (AHEAD + 2 + j), 2 + j)
            for q in range(2):
                u_lo(KEYS + q, q)
            for q in range(2):
                v_lo(KEYS - 2 + q, 2 + q)
            for q in range(2):
                u_lo(KEYS + 2 + q, q)
                v_lo(KEYS + q, q)
            with pool.Fori(0, KEYS // 4 - 1) as i:
                for j in range(4):
                    u_lo(i * 4 + (KEYS + 4 + j), j)
                    v_lo(i * 4 + (KEYS + 2 + j), 2 + j)
            for q in range(2):
                v_lo(2 * KEYS - 2 + q, 2 + q)


def kernel(x, norm_mix_w, w_in, hgrn_lb_param, hgrn_norm_w, diff_lambda, diff_norm_w, w_out, norm_ffn_w,
           peer_w_query, peer_sub_keys, peer_u, peer_v, norm_final_w):
    import concourse.bacc as bacc
    from concourse.bass_utils import run_bass_kernel_spmd

    def rows(a):
        return np.ascontiguousarray(np.asarray(a).reshape(-1, P, a.shape[-1]).transpose(1, 0, 2))

    def everywhere(a):
        return np.ascontiguousarray(np.broadcast_to(np.asarray(a), (P,) + a.shape))

    t = np.arange(P)
    level_masks = np.zeros((P, 8, P), np.float32)
    for l in range(LEVELS):
        m = 64 >> l
        same = t[:, None] // (2 * m) == t[None, :] // (2 * m)
        level_masks[:, l] = same & (t[None, :] % (2 * m) >= m) & (t[:, None] % (2 * m) < m)
    level_masks[:, 7] = np.eye(P)
    cst = np.concatenate([np.eye(P), np.ones((P, P)), np.broadcast_to(t, (P, P)),
                          np.broadcast_to(np.arange(16), (P, 16))], axis=1).astype(np.float32)
    x = np.asarray(x)
    ins = {
        "x_t": rows(x[0].T), "x_n": np.ascontiguousarray(x[0].reshape(TT, P, D)),
        "w_in": rows(w_in[0]), "w_out": rows(w_out[0]), "w_q": rows(peer_w_query[0]),
        "sub_t": np.ascontiguousarray(np.asarray(peer_sub_keys)[0].reshape(16, KEYS, P).transpose(2, 0, 1)),
        "u_t": np.ascontiguousarray(np.asarray(peer_u)[0].reshape(KEYS, P, KD, P).transpose(0, 3, 2, 1)),
        "v": np.ascontiguousarray(np.asarray(peer_v)[0].reshape(KEYS, P, D)),
        "norm_mix": np.ascontiguousarray(np.asarray(norm_mix_w)[0].reshape(KD, P).T),
        "norm_ffn": everywhere(norm_ffn_w[0]), "norm_fin": everywhere(norm_final_w),
        "lb": np.ascontiguousarray(np.asarray(hgrn_lb_param).reshape(2, HEADS, P).transpose(2, 0, 1)),
        "hg_norm": everywhere(hgrn_norm_w[0]), "da_norm": everywhere(diff_norm_w[0]),
        "lam": everywhere(diff_lambda[0]), "cst": cst, "level_masks": level_masks,
    }
    nc = bacc.Bacc("TRN2", target_bir_lowering=False, num_devices=1)
    args = {n: nc.dram_tensor(n, a.shape, F32, kind="ExternalInput").ap() for n, a in ins.items()}
    out = nc.dram_tensor("out", (TT, P, D), F32, kind="ExternalOutput").ap()
    h_dram = nc.dram_tensor("h_dram", (TT, P, D), F32, kind="Internal").ap()
    s_dram = nc.dram_tensor("s_dram", (TT, PEER_HEADS, P, 2 * KEYS), F32, kind="Internal").ap()
    gates_dram = nc.dram_tensor("gates_dram", (KEYS, KEYS, T), F32, kind="Internal").ap()
    n2_dram = nc.dram_tensor("n2_dram", (2, P, KD, HALF_T), F32, kind="Internal").ap()
    a_dram = nc.dram_tensor("a_dram", (KEYS // 2, P, HALF_T), F32, kind="Internal").ap()
    build(nc, **args, a_dram=a_dram, out=out, h_dram=h_dram, s_dram=s_dram, gates_dram=gates_dram, n2_dram=n2_dram)
    r = run_bass_kernel_spmd(nc, [ins], core_ids=[0])
    return r.results[0]["out"].reshape(1, T, D)
```
